# Optimizing a Trainium2 kernel written in Bass

```python
import math
import jax, jax.numpy as jnp
from jax import lax
import numpy as np

D_MODEL = 1024
BATCH = 1
SEQ = 512
DEPTH = 1

A_HEADS = 4
A_HEAD_DIM = 128
IDX_HEADS = 8
IDX_DIM = 64
TOPK_MAX = 256
B_HEADS = 4
B_KEY_DIM = 128
B_VAL_DIM = 128
B_CHUNK = 64
C_HEADS = 4
C_Q_RANK = 384
C_KV_RANK = 256
C_NOPE = 128
C_ROPE = 64
C_V = 128
ROPE_THETA = 10000.0
REL_BUCKETS = 32
REL_MAX_DIST = 128
D_FF = -(-8 * D_MODEL // (3 * 256)) * 256
QBLOCK = 128
EPS = 1e-6
N_BRANCH = 3
NEG_BIG = -1e30
LB_FLOOR = 1e-30

A_WIDTH = A_HEADS * A_HEAD_DIM
B_WIDTH = B_HEADS * B_VAL_DIM
C_WIDTH = C_HEADS * C_V
IN_SPLITS = (A_HEADS * A_HEAD_DIM, A_HEAD_DIM, A_HEAD_DIM,
             IDX_HEADS * IDX_DIM, IDX_DIM, IDX_HEADS,
             B_HEADS * B_KEY_DIM, B_HEADS * B_KEY_DIM,
             B_HEADS * B_VAL_DIM, B_HEADS * B_VAL_DIM,
             C_Q_RANK, C_KV_RANK, C_ROPE,
             N_BRANCH * D_MODEL)
IN_COLS = sum(IN_SPLITS)


def rms_norm(x, g):
    x32 = x.astype(jnp.float32)
    y = x32 * lax.rsqrt(jnp.mean(x32 * x32, axis=-1, keepdims=True) + EPS)
    return (y * g.astype(jnp.float32)).astype(x.dtype)

def apply_rope(x, cos, sin):
    x32 = x.astype(jnp.float32)
    x1, x2 = jnp.split(x32, 2, axis=-1)
    return jnp.concatenate([x1 * cos - x2 * sin, x2 * cos + x1 * sin], axis=-1).astype(x.dtype)

def t5_bucket(dist):
    max_exact = REL_BUCKETS // 2
    d = jnp.maximum(dist, 0)
    dl = jnp.maximum(d, max_exact).astype(jnp.float32)
    large = max_exact + (jnp.log(dl / max_exact) / math.log(REL_MAX_DIST / max_exact)
                         * (REL_BUCKETS - max_exact)).astype(jnp.int32)
    large = jnp.minimum(large, REL_BUCKETS - 1)
    return jnp.where(d < max_exact, d, large)

def dsa_attention(q, k, v, iq, ik, iw, positions, rel_bias):
    bsz, s_len = q.shape[0], q.shape[1]
    topk = min(TOPK_MAX, s_len // 4)
    n_blk = s_len // QBLOCK
    key_idx = jnp.arange(s_len)
    scale = A_HEAD_DIM ** -0.5
    idx_scale = (IDX_DIM ** -0.5) * (IDX_HEADS ** -0.5)
    ik32 = ik.astype(jnp.float32)
    gather = jax.vmap(lambda arr, ix: arr[ix])

    def block(i):
        start = i * QBLOCK
        qb = lax.dynamic_slice_in_dim(q, start, QBLOCK, axis=1)
        iqb = lax.dynamic_slice_in_dim(iq, start, QBLOCK, axis=1).astype(jnp.float32)
        iwb = lax.dynamic_slice_in_dim(iw, start, QBLOCK, axis=1).astype(jnp.float32)
        pb = lax.dynamic_slice_in_dim(positions, start, QBLOCK, axis=1)
        t_idx = start + jnp.arange(QBLOCK)
        causal = key_idx[None, :] <= t_idx[:, None]
        logits = jnp.einsum('bthd,bsd->bths', iqb, ik32)
        score = jnp.einsum('bths,bth->bts', jax.nn.relu(logits), iwb) * idx_scale
        score = jnp.where(causal[None], score, NEG_BIG)
        _, sel = lax.top_k(score, topk)
        k_sel = gather(k, sel)
        v_sel = gather(v, sel)
        p_sel = gather(positions, sel)
        bias = rel_bias[t5_bucket(pb[:, :, None] - p_sel)]
        s = (jnp.einsum('bthd,btkd->bthk', qb, k_sel).astype(jnp.float32) * scale
             + jnp.moveaxis(bias, -1, 2).astype(jnp.float32))
        valid = sel <= t_idx[None, :, None]
        s = jnp.where(valid[:, :, None, :], s, NEG_BIG)
        p = jax.nn.softmax(s, axis=-1).astype(v.dtype)
        return jnp.einsum('bthk,btkd->bthd', p, v_sel)

    out = lax.map(block, jnp.arange(n_blk))
    return jnp.moveaxis(out, 0, 1).reshape(bsz, s_len, A_WIDTH)

def hgrn2_mixer(q, f_raw, inp, g, lb, out_gain):
    bsz, s_len = q.shape[0], q.shape[1]
    f32 = jnp.float32
    n_chunk = s_len // B_CHUNK
    fr = f_raw.astype(f32)
    log_lb = jnp.log(jnp.maximum(lb, LB_FLOOR))
    log_f = jnp.logaddexp(log_lb, jnp.log1p(-lb) + jax.nn.log_sigmoid(fr))
    k_in = (1.0 - lb) * jax.nn.sigmoid(-fr)
    q_s = q.astype(f32) * (B_KEY_DIM ** -0.5)

    def chunks(t, d):
        return t.astype(f32).reshape(bsz, n_chunk, B_CHUNK, B_HEADS, d).transpose(1, 0, 3, 2, 4)

    causal = jnp.tril(jnp.ones((B_CHUNK, B_CHUNK), dtype=bool))

    def step(state, xs):
        qc, kc, vc, lfc = xs
        b = jnp.cumsum(lfc, axis=2)
        o_inter = jnp.einsum('bhck,bhkv->bhcv', qc * jnp.exp(b), state)
        diff = b[:, :, :, None, :] - b[:, :, None, :, :]
        decay = jnp.exp(jnp.where(causal[None, None, :, :, None], diff, NEG_BIG))
        attn = jnp.einsum('bhtk,bhsk,bhtsk->bhts', qc, kc, decay)
        o_intra = jnp.einsum('bhts,bhsv->bhtv', attn, vc)
        b_last = b[:, :, -1:, :]
        new_state = (jnp.exp(b_last[:, :, 0, :])[..., None] * state
                     + jnp.einsum('bhsk,bhsv->bhkv', kc * jnp.exp(b_last - b), vc))
        return new_state, o_inter + o_intra

    xs = (chunks(q_s, B_KEY_DIM), chunks(k_in, B_KEY_DIM), chunks(inp, B_VAL_DIM), chunks(log_f, B_KEY_DIM))
    state0 = jnp.zeros((bsz, B_HEADS, B_KEY_DIM, B_VAL_DIM), f32)
    _, o = lax.scan(step, state0, xs)
    o = o.transpose(1, 0, 3, 2, 4).reshape(bsz, s_len, B_HEADS, B_VAL_DIM)
    o = rms_norm(o, out_gain) * jax.nn.silu(g.astype(f32).reshape(bsz, s_len, B_HEADS, B_VAL_DIM))
    return o.reshape(bsz, s_len, B_WIDTH).astype(q.dtype)

def mla_attention(q_nope, q_pe, k_nope, k_pe, v):
    bsz, s_len = q_nope.shape[0], q_nope.shape[1]
    n_blk = s_len // QBLOCK
    scale = (C_NOPE + C_ROPE) ** -0.5
    key_idx = jnp.arange(s_len)

    def block(i):
        start = i * QBLOCK
        qn = lax.dynamic_slice_in_dim(q_nope, start, QBLOCK, axis=1)
        qp = lax.dynamic_slice_in_dim(q_pe, start, QBLOCK, axis=1)
        t_idx = start + jnp.arange(QBLOCK)
        causal = key_idx[None, :] <= t_idx[:, None]
        s = (jnp.einsum('bthd,bshd->bhts', qn, k_nope)
             + jnp.einsum('bthr,bsr->bhts', qp, k_pe)).astype(jnp.float32) * scale
        s = jnp.where(causal[None, None], s, NEG_BIG)
        p = jax.nn.softmax(s, axis=-1).astype(v.dtype)
        return jnp.einsum('bhts,bshd->bthd', p, v)

    out = lax.map(block, jnp.arange(n_blk))
    return jnp.moveaxis(out, 0, 1).reshape(bsz, s_len, C_WIDTH)

def first_inputs(seed: int = 0) -> dict:
    key = jax.random.key(seed)
    ks = jax.random.split(key, 24)
    f32 = jnp.float32
    res_scale = (2 * DEPTH) ** -0.5

    def dense(k, shape, fan_in, scale=1.0):
        return jax.random.normal(k, shape, f32) * (scale * fan_in ** -0.5)

    def gain(k, shape):
        return 1.0 + 0.02 * jax.random.normal(k, shape, f32)

    x = jax.random.normal(ks[0], (BATCH, SEQ, D_MODEL), f32)
    offset = jax.random.randint(ks[1], (BATCH, 1), 0, 4096, dtype=jnp.int32)
    positions = offset + jnp.arange(SEQ, dtype=jnp.int32)[None, :]
    return {
        'x': x,
        'positions': positions,
        'w_in': dense(ks[2], (DEPTH, D_MODEL, IN_COLS), D_MODEL),
        'w_up_a': dense(ks[3], (DEPTH, A_WIDTH, D_MODEL), A_WIDTH),
        'w_up_b': dense(ks[4], (DEPTH, B_WIDTH, D_MODEL), B_WIDTH),
        'w_up_c': dense(ks[5], (DEPTH, C_WIDTH, D_MODEL), C_WIDTH),
        'w_out': dense(ks[6], (DEPTH, D_MODEL, D_MODEL), D_MODEL, res_scale),
        'mla_q_norm': gain(ks[7], (DEPTH, C_Q_RANK)),
        'mla_w_qb': dense(ks[8], (DEPTH, C_Q_RANK, C_HEADS * (C_NOPE + C_ROPE)), C_Q_RANK),
        'mla_kv_norm': gain(ks[9], (DEPTH, C_KV_RANK)),
        'mla_w_kvb': dense(ks[10], (DEPTH, C_KV_RANK, C_HEADS * (C_NOPE + C_V)), C_KV_RANK),
        'hgrn_lb_logits': 0.5 * jax.random.normal(ks[11], (DEPTH, B_HEADS * B_KEY_DIM), f32),
        'hgrn_out_norm': gain(ks[12], (DEPTH, B_VAL_DIM)),
        'rel_bias': 0.5 * jax.random.normal(ks[13], (REL_BUCKETS, A_HEADS), f32),
        'attn_norm': gain(ks[14], (DEPTH, D_MODEL)),
        'ffn_norm': gain(ks[15], (DEPTH, D_MODEL)),
        'w_ffn_gate': dense(ks[16], (DEPTH, D_MODEL, D_FF), D_MODEL),
        'w_ffn_up': dense(ks[17], (DEPTH, D_MODEL, D_FF), D_MODEL),
        'w_ffn_down': dense(ks[18], (DEPTH, D_FF, D_MODEL), D_FF, res_scale),
        'final_norm': gain(ks[19], (D_MODEL,)),
    }

def first_block(x, positions, w_in, w_up_a, w_up_b, w_up_c, w_out, mla_q_norm, mla_w_qb, mla_kv_norm,
              mla_w_kvb, hgrn_lb_logits, hgrn_out_norm, rel_bias, attn_norm, ffn_norm, w_ffn_gate,
              w_ffn_up, w_ffn_down, final_norm):
    bsz, s_len, _ = x.shape
    f32 = jnp.float32
    split_pts = np.cumsum(IN_SPLITS)[:-1].tolist()
    p_lb = jax.nn.softmax(hgrn_lb_logits.astype(f32), axis=0)
    lower_bounds = jnp.cumsum(p_lb, axis=0) - p_lb[0:1]
    inv_freq = ROPE_THETA ** (-jnp.arange(0, C_ROPE, 2, dtype=f32) / C_ROPE)
    ang = positions.astype(f32)[..., None] * inv_freq
    cos, sin = jnp.cos(ang), jnp.sin(ang)

    for l in range(DEPTH):
        h = rms_norm(x, attn_norm[l])
        proj = h @ w_in[l]
        (aq, ak, av, iq, ik, iw, bq, bf, bi, bg, cq, ckv, ckpe, gate_logits) = jnp.split(proj, split_pts, axis=-1)
        o_a = dsa_attention(aq.reshape(bsz, s_len, A_HEADS, A_HEAD_DIM), ak, av,
                            iq.reshape(bsz, s_len, IDX_HEADS, IDX_DIM), ik, iw, positions, rel_bias)
        o_b = hgrn2_mixer(bq, bf, bi, bg, lower_bounds[l], hgrn_out_norm[l])
        q_c = (rms_norm(cq, mla_q_norm[l]) @ mla_w_qb[l]).reshape(bsz, s_len, C_HEADS, C_NOPE + C_ROPE)
        q_nope, q_pe = q_c[..., :C_NOPE], q_c[..., C_NOPE:]
        kv_c = (rms_norm(ckv, mla_kv_norm[l]) @ mla_w_kvb[l]).reshape(bsz, s_len, C_HEADS, C_NOPE + C_V)
        k_nope, v_c = kv_c[..., :C_NOPE], kv_c[..., C_NOPE:]
        q_pe = apply_rope(q_pe, cos[:, :, None, :], sin[:, :, None, :])
        k_pe = apply_rope(ckpe, cos, sin)
        o_c = mla_attention(q_nope, q_pe, k_nope, k_pe, v_c)
        gates = jax.nn.sigmoid(gate_logits.astype(f32)).astype(x.dtype)
        g_a, g_b, g_c = jnp.split(gates, N_BRANCH, axis=-1)
        mixed = g_a * (o_a @ w_up_a[l]) + g_b * (o_b @ w_up_b[l]) + g_c * (o_c @ w_up_c[l])
        x = x + mixed @ w_out[l]
        h = rms_norm(x, ffn_norm[l])
        x = x + (jax.nn.silu(h @ w_ffn_gate[l]) * (h @ w_ffn_up[l])) @ w_ffn_down[l]

    return rms_norm(x, final_norm)


ATTN_WIDTH = 512
N_HEADS = 8
HEAD_DIM = 64
N_KV_GROUPS = 2
HEADS_PER_GROUP = N_HEADS // N_KV_GROUPS
KV_WIDTH = N_KV_GROUPS * HEAD_DIM
CMP_LEN = 32
CMP_STRIDE = 16
CMP_HIDDEN = 256
SEL_BLOCK = 64
SEL_TOPN = 16
WINDOW = 512
Q_BLOCK = 64
SSM_WIDTH = D_MODEL - ATTN_WIDTH
SSM_GROUP = 16
SSM_GROUPS = SSM_WIDTH // SSM_GROUP
SSM_STATE = 64
SSM_CHUNK = 128
DT_MIN = 1e-3
DT_MAX = 1e-1
IN_WIDTH = ATTN_WIDTH + 6 * KV_WIDTH + ATTN_WIDTH + N_BRANCH * N_HEADS + 2 * SSM_WIDTH


def rms_norm_2(x, g):
    xf = x.astype(jnp.float32)
    y = xf * lax.rsqrt(jnp.mean(xf * xf, axis=-1, keepdims=True) + EPS)
    return (y * g.astype(jnp.float32)).astype(x.dtype)

def rope_tables(T, dtype):
    inv = 1.0 / (ROPE_THETA ** (jnp.arange(0, HEAD_DIM, 2, dtype=jnp.float32) / HEAD_DIM))
    ang = jnp.arange(T, dtype=jnp.float32)[:, None] * inv[None, :]
    return jnp.cos(ang).astype(dtype), jnp.sin(ang).astype(dtype)

def apply_rope_2(x, cos, sin):
    x1, x2 = jnp.split(x, 2, axis=-1)
    c = cos[None, :, None, :]
    s = sin[None, :, None, :]
    return jnp.concatenate([x1 * c - x2 * s, x2 * c + x1 * s], axis=-1)

def masked_softmax(s, mask):
    s = jnp.where(mask, s.astype(jnp.float32), -jnp.inf)
    m = jnp.max(s, axis=-1, keepdims=True)
    m = jnp.where(jnp.isfinite(m), m, 0.0)
    e = jnp.where(mask, jnp.exp(s - m), 0.0)
    return e / jnp.maximum(jnp.sum(e, axis=-1, keepdims=True), 1e-30)

def compress(kv_raw, pos, w1, w2):
    B, T = kv_raw.shape[0], kv_raw.shape[1]
    nc = (T - CMP_LEN) // CMP_STRIDE + 1
    idx = jnp.arange(nc)[:, None] * CMP_STRIDE + jnp.arange(CMP_LEN)[None, :]
    blocks = kv_raw[:, idx] + pos[None, None, :, None, :]
    blocks = blocks.transpose(0, 1, 3, 2, 4).reshape(B, nc, N_KV_GROUPS, CMP_LEN * HEAD_DIM)
    return jax.nn.gelu(blocks @ w1) @ w2

def block_importance(p_cmp, nsb):
    r = SEL_BLOCK // CMP_STRIDE
    ov = CMP_LEN // CMP_STRIDE
    nc = p_cmp.shape[-1]
    left = ov - 1
    right = r * nsb + r - nc
    pp = jnp.pad(p_cmp, [(0, 0)] * (p_cmp.ndim - 1) + [(left, right)])
    terms = []
    for m in range(r):
        for n in range(ov):
            start = m - n + left
            terms.append(pp[..., start:start + r * (nsb - 1) + 1:r])
    return sum(terms[1:], terms[0])

def nsa_attention(q, kc, vc, k_slc, v_slc, k_win, v_win, gates):
    B, T = q.shape[0], q.shape[1]
    cos, sin = rope_tables(T, q.dtype)
    q_r = apply_rope_2(q, cos, sin)
    k_slc = apply_rope_2(k_slc, cos, sin)
    k_win = apply_rope_2(k_win, cos, sin)
    q_g = q.reshape(B, T, N_KV_GROUPS, HEADS_PER_GROUP, HEAD_DIM)
    q_rg = q_r.reshape(B, T, N_KV_GROUPS, HEADS_PER_GROUP, HEAD_DIM)
    gates = gates.reshape(B, T, N_KV_GROUPS, HEADS_PER_GROUP, N_BRANCH)
    nsb = T // SEL_BLOCK
    n_sel = min(SEL_TOPN, nsb)
    nc = kc.shape[1]
    k_blocks = k_slc.reshape(B, nsb, SEL_BLOCK, N_KV_GROUPS, HEAD_DIM).transpose(0, 3, 1, 2, 4)
    v_blocks = v_slc.reshape(B, nsb, SEL_BLOCK, N_KV_GROUPS, HEAD_DIM).transpose(0, 3, 1, 2, 4)
    k_win_p = jnp.pad(k_win, ((0, 0), (WINDOW, 0), (0, 0), (0, 0)))
    v_win_p = jnp.pad(v_win, ((0, 0), (WINDOW, 0), (0, 0), (0, 0)))
    cmp_end = jnp.arange(nc) * CMP_STRIDE + CMP_LEN - 1
    blk = jnp.arange(nsb)
    scale = HEAD_DIM ** -0.5
    gather = jax.vmap(jax.vmap(lambda kb, ix: kb[ix]))
    n_keys = n_sel * SEL_BLOCK

    def block_fn(qb):
        t0 = qb * Q_BLOCK
        t = t0 + jnp.arange(Q_BLOCK)
        qc = lax.dynamic_slice_in_dim(q_g, t0, Q_BLOCK, 1)
        qr = lax.dynamic_slice_in_dim(q_rg, t0, Q_BLOCK, 1)
        g = lax.dynamic_slice_in_dim(gates, t0, Q_BLOCK, 1)
        s = jnp.einsum('bqghd,bngd->bghqn', qc, kc) * scale
        p = masked_softmax(s, cmp_end[None, :] <= t[:, None])
        o_cmp = jnp.einsum('bghqn,bngd->bqghd', p.astype(vc.dtype), vc)
        imp = block_importance(jnp.sum(p, axis=2), nsb)
        cur = t // SEL_BLOCK
        forced = (blk[None, :] == 0) | (blk[None, :] == cur[:, None]) | (blk[None, :] == cur[:, None] - 1)
        valid = blk[None, :] * SEL_BLOCK <= t[:, None]
        imp = jnp.where(forced, jnp.inf, jnp.where(valid, imp, -jnp.inf))
        _, idx = lax.top_k(imp, n_sel)
        ks = gather(k_blocks, idx).reshape(B, N_KV_GROUPS, Q_BLOCK, n_keys, HEAD_DIM)
        vs = gather(v_blocks, idx).reshape(B, N_KV_GROUPS, Q_BLOCK, n_keys, HEAD_DIM)
        kpos = (idx[..., None] * SEL_BLOCK + jnp.arange(SEL_BLOCK)).reshape(B, N_KV_GROUPS, Q_BLOCK, n_keys)
        s = jnp.einsum('bqghd,bgqkd->bghqk', qr, ks) * scale
        p = masked_softmax(s, (kpos <= t[:, None])[:, :, None])
        o_slc = jnp.einsum('bghqk,bgqkd->bqghd', p.astype(vs.dtype), vs)
        kw = lax.dynamic_slice_in_dim(k_win_p, t0, WINDOW + Q_BLOCK, 1)
        vw = lax.dynamic_slice_in_dim(v_win_p, t0, WINDOW + Q_BLOCK, 1)
        wpos = t0 - WINDOW + jnp.arange(WINDOW + Q_BLOCK)
        dist = t[:, None] - wpos[None, :]
        wmask = (dist >= 0) & (dist < WINDOW) & (wpos[None, :] >= 0)
        s = jnp.einsum('bqghd,bkgd->bghqk', qr, kw) * scale
        p = masked_softmax(s, wmask)
        o_win = jnp.einsum('bghqk,bkgd->bqghd', p.astype(vw.dtype), vw)
        return g[..., 0:1] * o_cmp + g[..., 1:2] * o_slc + g[..., 2:3] * o_win

    out = lax.map(block_fn, jnp.arange(T // Q_BLOCK))
    return out.transpose(1, 0, 2, 3, 4, 5).reshape(B, T, ATTN_WIDTH)

def s5_mixer(u, a_re, a_im, log_dt, b_re, b_im, c_re, c_im, d_skip):
    B, T = u.shape[0], u.shape[1]
    f32 = jnp.float32
    uf = u.astype(f32)
    lam = lax.complex(a_re.astype(f32), a_im.astype(f32))
    dt = jnp.exp(log_dt.astype(f32))[:, None]
    lam_bar = jnp.exp(lam * dt)
    b_bar = ((lam_bar - 1.0) / lam)[..., None] * lax.complex(b_re.astype(f32), b_im.astype(f32))
    c_mat = lax.complex(c_re.astype(f32), c_im.astype(f32))
    nch = T // SSM_CHUNK
    uc = uf.reshape(B, nch, SSM_CHUNK, SSM_GROUPS, SSM_GROUP).transpose(1, 0, 2, 3, 4)

    def binop(e1, e2):
        a1, b1 = e1
        a2, b2 = e2
        return a1 * a2, a2 * b1 + b2

    def step(carry, u_chunk):
        bu = jnp.einsum('btgc,gpc->btgp', u_chunk.astype(jnp.complex64), b_bar)
        a = jnp.broadcast_to(lam_bar, bu.shape)
        a_cum, b_cum = lax.associative_scan(binop, (a, bu), axis=1)
        s = a_cum * carry[:, None] + b_cum
        y = jnp.real(jnp.einsum('gcp,btgp->btgc', c_mat, s))
        return s[:, -1], y

    carry0 = jnp.zeros((B, SSM_GROUPS, SSM_STATE), jnp.complex64)
    _, y = lax.scan(step, carry0, uc)
    y = y.transpose(1, 0, 2, 3, 4).reshape(B, T, SSM_WIDTH)
    return y + d_skip.astype(f32) * uf

def hybrid_layer(x, c, w_ada, b_ada, norm_g, w_in, q_norm_g, k_cmp_norm_g, k_slc_norm_g, k_win_norm_g,
                 cmp_pos_k, cmp_pos_v, cmp_w1_k, cmp_w2_k, cmp_w1_v, cmp_w2_v,
                 ssm_a_re, ssm_a_im, ssm_log_dt, ssm_b_re, ssm_b_im, ssm_c_re, ssm_c_im, ssm_d,
                 glu_w, glu_b, w_out):
    B, T = x.shape[0], x.shape[1]
    mod = jax.nn.silu(c) @ w_ada + b_ada
    shift, scale, gate = jnp.split(mod, 3, axis=-1)
    h = rms_norm_2(x, norm_g) * (1 + scale[:, None, :]) + shift[:, None, :]
    proj = h @ w_in
    widths = [ATTN_WIDTH] + [KV_WIDTH] * 6 + [ATTN_WIDTH, N_BRANCH * N_HEADS, SSM_WIDTH, SSM_WIDTH]
    offs = [int(v) for v in np.cumsum(widths)[:-1]]
    q, kcr, vcr, ksl, vsl, kwn, vwn, z_a, g_br, u, z_s = jnp.split(proj, offs, axis=-1)

    def kv_heads(t):
        return t.reshape(B, T, N_KV_GROUPS, HEAD_DIM)

    q = rms_norm_2(q.reshape(B, T, N_HEADS, HEAD_DIM), q_norm_g)
    kc = rms_norm_2(compress(kv_heads(kcr), cmp_pos_k, cmp_w1_k, cmp_w2_k), k_cmp_norm_g)
    vc = compress(kv_heads(vcr), cmp_pos_v, cmp_w1_v, cmp_w2_v)
    k_slc = rms_norm_2(kv_heads(ksl), k_slc_norm_g)
    k_win = rms_norm_2(kv_heads(kwn), k_win_norm_g)
    gates = jax.nn.sigmoid(g_br).reshape(B, T, N_HEADS, N_BRANCH)
    attn = nsa_attention(q, kc, vc, k_slc, kv_heads(vsl), k_win, kv_heads(vwn), gates)
    attn = attn * jax.nn.silu(z_a)

    y = s5_mixer(u, ssm_a_re, ssm_a_im, ssm_log_dt, ssm_b_re, ssm_b_im, ssm_c_re, ssm_c_im, ssm_d)
    y = jax.nn.gelu(y)
    y = y * jax.nn.sigmoid(y @ glu_w.astype(jnp.float32) + glu_b.astype(jnp.float32))
    ssm = y.astype(x.dtype) * jax.nn.silu(z_s)

    mix = jnp.concatenate([attn, ssm], axis=-1) @ w_out
    return x + gate[:, None, :] * mix

def second_inputs(seed: int = 0) -> dict:
    key = jax.random.key(seed)
    ks = jax.random.split(key, 32)
    f32 = jnp.float32

    def nrm(k, shape, s):
        return jax.random.normal(k, shape, f32) * s

    D = D_MODEL
    L = DEPTH
    ng, p, cg = SSM_GROUPS, SSM_STATE, SSM_GROUP
    return {
        "x": nrm(ks[0], (BATCH, SEQ, D), 1.0),
        "c": nrm(ks[1], (BATCH, D), 1.0),
        "w_ada": nrm(ks[2], (L, D, 3 * D), 0.5 * D ** -0.5),
        "b_ada": nrm(ks[3], (L, 3 * D), 0.01),
        "norm_g": 1.0 + nrm(ks[4], (L, D), 0.02),
        "w_in": nrm(ks[5], (L, D, IN_WIDTH), D ** -0.5),
        "q_norm_g": 1.0 + nrm(ks[6], (L, HEAD_DIM), 0.02),
        "k_cmp_norm_g": 1.0 + nrm(ks[7], (L, HEAD_DIM), 0.02),
        "k_slc_norm_g": 1.0 + nrm(ks[8], (L, HEAD_DIM), 0.02),
        "k_win_norm_g": 1.0 + nrm(ks[9], (L, HEAD_DIM), 0.02),
        "cmp_pos_k": nrm(ks[10], (L, CMP_LEN, HEAD_DIM), 0.1),
        "cmp_pos_v": nrm(ks[11], (L, CMP_LEN, HEAD_DIM), 0.1),
        "cmp_w1_k": nrm(ks[12], (L, CMP_LEN * HEAD_DIM, CMP_HIDDEN), (CMP_LEN * HEAD_DIM) ** -0.5),
        "cmp_w2_k": nrm(ks[13], (L, CMP_HIDDEN, HEAD_DIM), CMP_HIDDEN ** -0.5),
        "cmp_w1_v": nrm(ks[14], (L, CMP_LEN * HEAD_DIM, CMP_HIDDEN), (CMP_LEN * HEAD_DIM) ** -0.5),
        "cmp_w2_v": nrm(ks[15], (L, CMP_HIDDEN, HEAD_DIM), CMP_HIDDEN ** -0.5),
        "ssm_a_re": -0.5 + nrm(ks[16], (L, ng, p), 0.01),
        "ssm_a_im": math.pi * jnp.arange(p, dtype=f32)[None, None, :] + nrm(ks[17], (L, ng, p), 0.01),
        "ssm_log_dt": jax.random.uniform(ks[18], (L, ng), f32, math.log(DT_MIN), math.log(DT_MAX)),
        "ssm_b_re": nrm(ks[19], (L, ng, p, cg), (2 * cg) ** -0.5),
        "ssm_b_im": nrm(ks[20], (L, ng, p, cg), (2 * cg) ** -0.5),
        "ssm_c_re": nrm(ks[21], (L, ng, cg, p), p ** -0.5),
        "ssm_c_im": nrm(ks[22], (L, ng, cg, p), p ** -0.5),
        "ssm_d": nrm(ks[23], (L, SSM_WIDTH), 1.0),
        "glu_w": nrm(ks[24], (L, SSM_WIDTH, SSM_WIDTH), SSM_WIDTH ** -0.5),
        "glu_b": nrm(ks[25], (L, SSM_WIDTH), 0.01),
        "w_out": nrm(ks[26], (L, D, D), D ** -0.5),
    }

def second_block(x, c, w_ada, b_ada, norm_g, w_in, q_norm_g, k_cmp_norm_g, k_slc_norm_g, k_win_norm_g,
              cmp_pos_k, cmp_pos_v, cmp_w1_k, cmp_w2_k, cmp_w1_v, cmp_w2_v,
              ssm_a_re, ssm_a_im, ssm_log_dt, ssm_b_re, ssm_b_im, ssm_c_re, ssm_c_im, ssm_d,
              glu_w, glu_b, w_out):
    for l in range(DEPTH):
        x = hybrid_layer(x, c, w_ada[l], b_ada[l], norm_g[l], w_in[l], q_norm_g[l], k_cmp_norm_g[l],
                         k_slc_norm_g[l], k_win_norm_g[l], cmp_pos_k[l], cmp_pos_v[l], cmp_w1_k[l],
                         cmp_w2_k[l], cmp_w1_v[l], cmp_w2_v[l], ssm_a_re[l], ssm_a_im[l], ssm_log_dt[l],
                         ssm_b_re[l], ssm_b_im[l], ssm_c_re[l], ssm_c_im[l], ssm_d[l], glu_w[l], glu_b[l],
                         w_out[l])
    return x


def setup_inputs(seed=0):
    out = dict(first_inputs(seed))
    for name, value in second_inputs(seed + 1).items():
        if name != "x":
            out[name + "_2"] = value
    return out


def reference(
    x, positions, w_in, w_up_a, w_up_b, w_up_c, w_out, mla_q_norm, mla_w_qb, mla_kv_norm,
    mla_w_kvb, hgrn_lb_logits, hgrn_out_norm, rel_bias, attn_norm, ffn_norm, w_ffn_gate,
    w_ffn_up, w_ffn_down, final_norm, c_2, w_ada_2, b_ada_2, norm_g_2, w_in_2, q_norm_g_2,
    k_cmp_norm_g_2, k_slc_norm_g_2, k_win_norm_g_2, cmp_pos_k_2, cmp_pos_v_2, cmp_w1_k_2,
    cmp_w2_k_2, cmp_w1_v_2, cmp_w2_v_2, ssm_a_re_2, ssm_a_im_2, ssm_log_dt_2, ssm_b_re_2,
    ssm_b_im_2, ssm_c_re_2, ssm_c_im_2, ssm_d_2, glu_w_2, glu_b_2, w_out_2,
):
    x = first_block(
        x, positions, w_in, w_up_a, w_up_b, w_up_c, w_out, mla_q_norm, mla_w_qb, mla_kv_norm,
        mla_w_kvb, hgrn_lb_logits, hgrn_out_norm, rel_bias, attn_norm, ffn_norm, w_ffn_gate,
        w_ffn_up, w_ffn_down, final_norm,
    )
    return second_block(
        x, c_2, w_ada_2, b_ada_2, norm_g_2, w_in_2, q_norm_g_2, k_cmp_norm_g_2, k_slc_norm_g_2,
        k_win_norm_g_2, cmp_pos_k_2, cmp_pos_v_2, cmp_w1_k_2, cmp_w2_k_2, cmp_w1_v_2,
        cmp_w2_v_2, ssm_a_re_2, ssm_a_im_2, ssm_log_dt_2, ssm_b_re_2, ssm_b_im_2, ssm_c_re_2,
        ssm_c_im_2, ssm_d_2, glu_w_2, glu_b_2, w_out_2,
    )


_drawn_inputs = setup_inputs


def setup_inputs(seed=0):
    import zlib

    import numpy as np

    out = dict(_drawn_inputs(seed))
    spreads = {}
    factors = {'mla_q_norm': 8.0,
     'mla_kv_norm': 8.0,
     'hgrn_out_norm': 8.0,
     'attn_norm': 4.16,
     'ffn_norm': 5.251,
     'final_norm': 2.828,
     'b_ada_2': 8.0,
     'norm_g_2': 8.0,
     'q_norm_g_2': 8.0,
     'k_cmp_norm_g_2': 8.0,
     'k_slc_norm_g_2': 8.0,
     'k_win_norm_g_2': 8.0,
     'cmp_pos_k_2': 8.0,
     'cmp_pos_v_2': 8.0,
     'cmp_w1_k_2': 5.345,
     'cmp_w2_k_2': 5.165,
     'ssm_a_re_2': 64.0,
     'ssm_a_im_2': 64.0,
     'ssm_log_dt_2': 64.0,
     'ssm_b_re_2': 64.0,
     'ssm_b_im_2': 64.0,
     'ssm_c_re_2': 64.0,
     'ssm_c_im_2': 64.0,
     'glu_w_2': 3.237,
     'glu_b_2': 180.244}
    for name, (base, spread) in spreads.items():
        noise = np.random.default_rng([zlib.crc32(name.encode()), seed]).standard_normal(out[name].shape)
        drawn = base * np.exp(spread * noise) if base else spread * noise
        out[name] = __import__('jax').numpy.asarray(drawn.astype(out[name].dtype))
    for name, factor in factors.items():
        out[name] = (out[name] * factor).astype(out[name].dtype)
    return out
```

```python
import math

import numpy as np

import concourse.bass as bass
from concourse import mybir

F32 = mybir.dt.float32
I32 = mybir.dt.int32
BF16 = mybir.dt.bfloat16
ALU = mybir.AluOpType
ACT = mybir.ActivationFunctionType
AX = mybir.AxisListType

P = 128
T = 512
NT = T // P
D = 1024
KD = D // P
NEG = -1e30
TAKEN = -3e38
EPS = 1e-6
CHUNK = 3072
SLOTS = 4
FF = 2816
NFF = FF // P
TOPK = min(256, T // 4)
NCMP = (T - 32) // 16 + 1
LEVELS = 7
TWO_PI = 2.0 * math.pi
ROUND = 1.5 * 2.0 ** 23
TWO_PI_IN = 6.283184
PI_IN = 3.141592
PI_PARTS = (6.28125, 0.00193500518798828125, 3.019915981956753e-07)
LOG_FLOOR = math.log(1e-30)
MLA_SCALE = 192 ** -0.5
TURN_CHUNKS = ("up_", "ff_", "dow", "wou", "ssm")


def bucket_steps():
    d = np.arange(0, 2048)
    dl = np.maximum(d, 16).astype(np.float32)
    large = 16 + (np.log(dl / np.float32(16)) / np.float32(math.log(8)) * np.float32(16)).astype(np.int32)
    b = np.where(d < 16, d, np.minimum(large, 31))
    return [int(np.argmax(b >= n)) for n in range(1, 32)]


def constants():
    p = np.arange(P)[:, None]
    c = {}
    c["ident"] = (p == np.arange(P)).astype(np.float32)
    c["ones"] = np.ones((P, P), np.float32)
    c["causal"] = np.where(np.arange(P) <= p, 0.0, NEG).astype(np.float32)
    s, t = p, np.arange(P)[None]
    lev = [(s == t)]
    for l in range(LEVELS):
        m = 1 << l
        lev.append((s // (2 * m) == t // (2 * m)) & (s % (2 * m) < m) & (t % (2 * m) >= m))
    c["level"] = np.stack(lev, 1).astype(np.float32).reshape(P, -1)
    c["reset"] = np.broadcast_to((np.arange(T) % P != 0).astype(np.float32), (P, T))
    c["time"] = np.broadcast_to(np.arange(T, dtype=np.float32), (P, T))
    c["invf"] = np.broadcast_to((np.float32(10000.0) ** (-np.arange(0, 64, 2, dtype=np.float32) / np.float32(64))).astype(np.float32), (P, 32))
    inv = (1.0 / (np.float32(10000.0) ** (np.arange(0, 64, 2, dtype=np.float32) / np.float32(64)))).astype(np.float32)
    ang = np.arange(T, dtype=np.float32)[:, None] * inv[None]
    c["cos2"] = np.cos(ang).astype(np.float32).reshape(NT, P, 32).transpose(1, 0, 2).reshape(P, -1)
    c["sin2"] = np.sin(ang).astype(np.float32).reshape(NT, P, 32).transpose(1, 0, 2).reshape(P, -1)
    tt = np.arange(T).reshape(NT, P).T[:, :, None]
    ok = (np.arange(NCMP) * 16 + 31)[None, None] <= tt
    c["cmp_neg"] = np.where(ok, 0.0, NEG).astype(np.float32).reshape(P, -1)
    c["cmp_ok"] = ok.astype(np.float32).reshape(P, -1)
    c["misc"] = np.tile(np.array([-0.5, EPS, math.pi / 2, -LOG_FLOOR], np.float32), (P, 1))
    return c


def tiles_of(w, cols):
    w = w[:, cols]
    return w.reshape(w.shape[0] // P, P, w.shape[1]).transpose(1, 0, 2).reshape(P, -1)


SPLITS = [512, 128, 128, 512, 64, 8, 512, 512, 512, 512, 384, 256, 64, 3072]
NAMES = ["aq", "ak", "av", "iq", "ik", "iw", "bq", "bf", "bi", "bg", "cq", "ckv", "ckpe", "gate"]
AT1 = dict(zip(NAMES, np.cumsum([0] + SPLITS[:-1]).tolist()))
SPLITS2 = [512] + [128] * 6 + [512, 24, 512, 512]
NAMES2 = ["q", "kcr", "vcr", "ksl", "vsl", "kwn", "vwn", "za", "gbr", "u", "zs"]
AT2 = dict(zip(NAMES2, np.cumsum([0] + SPLITS2[:-1]).tolist()))

PROJ1 = [("iq", 0), ("iq", 1), ("iq", 2), ("iq", 3), ("ik", 0), ("bf", 0)]
PROJ1B = ([("bf", 1), ("bf", 2), ("bf", 3)] + [("bq", i) for i in range(4)] + [("aq", i) for i in range(4)]
          + [("ak", 0)] + [("bg", i) for i in range(4)])
PROJ2 = [("kcr", 0), ("vcr", 0)] + [("u", i) for i in range(4)] + [("za", i) for i in range(4)] + [("zs", i) for i in range(4)]


def columns(name, i, at):
    if name == "ik":
        one = np.arange(at["ik"], at["ik"] + 64)
        return np.concatenate([one, one])
    return np.arange(at[name] + P * i, at[name] + P * (i + 1))


def by_threes(tiles):
    return [tiles[i:i + 3] for i in range(0, len(tiles), 3)]


def span(at, *parts):
    return np.concatenate([np.arange(at[n] + a, at[n] + b) for n, a, b in parts])


ROWS1 = [("av", [("av", 0, 128), ("iw", 0, 8), ("ckpe", 0, 64)])]
ROWS1B = [("bi0", [("bi", 0, 384)]), ("bi1", [("bi", 384, 512), ("ckv", 0, 256)]), ("cq", [("cq", 0, 384)])]
ROWS2 = [("q0", [("q", 0, 384)]), ("q1", [("q", 384, 512), ("ksl", 0, 128), ("vsl", 0, 128)]),
         ("w", [("kwn", 0, 128), ("vwn", 0, 128), ("gbr", 0, 24)])]


def plan():
    out = [(f"proj1_{i}", len(c) * KD * P) for i, c in enumerate(by_threes(PROJ1))]
    out += [("rows1_av", KD * 200)]
    out += [(f"proj1b_{i}", len(c) * KD * P) for i, c in enumerate(by_threes(PROJ1B))]
    out += [(f"rows1_{n}", KD * 384) for n, _ in ROWS1B]
    out += [("qb", 3 * 768), ("kvb", 2 * 1024)]
    for j in range(8):
        out.append((f"gate_{j}", 3 * KD * P))
        if j % 2 == 0:
            out.append((f"up_{j // 2}", 2 * 3 * 4 * P))
    out += [(f"wout_{i}", len(c) * KD * P) for i, c in enumerate(by_threes(range(8)))]
    out += [(f"ff_{j}", 2 * KD * P) for j in range(NFF)]
    out += [(f"down_{j}", NFF * P) for j in range(8)]
    out += [(f"ada_{i}", 3 * KD * P) for i in range(8)]
    out += [(f"proj2_{i}", len(c) * KD * P) for i, c in enumerate(by_threes(PROJ2))]
    out += [(f"rows2_{n}", KD * sum(b - a for _, a, b in parts)) for n, parts in ROWS2]
    out += [(f"cmp_{kv}{i}", 256 * n) for kv in "kv" for i, n in enumerate((12, 12, 8))]
    out += [("ssm", 4 * 512), ("glu", 4 * 512)]
    out += [(f"wout2_{i}", len(c) * KD * P) for i, c in enumerate(by_threes(range(8)))]
    return out


def weight_stream(a):
    out = np.zeros((len(plan()), P, CHUNK), np.float32)
    at = {n: i for i, (n, _) in enumerate(plan())}

    def put(name, block):
        out[at[name], :, :block.shape[1]] = block

    w = a["w_in"][0]
    for tag, tiles in (("proj1", PROJ1), ("proj1b", PROJ1B)):
        for i, c in enumerate(by_threes(tiles)):
            put(f"{tag}_{i}", np.concatenate([tiles_of(w, columns(n, k, AT1)) for n, k in c], 1))
    for n, parts in ROWS1 + ROWS1B:
        put(f"rows1_{n}", tiles_of(w, span(AT1, *parts)))
    h = np.arange(4)[:, None]
    put("qb", tiles_of(a["mla_w_qb"][0], np.concatenate([(h * 192 + np.arange(128)).ravel(), (h * 192 + 128 + np.arange(64)).ravel()])))
    put("kvb", tiles_of(a["mla_w_kvb"][0], np.concatenate([(h * 256 + np.arange(128)).ravel(), (h * 256 + 128 + np.arange(128)).ravel()])))
    for j in range(8):
        put(f"gate_{j}", np.concatenate([tiles_of(w, AT1["gate"] + D * b + P * j + np.arange(P)) for b in range(3)], 1))
        if j % 2 == 0:
            put(f"up_{j // 2}", np.concatenate([tiles_of(a[f"w_up_{b}"][0], P * (j + e) + np.arange(P)) for e in range(2) for b in "abc"], 1))
    for i, c in enumerate(by_threes(range(8))):
        put(f"wout_{i}", np.concatenate([tiles_of(a["w_out"][0], P * j + np.arange(P)) for j in c], 1))
        put(f"wout2_{i}", np.concatenate([tiles_of(a["w_out_2"][0], P * j + np.arange(P)) for j in c], 1))
    for j in range(NFF):
        put(f"ff_{j}", np.concatenate([tiles_of(a[n][0], P * j + np.arange(P)) for n in ("w_ffn_gate", "w_ffn_up")], 1))
    for j in range(8):
        put(f"down_{j}", tiles_of(a["w_ffn_down"][0], P * j + np.arange(P)))
        put(f"ada_{j}", np.concatenate([tiles_of(a["w_ada_2"][0], P * (3 * j + e) + np.arange(P)) for e in range(3)], 1))
    w2 = a["w_in_2"][0]
    for i, c in enumerate(by_threes(PROJ2)):
        put(f"proj2_{i}", np.concatenate([tiles_of(w2, columns(n, k, AT2)) for n, k in c], 1))
    for n, parts in ROWS2:
        put(f"rows2_{n}", tiles_of(w2, span(AT2, *parts)))
    for kv in "kv":
        m = a[f"cmp_w1_{kv}_2"][0].reshape(32, 64, 256).transpose(1, 0, 2).reshape(64, -1)
        m = np.concatenate([m, m], 0)
        for i, (lo, n) in enumerate(((0, 12), (12, 12), (24, 8))):
            put(f"cmp_{kv}{i}", m[:, lo * 256:(lo + n) * 256])
    put("ssm", state_space_matrices(a))
    put("glu", tiles_of(a["glu_w_2"][0], np.arange(512)))
    return out


def small_inputs(a):
    def col(v):
        return v.reshape(-1, P).T

    def row(v):
        return np.broadcast_to(v.reshape(1, -1), (P, v.size))

    c = {
        "g_attn": col(a["attn_norm"][0]), "g_ffn": col(a["ffn_norm"][0]), "g_final": col(a["final_norm"]),
        "g_cq": col(a["mla_q_norm"][0]), "g_ckv": col(a["mla_kv_norm"][0]), "g_ob": col(a["hgrn_out_norm"][0]),
        "g_2": col(a["norm_g_2"][0]), "b_ada": col(a["b_ada_2"][0]), "c2": col(a["c_2"][0]),
        "glu_b": col(a["glu_b_2"][0]), "ssm_d": col(a["ssm_d_2"][0]), "rel": row(a["rel_bias"]),
        "g_q": row(a["q_norm_g_2"][0]), "g_kc": row(a["k_cmp_norm_g_2"][0]), "g_ks": row(a["k_slc_norm_g_2"][0]),
        "g_kw": row(a["k_win_norm_g_2"][0]),
    }
    for kv in "kv":
        pos = a[f"cmp_pos_{kv}_2"][0].T
        c[f"pos_{kv}"] = np.concatenate([pos, pos], 0)
        c[f"w2_{kv}"] = tiles_of(a[f"cmp_w2_{kv}_2"][0], np.arange(64))
    c["a_re"] = a["ssm_a_re_2"][0].reshape(16, P).T
    c["a_im"] = a["ssm_a_im_2"][0].reshape(16, P).T
    c["log_dt"] = np.repeat(a["ssm_log_dt_2"][0].reshape(16, 2), 64, axis=1).T
    return c


def state_space_matrices(a):
    parts = []
    for z in ("re", "im"):
        b = a[f"ssm_b_{z}_2"][0]
        m = np.zeros((P, 4, P), np.float32)
        for g in range(32):
            ct, r = divmod(g, 8)
            m[16 * r:16 * r + 16, ct, 64 * (g % 2):64 * (g % 2) + 64] = b[g].T
        parts.append(m.reshape(P, -1))
        cc = a[f"ssm_c_{z}_2"][0]
        m = np.zeros((P, 16, 32), np.float32)
        for g in range(32):
            m[64 * (g % 2):64 * (g % 2) + 64, g // 2, 16 * (g % 2):16 * (g % 2) + 16] = cc[g].T
        parts.append(m.reshape(P, -1))
    return np.concatenate(parts, 1)


SMALL = {"g_attn": 8, "g_ffn": 8, "g_final": 8, "g_cq": 3, "g_ckv": 2, "g_ob": 1, "g_2": 8, "b_ada": 24, "c2": 8,
         "glu_b": 4, "ssm_d": 4, "rel": 128, "g_q": 64, "g_kc": 64, "g_ks": 64, "g_kw": 64, "pos_k": 32, "w2_k": 128,
         "pos_v": 32, "w2_v": 128, "a_re": 16, "a_im": 16, "log_dt": 16}
CONST = {"ident": P, "ones": P, "causal": P, "level": (LEVELS + 1) * P, "reset": T, "time": T, "invf": 32,
         "cos2": P, "sin2": P, "cmp_neg": NT * NCMP, "cmp_ok": NT * NCMP, "misc": 4}


def offsets(sizes):
    at, out = 0, {}
    for n, k in sizes.items():
        out[n] = (at, at + k)
        at += k
    return out, at


class Tally:

    def __init__(self, known):
        self.count, self.known, self.named = {}, known, {}

    def up(self, sem, name=None, by=1):
        n = self.count[sem.name] = self.count.get(sem.name, 0) + by
        if name is not None:
            assert name not in self.named, name
            self.named[name] = n
        return n

    def at(self, name):
        return self.known[name] if self.known is not None else 1


def two_blocks_kernel(nc, wstream, xT, consts, small, pos_row, pos_col, outT, known):
    tally = Tally(known)
    up, at = tally.up, tally.at

    def sb(name, cols, dt=F32):
        return nc.alloc_sbuf_tensor(name, [P, cols], dt)

    ring = sb("ring", SLOTS * CHUNK)
    x_sb = sb("x_sb", KD * T)
    h_sb = sb("h_sb", KD * T)
    tiles = sb("tiles", 22 * T)
    rows = sb("rows", NT * 712)
    wide = sb("wide", 5760)
    work = sb("work", 4608)
    probs = sb("probs", 2 * T)
    probsT = sb("probsT", 2 * T)
    cst = sb("cst", sum(CONST.values()))
    sml = sb("sml", sum(SMALL.values()))
    chosen = sb("chosen", NT * (NT + 1) // 2 * P, BF16)
    prow = sb("prow", T, I32)
    pcol = sb("pcol", NT, I32)
    stat = sb("stat", 512)
    trig = sb("trig", 2 * NT * 32)

    X = x_sb[:, :].rearrange("p (k t) -> p k t", k=KD)
    H = h_sb[:, :].rearrange("p (k t) -> p k t", k=KD)
    TL = tiles[:, :].rearrange("p (k t) -> p k t", k=22)
    ROW = rows[:, :].rearrange("p (n c) -> p n c", n=NT)
    coff, _ = offsets(CONST)
    soff, _ = offsets(SMALL)

    def con(name):
        a, b = coff[name]
        return cst[:, a:b]

    def sm(name):
        a, b = soff[name]
        return sml[:, a:b]

    ident, ones, causal = con("ident"), con("ones"), con("causal")
    G = [nc.alloc_psum_tensor(f"gemm{i}", [P, T], F32) for i in range(3)]
    S = [nc.alloc_psum_tensor(f"score{i}", [P, T], F32) for i in range(2)]
    U = [nc.alloc_psum_tensor(f"turn{i}", [P, T], F32) for i in range(2)]
    O = [nc.alloc_psum_tensor("sum0", [P, T], F32)]

    def part(t, a, n, **shape):
        v = t[:, a:a + n]
        return v.rearrange("p (k t) -> p k t", **shape) if shape else v

    REC_E = [part(work, 0, T), part(work, T, T)]
    REC_QK = [part(work, 2 * T, T), part(work, 3 * T, T)]
    REC_QX, REC_KX, REC_AT = part(work, 4 * T, T), part(work, 5 * T, T), part(work, 6 * T, T)
    REC_X = part(work, 7 * T, 6 * P)
    REC_O, REC_QS = part(wide, 2560, 4 * T, k=NT), part(wide, 4608, 3 * P)

    def REC_FAR(a, c):
        i = {(0, 1): 0, (1, 2): 1, (2, 3): 2, (0, 2): 3, (1, 3): 4, (0, 3): 5}[a, c]
        return REC_X[:, i * P:(i + 1) * P]

    CQ, CKV = part(wide, 0, 1536, k=NT), part(wide, 1536, 1024, k=NT)
    VC, QPE = part(wide, 2560, 2048, k=NT), part(wide, 4608, 1024, k=NT)
    KPE2 = part(wide, 0, 512, k=NT)
    CQT, CKVT = part(work, 0, 1536, k=3), part(work, 1536, 1024, k=2)
    QPET, KPET = part(work, 2560, 1024, k=2), part(work, 3584, T)
    BIAS = part(wide, 0, 5120, k=4)
    INDEX = [None] + [part(work, n * T, (n + 1) * P) for n in range(1, NT)]
    LOGITS = [part(work, 4 * T, T), part(work, 5 * T, T)]

    def upto(n):
        return n * (n + 1) // 2 * P

    MIX = [0, 1, 2, 3, 4, 18, 19, 20]
    GATE = [part(work, (6 + b) * T, T) for b in range(3)]
    SILU_C, MOD, GAIN2, POSB = stat[:, 192:200], stat[:, 200:224], stat[:, 224:232], stat[:, 232:240]
    R2 = part(wide, 0, NT * 1048, k=NT)
    KT2 = part(rows, 0, 4 * T, k=4)

    def HID(kv):
        return rows[:, 2048 + 128 * (kv == "v"):2176 + 128 * (kv == "v")].rearrange("p (g k t) -> p g k t", g=2, k=2)

    KC2, VCMP, KCT = part(rows, 2304, 256, k=2), part(rows, 2560, 128), part(rows, 2688, 64)
    CMP_P = part(probs, 0, 4 * NCMP)
    ATT = part(work, 0, 4 * T, k=NT)

    def K2(i):
        return part(work, 4 * T + i * T, T, k=NT)

    GB = [part(wide, 4712 + 32 * z, 32, k=NT) for z in range(3)]
    KCRAW = part(work, 0, P)
    GLUB = stat[:, 236:240]
    CC = [part(rows, 0, 512, k=16), part(rows, 512, 512, k=16)]

    def SSM(name):
        return part(work, ["sr", "si", "zr", "zi", "t1", "t2"].index(name) * T, T)

    TURNS, SIN, COS = [[part(wide, (2 * a + b) * T, T) for b in range(2)] for a in range(3)]
    SC = {n: stat[:, 240 + 16 * i:256 + 16 * i] for i, n in enumerate(
        ("dt", "turn", "hi", "lo", "rho", "t", "u", "s", "c", "h", "x", "y", "den", "kr", "ki", "v"))}

    def sem(name):
        return nc.alloc_semaphore(name)

    const_in, small_in, x_in = sem("const_in"), sem("small_in"), sem("x_in")
    slot_in = [sem(f"slot{i}_in") for i in range(SLOTS)]
    gemm_full, gemm_done = sem("gemm_full"), sem("gemm_done")
    score_full, score_done = sem("score_full"), sem("score_done")
    turn_full, turn_done = sem("turn_full"), sem("turn_done")
    sum_full, sum_done = sem("sum_full"), sem("sum_done")
    act_step, dve_step, pool_step = sem("act_step"), sem("dve_step"), sem("pool_step")
    stored = sem("stored")

    chunks = plan()
    chunk_at = {n: i for i, (n, _) in enumerate(chunks)}

    def chunk(name):
        i = chunk_at[name]
        return ring[:, (i % SLOTS) * CHUNK:(i % SLOTS) * CHUNK + chunks[i][1]]

    block = nc.Block()
    with block:
        @block.sync
        def _(sp):
            sp.dma_start(cst[:, :], consts).then_inc(const_in, 16)
            sp.dma_start(sml[:, :], small).then_inc(small_in, 16)
            sp.dma_start(x_sb[:, :], xT).then_inc(x_in, 16)
            sp.dma_start(prow[:, :], pos_row).then_inc(small_in, 16)
            sp.dma_start(pcol[:, :], pos_col).then_inc(small_in, 16)
            for i, (name, cols) in enumerate(chunks):
                if i >= SLOTS:
                    last = chunks[i - SLOTS][0]
                    sp.wait_ge(turn_full if last[:3] in TURN_CHUNKS else gemm_full, at(f"used {last}"))
                sp.dma_start(ring[:, (i % SLOTS) * CHUNK:(i % SLOTS) * CHUNK + cols],
                             wstream[i, :, 0:cols]).then_inc(slot_in[i % SLOTS], 16)
            sp.wait_ge(dve_step, at("out ready"))
            sp.dma_start(outT, x_sb[:, :]).then_inc(stored, 16)
            sp.wait_ge(stored, 16)

        @block.tensor
        def _(pe):
            seen, sums = set(), [0]

            def have(name):
                if name not in seen:
                    seen.add(name)
                    i = chunk_at[name]
                    pe.wait_ge(slot_in[i % SLOTS], 16 * (i // SLOTS + 1))
                return chunk(name)

            def gemm_bank():
                n = tally.count.get("gemm_full", 0)
                if n >= 3:
                    pe.wait_ge(gemm_done, n - 2)
                return G[n % 3]

            def score_bank():
                n = tally.count.get("score_full", 0)
                if n >= 2:
                    pe.wait_ge(score_done, n - 1)
                return S[n % 2]

            def turn_bank():
                n = tally.count.get("turn_full", 0)
                if n >= 2:
                    pe.wait_ge(turn_done, n - 1)
                return U[n % 2]

            def sum_bank():
                n = sums[0]
                sums[0] += 1
                if n >= 1:
                    pe.wait_ge(sum_done, n)
                return O[0]

            def product(out, pairs):
                for i, (l, r) in enumerate(pairs):
                    mm = pe.matmul(out, l, r, start=(i == 0), stop=(i == len(pairs) - 1))
                return mm

            def feature_tiles(tag, tiles_, acts, to_turn=False):
                full = turn_full if to_turn else gemm_full
                for i, c in enumerate(by_threes(tiles_)):
                    w = have(f"{tag}_{i}").rearrange("p (c k n) -> p c k n", c=len(c), k=KD)
                    for e in range(len(c)):
                        b = turn_bank() if to_turn else gemm_bank()
                        mm = product(b[:, :], [(w[:, e, k, :], acts(k)) for k in range(KD)])
                        mm.then_inc(full, 1)
                        up(full)
                    tally.named[f"used {tag}_{i}"] = tally.count[full.name]

            def row_tiles(chunk_name, cols, acts, kt=KD):
                w = have(chunk_name).rearrange("p (k n) -> p k n", k=kt)
                for n in range(NT):
                    b = gemm_bank()
                    mm = product(b[:, 0:cols], [(acts[:, k, n * P:(n + 1) * P], w[:, k, :]) for k in range(kt)])
                    mm.then_inc(gemm_full, 1)
                    up(gemm_full, f"full {chunk_name} {n}")
                tally.named[f"used {chunk_name}"] = tally.count["gemm_full"]

            def square_sums(name, src):
                pe.wait_ge(dve_step, at(f"squares {name}"))
                b = gemm_bank()
                product(b[:, :], [(ones, src[:, k, :]) for k in range(KD)]).then_inc(gemm_full, 1)
                up(gemm_full, f"full sums {name}")

            def turn(name, blocks, ready):
                b = turn_bank()
                pe.wait_ge(*ready)
                for src, r, dst in blocks:
                    mm = pe.transpose(b[0:src.shape[1], dst:dst + r], src, ident[0:r, 0:r])
                mm.then_inc(turn_full, 1)
                up(turn_full, f"full turn {name}")

            def attention(name, heads, query, key, value, width, before, turn_o=True):
                items = [(n, h) for n in range(NT) for h in range(heads)]
                last = len(items)
                for i in range(last + 3):
                    if i < last:
                        n, h = items[i]
                        cols = (n + 1) * P
                        b = score_bank()
                        if h == 0:
                            before(n)
                        pairs = [(q[:, n * P:(n + 1) * P], k[:, 0:cols]) for q, k in zip(query(h), key(h))]
                        for j, (l, r) in enumerate(pairs):
                            mm = pe.matmul(b[:, 0:cols], l, r, start=(j == 0), stop=False)
                        mm = pe.matmul(b[:, n * P:cols], ident, causal, start=False, stop=True)
                        mm.then_inc(score_full, 1)
                        up(score_full, f"full {name} score {i}")
                    if 1 <= i <= last:
                        n, h = items[i - 1]
                        b = turn_bank()
                        pe.wait_ge(score_done, at(f"{name} probs {i - 1}"))
                        for j in range(n + 1):
                            mm = pe.transpose(b[:, j * P:(j + 1) * P],
                                              probs[:, (i - 1) % 2 * T + j * P:(i - 1) % 2 * T + (j + 1) * P], ident)
                        mm.then_inc(turn_full, 1)
                        up(turn_full, f"full {name} turn {i - 1}")
                    if 2 <= i <= last + 1:
                        n, h = items[i - 2]
                        if h == 0:
                            b = sum_bank()
                        pe.wait_ge(turn_done, at(f"{name} probsT {i - 2}"))
                        for j in range(n + 1):
                            mm = pe.matmul(O[0][:, h * width:(h + 1) * width],
                                           probsT[:, (i - 2) % 2 * T + j * P:(i - 2) % 2 * T + (j + 1) * P],
                                           value(h, j), start=(j == 0), stop=(j == n))
                        mm.then_inc(sum_full, 1)
                        up(sum_full, f"{name} summed {i - 2}")
                    if i >= 3 and items[i - 3][1] == heads - 1:
                        n = items[i - 3][0]
                        if turn_o:
                            turn(f"{name} o {n}", [(work[:, j * P:(j + 1) * P], P, j * P) for j in range(4)],
                                 (sum_done, at(f"{name} o {n}")))


            def rows_out(name, cols, acts, w, kt, used):
                for n in range(NT):
                    b = gemm_bank()
                    product(b[:, 0:cols], [(acts(k)[:, n * P:(n + 1) * P], w(k)) for k in range(kt)]).then_inc(gemm_full, 1)
                    up(gemm_full)

            pe.wait_ge(const_in, 16)
            square_sums("attn", H)
            pe.wait_ge(dve_step, at("normed attn"))
            feature_tiles("proj1", PROJ1, lambda k: H[:, k, :])
            row_tiles("rows1_av", 200, H)
            pe.wait_ge(gemm_done, at("have ik"))
            for i in range(3 * 8):
                n, h = 1 + i // 8, i % 8
                b, r = score_bank(), slice(64 * (h % 2), 64 * (h % 2) + 64)
                pe.matmul(b[:, 0:(n + 1) * P], TL[r, h // 2, n * P:(n + 1) * P], TL[r, 4, 0:(n + 1) * P],
                          start=True, stop=True).then_inc(score_full, 1)
                up(score_full, f"full index {i}")
            feature_tiles("proj1b", PROJ1B, lambda k: H[:, k, :])
            for n_ in ("bi0", "bi1", "cq"):
                row_tiles(f"rows1_{n_}", 384, H)

            V = ROW[:, :, 200:712]
            for h in range(4):
                q, k = TL[:, 9 + h, :], TL[:, h, :]
                pe.wait_ge(gemm_done, at("have bg"))
                pe.wait_ge(dve_step, at("keys rec"))

                def blocks(name, pairs, ready):
                    b = turn_bank()
                    pe.wait_ge(dve_step, at(ready))
                    for j, (l, r) in enumerate(pairs):
                        mm = pe.matmul(b[:, j * P:(j + 1) * P], l, r, start=True, stop=True)
                    mm.then_inc(turn_full, 1)
                    up(turn_full, name)

                def ch(a, c):
                    return a[:, c * P:(c + 1) * P]

                blocks(f"full rec diag {h}", [(ch(k, c), ch(q, c)) for c in range(4)], "keys rec")
                blocks(f"full rec near {h}", [(ch(REC_KX, 0), ch(REC_QX, 1)), (ch(REC_KX, 1), ch(REC_QX, 2)),
                                              (ch(REC_KX, 2), ch(REC_QX, 3)), (ch(REC_KX, 0), ch(REC_QS, 0))], f"rec cross {h}")
                blocks(f"full rec far {h}", [(ch(REC_KX, 1), ch(REC_QS, 1)), (ch(REC_KX, 0), ch(REC_QS, 2))], f"rec cross {h}")
                for l in range(LEVELS):
                    qk = REC_QK[l % 2]
                    blocks(f"full rec level {h} {l}", [(ch(qk, c), ch(qk, c)) for c in range(4)], f"rec scaled {h} {l}")
                b = sum_bank()
                pe.wait_ge(turn_done, at(f"rec weights {h}"))
                for c in range(4):
                    parts = [(REC_FAR(a, c), V[:, a, h * P:(h + 1) * P]) for a in range(c)] + [(ch(REC_AT, c), V[:, c, h * P:(h + 1) * P])]
                    mm = product(b[:, c * P:(c + 1) * P], parts)
                mm.then_inc(sum_full, 1)
                up(sum_full, f"full rec o {h}")
            for n in range(NT):
                turn(f"rec o {n}", [(REC_O[:, n, j * P:(j + 1) * P], P, j * P) for j in range(4)], (dve_step, at("rec normed")))

            for j in range(3):
                turn(f"cq {j}", [(CQ[:, n, j * P:(j + 1) * P], P, n * P) for n in range(NT)], (dve_step, at("latents normed")))
            for j in range(2):
                turn(f"ckv {j}", [(CKV[:, n, j * P:(j + 1) * P], P, n * P) for n in range(NT)], (dve_step, at("latents normed")))
            pe.wait_ge(turn_done, at("ckvT"))
            w = have("qb").rearrange("p (k n) -> p k n", k=3)
            for j in range(4):
                b = gemm_bank()
                product(b[:, :], [(w[:, k, j * P:(j + 1) * P], CQT[:, k, :]) for k in range(3)]).then_inc(gemm_full, 1)
                up(gemm_full)
            rows_out("qpe", 256, lambda k: CQT[:, k, :], lambda k: w[:, k, 512:768], 3, "qb")
            tally.named["used qb"] = tally.count["gemm_full"]
            w2 = have("kvb").rearrange("p (k n) -> p k n", k=2)
            for j in range(4):
                b = gemm_bank()
                product(b[:, :], [(w2[:, k, j * P:(j + 1) * P], CKVT[:, k, :]) for k in range(2)]).then_inc(gemm_full, 1)
                up(gemm_full)
            rows_out("vc", 512, lambda k: CKVT[:, k, :], lambda k: w2[:, k, 512:1024], 2, "kvb")
            tally.named["used kvb"] = tally.count["gemm_full"]
            turn("kpe", [(KPE2[:, n, :], P, n * P) for n in range(NT)], (dve_step, at("roped")))
            for j in range(2):
                turn(f"qpe {j}", [(QPE[:, n, j * P:(j + 1) * P], P, n * P) for n in range(NT)], (dve_step, at("roped")))
            pe.wait_ge(turn_done, at("qpeT"))
            pe.wait_ge(gemm_done, at("have vc"))

            def half(t, h):
                return t[64 * (h % 2):64 * (h % 2) + 64]

            attention("mla", 4, lambda h: [TL[:, 5 + h, :], half(QPET[:, h // 2, :], h)],
                      lambda h: [TL[:, h, :], half(KPET, h)],
                      lambda h, j: VC[:, j, h * P:(h + 1) * P], P, lambda n: None)
            attention("dsa", 4, lambda h: [TL[:, 13 + h, :]], lambda h: [TL[:, 17, :]],
                      lambda h, j: ROW[:, j, 0:128], P, lambda n: None)

            branch = {0: 13, 1: 9, 2: 5}
            for j in range(8):
                w = have(f"gate_{j}").rearrange("p (b k n) -> p b k n", b=3, k=KD)
                for b_ in range(3):
                    b = gemm_bank()
                    product(b[:, :], [(w[:, b_, k, :], H[:, k, :]) for k in range(KD)]).then_inc(gemm_full, 1)
                    up(gemm_full)
                tally.named[f"used gate_{j}"] = tally.count["gemm_full"]
                w = have(f"up_{j // 2}").rearrange("p (e b k n) -> p e b k n", e=2, b=3, k=4)
                if j == 0:
                    pe.wait_ge(turn_done, at("dsa oT 3"))
                for b_ in range(3):
                    b = turn_bank()
                    product(b[:, :], [(w[:, j % 2, b_, k, :], TL[:, branch[b_] + k, :]) for k in range(4)]).then_inc(turn_full, 1)
                    up(turn_full)
                if j % 2:
                    tally.named[f"used up_{j // 2}"] = tally.count["turn_full"]
            pe.wait_ge(dve_step, at("mixed"))
            feature_tiles("wout", range(8), lambda k: TL[:, MIX[k], :], to_turn=True)

            square_sums("ffn", H)
            pe.wait_ge(dve_step, at("normed ffn"))
            for j in range(NFF):
                w = have(f"ff_{j}").rearrange("p (b k n) -> p b k n", b=2, k=KD)
                b = gemm_bank()
                product(b[:, :], [(w[:, 0, k, :], H[:, k, :]) for k in range(KD)]).then_inc(gemm_full, 1)
                up(gemm_full)
                b = turn_bank()
                product(b[:, :], [(w[:, 1, k, :], H[:, k, :]) for k in range(KD)]).then_inc(turn_full, 1)
                up(turn_full)
                tally.named[f"used ff_{j}"] = tally.count["turn_full"]
            pe.wait_ge(turn_done, at("ff hidden"))
            for j in range(8):
                w = have(f"down_{j}").rearrange("p (k n) -> p k n", k=NFF)
                b = turn_bank()
                product(b[:, :], [(w[:, k, :], TL[:, k, :]) for k in range(NFF)]).then_inc(turn_full, 1)
                up(turn_full)
                tally.named[f"used down_{j}"] = tally.count["turn_full"]
            square_sums("final", H)

            pe.wait_ge(dve_step, at("silu c"))
            for i in range(8):
                b = gemm_bank()
                w = have(f"ada_{i}").rearrange("p (c k n) -> p c k n", c=3, k=KD)
                for e in range(3):
                    mm = product(b[:, e:e + 1], [(w[:, e, k, :], SILU_C[:, k:k + 1]) for k in range(KD)])
                mm.then_inc(gemm_full, 1)
                up(gemm_full, f"used ada_{i}")
            square_sums("block2", H)
            pe.wait_ge(dve_step, at("normed block2"))
            feature_tiles("proj2", PROJ2, lambda k: H[:, k, :])
            row_tiles("rows2_q0", 384, H)
            row_tiles("rows2_q1", 384, H)
            row_tiles("rows2_w", 280, H)

            pe.wait_ge(gemm_done, at("have zs"))
            for kv, tile in (("k", 0), ("v", 1)):
                pos = sm(f"pos_{kv}")
                parts = [(have(f"cmp_{kv}{i}").rearrange("p (l n) -> p l n", n=256), lo, n)
                         for i, (lo, n) in enumerate(((0, 12), (12, 12), (24, 8)))]
                for g in range(2):
                    r = slice(64 * g, 64 * g + 64)
                    b = gemm_bank()
                    for hid in range(2):
                        mm = product(b[:, 32 * hid:32 * hid + NCMP],
                                     [(w[r, l, hid * P:(hid + 1) * P], TL[r, tile, lo + l:lo + l + 16 * NCMP - 15:16])
                                      for w, lo, n in parts for l in range(n)])
                        mm = product(b[:, 32 * hid + 31:32 * hid + 32],
                                     [(w[r, l, hid * P:(hid + 1) * P], pos[r, lo + l:lo + l + 1])
                                      for w, lo, n in parts for l in range(n)])
                    mm.then_inc(gemm_full, 1)
                    up(gemm_full)
                for i in range(3):
                    tally.named[f"used cmp_{kv}{i}"] = tally.count["gemm_full"]
            for kv in "kv":
                b = gemm_bank()
                pe.wait_ge(act_step, at(f"hidden {kv}"))
                w2_ = sm(f"w2_{kv}").rearrange("p (k n) -> p k n", k=2)
                for g in range(2):
                    mm = product(b[0:NCMP, 64 * g:64 * g + 64], [(HID(kv)[:, g, k, 0:NCMP], w2_[:, k, :]) for k in range(2)])
                mm.then_inc(gemm_full, 1)
                up(gemm_full)
            turn("kc", [(KC2[0:NCMP, g, :], NCMP, 32 * g) for g in range(2)], (dve_step, at("kc normed")))
            for j in range(4):
                turn(f"q {j}", [(R2[:, n, j * P:(j + 1) * P], P, n * P) for n in range(NT)], (dve_step, at("q normed")))
            for j in range(4):
                turn(f"qr {j}", [(R2[:, n, j * P:(j + 1) * P], P, n * P) for n in range(NT)], (dve_step, at("q roped")))
            for i in range(4):
                turn(f"k2 {i}", [(K2(i)[:, n, :], P, n * P) for n in range(NT)], (dve_step, at("k roped")))
            pe.wait_ge(turn_done, at("kT 3"))
            def cmp_scores(i):
                n, e = divmod(i, 2)
                b = score_bank()
                for q_ in range(4):
                    h = 2 * q_ + e
                    r = slice(64 * e, 64 * e + 64)
                    mm = pe.matmul(b[:, q_ * NCMP:(q_ + 1) * NCMP], TL[r, 14 + h // 2, n * P:(n + 1) * P],
                                   KCT[r, 32 * (h // 4):32 * (h // 4) + NCMP], start=True, stop=True)
                mm.then_inc(score_full, 1)
                up(score_full, f"full cmp {i}")

            for i in range(8):
                cmp_scores(i)
                n, e = divmod(i, 2)
                b = turn_bank()
                pe.wait_ge(dve_step, at(f"cmp probs {i}"))
                for q_ in range(4):
                    mm = pe.transpose(b[0:NCMP, q_ * P:(q_ + 1) * P], CMP_P[:, q_ * NCMP:(q_ + 1) * NCMP], ident)
                mm.then_inc(turn_full, 1)
                up(turn_full)
                if e == 0:
                    b = sum_bank()
                pe.wait_ge(turn_done, at(f"cmp probsT {i}"))
                for q_ in range(4):
                    h = 2 * q_ + e
                    mm = pe.matmul(O[0][:, 64 * h:64 * h + 64], probsT[0:NCMP, q_ * P:(q_ + 1) * P],
                                   VCMP[0:NCMP, 64 * (h // 4):64 * (h // 4) + 64], start=True, stop=True)
                mm.then_inc(sum_full, 1)
                up(sum_full, f"cmp summed {i}")

            def both(t, h):
                return t[64 * (h % 2):64 * (h % 2) + 64, :]

            for a_, name in enumerate(("slc", "win")):
                attention(name, 8, lambda h: [both(TL[:, 18 + h // 2, :], h)],
                          lambda h: [both(KT2[:, 2 * a_ + h // 4, :], h)],
                          lambda h, j: R2[:, j, (640 if a_ == 0 else 896) + 64 * (h // 4):(640 if a_ == 0 else 896) + 64 * (h // 4) + 64],
                          64, lambda n: None, turn_o=False)
            for n in range(NT):
                turn(f"attn {n}", [(ATT[:, n, j * P:(j + 1) * P], P, j * P) for j in range(4)], (sum_done, at("win o 3")))

            wssm = have("ssm")
            B = [wssm[:, 0:512].rearrange("p (c n) -> p c n", c=4), wssm[:, 1024:1536].rearrange("p (c n) -> p c n", c=4)]
            for j in range(17):
                if j < 16:
                    r = slice(32 * (j % 4), 32 * (j % 4) + 32)
                    for z in range(2):
                        b = turn_bank()
                        mm = pe.matmul(b[:, :], B[z][r, j // 4, :], TL[r, 2 + j // 4, :], start=True, stop=True)
                        mm.then_inc(turn_full, 1)
                        up(turn_full, f"full bu {j} {z}")
                if j >= 1:
                    i = j - 1
                    if i % 4 == 0:
                        b = sum_bank()
                    pe.wait_ge(dve_step, at(f"states {i}"))
                    q_ = slice(32 * (i % 4), 32 * (i % 4) + 32)
                    pe.matmul(O[0][q_, :], CC[0][:, i, :], SSM("sr"), start=True, stop=False)
                    mm = pe.matmul(O[0][q_, :], CC[1][:, i, :], SSM("si"), start=False, stop=True)
                    mm.then_inc(sum_full, 1)
                    up(sum_full, f"full y {i}")
            tally.named["used ssm"] = tally.named["full bu 15 1"]
            w = have("glu").rearrange("p (k n) -> p k n", k=4)
            pe.wait_ge(act_step, at("y gelu"))
            for j in range(4):
                b = gemm_bank()
                product(b[:, :], [(w[:, k, j * P:(j + 1) * P], TL[:, 2 + k, :]) for k in range(4)]).then_inc(gemm_full, 1)
                up(gemm_full)
            tally.named["used glu"] = tally.count["gemm_full"]
            pe.wait_ge(dve_step, at("ssm out"))
            feature_tiles("wout2", range(8), lambda k: TL[:, 6 + k, :], to_turn=True)

        @block.scalar
        def _(act):
            def step(ins, name=None, sem_=act_step):
                n = up(sem_, name)
                ins.then_inc(sem_, 1)
                act.wait_ge(sem_, n)

            drained = [0]

            def drain(fills, out, name=None, func=ACT.Identity, bias=0.0, scale=1.0, cols=T, rows_=P, src=None):
                n = drained[0]
                drained[0] += 1
                act.wait_ge(gemm_full, n + 1)
                b = G[n % 3][0:rows_, 0:cols] if src is None else src(G[n % 3])
                step(act.activation(out, b, func, bias=bias, scale=scale), name, gemm_done)

            def attention_exp(name, heads, logits=None):
                for i in range(NT * heads):
                    n, h = divmod(i, heads)
                    cols = (n + 1) * P
                    act.wait_ge(dve_step, at(f"{name} max {i}"))
                    if i >= 2:
                        act.wait_ge(turn_full, at(f"full {name} turn {i - 2}"))
                    if h == 0 and n >= 2:
                        act.wait_ge(sum_done, at(f"{name} o {n - 2}"))
                    src = S[(at(f"full {name} score {i}") - 1) % 2][:, 0:cols] if logits is None else logits(i, cols)
                    step(act.activation(probs[:, i % 2 * T:i % 2 * T + cols], src, ACT.Exp,
                                        bias=stat[:, 8 + i % 2:9 + i % 2], scale=1.0,
                                        accum_out=stat[:, 16 + (n % 2) * 8 + h:17 + (n % 2) * 8 + h]),
                         f"{name} probs {i}", score_done)


            def sums_out(name):
                drain(1, work[:, 0:T], f"mean {name}", bias=con("misc")[:, 1:2], scale=1.0 / D)
                step(act.activation(work[:, T:2 * T], work[:, 0:T], ACT.Sqrt), f"root {name}")

            act.wait_ge(const_in, 16)
            sums_out("attn")
            dest = {"iq": 0, "ik": 4, "bf": 5, "bq": 9, "aq": 13, "ak": 17, "bg": 18}
            scales = {"bq": P ** -0.5, "aq": P ** -0.5, "bg": 0.5}

            def project(tiles_, names=()):
                for n, i in tiles_:
                    drain(1, TL[:, dest[n] + i, :], f"tile {n} {i}", scale=scales.get(n, 1.0))

            project(PROJ1)
            for n in range(NT):
                drain(1, ROW[:, n, 0:200], "have ik" if n == NT - 1 else None, cols=200)
            for i in range(24):
                n = 1 + i // 8
                act.wait_ge(score_full, at(f"full index {i}"))
                if i >= 2:
                    act.wait_ge(dve_step, at(f"index added {i - 2}"))
                step(act.activation(probs[:, i % 2 * T:i % 2 * T + (n + 1) * P], S[i % 2][:, 0:(n + 1) * P], ACT.Relu),
                     f"index relu {i}", score_done)
            project(PROJ1B)
            for n in range(NT):
                drain(1, ROW[:, n, 200:584], cols=384)
            for n in range(NT):
                k = drained[0]
                drained[0] += 1
                act.wait_ge(gemm_full, k + 1)
                step(act.activation(ROW[:, n, 584:712], G[k % 3][:, 0:128], ACT.Identity))
                step(act.activation(CKV[:, n, :], G[k % 3][:, 128:384], ACT.Identity), None, gemm_done)
            for n in range(NT):
                drain(1, CQ[:, n, :], "have bg" if n == NT - 1 else None, cols=384)

            f4, k4, w0 = tiles[:, 5 * T:9 * T], tiles[:, 0:4 * T], work[:, 0:4 * T]
            act.wait_ge(dve_step, at("chosen"))
            step(act.activation(k4, f4, ACT.Abs))
            step(act.activation(w0, k4, ACT.Exp, scale=-1.0), "rec u")
            step(act.activation(k4, f4, ACT.Relu))
            step(act.activation(k4, k4, ACT.Exp, scale=-1.0), "rec num")
            act.wait_ge(dve_step, at("rec one plus u"))
            step(act.activation(w0, w0, ACT.Ln, bias=1.0), "rec ln")
            act.wait_ge(dve_step, at("rec log sigmoid"))
            step(act.activation(w0, f4, ACT.Abs, bias=con("misc")[:, 3:4], scale=1.0))
            step(act.activation(w0, w0, ACT.Exp, scale=-1.0))
            step(act.activation(w0, w0, ACT.Ln, bias=1.0), "rec floor")
            act.wait_ge(dve_step, at("rec log f"))
            step(act.activation(w0, tiles[:, 18 * T:22 * T], ACT.Tanh), "rec gate")
            for h in range(4):
                bt = TL[:, 5 + h, :]
                act.wait_ge(dve_step, at(f"rec args {h}"))
                step(act.activation(REC_E[0], bt, ACT.Exp), f"rec eb {h}")
                step(act.activation(REC_E[1], REC_E[1], ACT.Exp), f"rec el {h}")
                for l in range(LEVELS):
                    act.wait_ge(dve_step, at(f"rec args {h} {l}"))
                    step(act.activation(REC_E[l % 2], REC_E[l % 2], ACT.Exp), f"rec e {h} {l}")

            for j in range(4):
                drain(1, TL[:, 5 + j, :], scale=MLA_SCALE)
            for n in range(NT):
                drain(1, QPE[:, n, :], "have qpe" if n == NT - 1 else None, scale=MLA_SCALE, cols=256)
            for j in range(4):
                drain(1, TL[:, j, :])
            for n in range(NT):
                drain(1, VC[:, n, :], "have vc" if n == NT - 1 else None)
            act.wait_ge(dve_step, at("angles"))
            step(act.activation(trig[:, P:2 * P], trig[:, 0:P], ACT.Sin))
            step(act.activation(trig[:, 0:P], trig[:, 0:P], ACT.Abs))
            step(act.activation(trig[:, 0:P], trig[:, 0:P], ACT.Sin, bias=con("misc")[:, 2:3], scale=-1.0), "trig")
            attention_exp("mla", 4)
            attention_exp("dsa", 4, lambda i, cols: LOGITS[i % 2][:, 0:cols])

            for j in range(8):
                for b_ in range(3):
                    if j >= 1 or b_ == 0:
                        act.wait_ge(dve_step, at(f"mixed {j - 1}") if j else at("dsa done"))
                    drain(1, GATE[b_], f"gate {j} {b_}", func=ACT.Tanh, scale=0.5)

            sums_out("ffn")
            for j in range(NFF):
                if j >= 2:
                    act.wait_ge(turn_done, at(f"ff {j - 2}"))
                elif j == 0:
                    act.wait_ge(dve_step, at("normed ffn"))
                k = drained[0]
                drained[0] += 1
                act.wait_ge(gemm_full, k + 1)
                step(act.activation(part(work, j % 2 * T, T), G[k % 3][:, :], ACT.Tanh, scale=0.5))
                step(act.activation(part(work, (2 + j % 2) * T, T), G[k % 3][:, :], ACT.Identity, scale=0.5),
                     f"ff gate {j}", gemm_done)
            sums_out("final")
            act.wait_ge(small_in, 48)
            step(act.activation(SILU_C, sm("c2"), ACT.Tanh, scale=0.5), "tanh c")
            for i in range(8):
                drain(1, MOD[:, 3 * i:3 * i + 3], "have mod" if i == 7 else None, cols=3)
            sums_out("block2")
            scale2 = {"za": 0.5, "zs": 0.25}
            dest2 = {"kcr": 0, "vcr": 1, "u": 2, "za": 6, "zs": 10}
            for n, i in PROJ2:
                drain(1, TL[:, dest2[n] + i, :], "have zs" if (n, i) == ("zs", 3) else None, scale=scale2.get(n, 1.0))
            for a_, c_ in ((0, 384), (384, 384), (768, 280)):
                for n in range(NT):
                    drain(1, R2[:, n, a_:a_ + c_], "have rows2" if (a_, n) == (768, NT - 1) else None, cols=c_)
            for i, kv in enumerate("kv"):
                for g in range(2):
                    k = drained[0]
                    drained[0] += 1
                    act.wait_ge(gemm_full, k + 1)
                    b = G[k % 3]
                    for hid in range(2):
                        step(act.activation(POSB[:, hid:hid + 1], b[:, 32 * hid + 31:32 * hid + 32], ACT.Identity))
                    for hid in range(2):
                        step(act.activation(HID(kv)[:, g, hid, 0:NCMP], b[:, 32 * hid:32 * hid + NCMP], ACT.Gelu_apprx_tanh,
                                            bias=POSB[:, hid:hid + 1]), None, gemm_done if hid else act_step)
                step(act.activation(POSB[:, 0:1], POSB[:, 0:1], ACT.Identity), f"hidden {kv}")
            drain(1, KCRAW[0:NCMP, :], "have kc", cols=P, rows_=NCMP)
            drain(1, VCMP[0:NCMP, :], "have vcmp", cols=P, rows_=NCMP)
            act.wait_ge(dve_step, at("branch logits"))
            for z in range(3):
                step(act.activation(GB[z], GB[z], ACT.Tanh, scale=0.5), "branch gates" if z == 2 else None)
            for i in range(8):
                n, e = divmod(i, 2)
                act.wait_ge(score_full, at(f"full cmp {i}"))
                if i >= 1:
                    act.wait_ge(turn_done, at(f"cmp probsT {i - 1}"))
                step(act.activation(CMP_P, S[(at(f"full cmp {i}") - 1) % 2][:, 0:4 * NCMP], ACT.Identity),
                     f"cmp score {i}", score_done)
                act.wait_ge(dve_step, at(f"cmp less max {i}"))
                step(act.activation(CMP_P, CMP_P, ACT.Exp), f"cmp exp {i}")
            attention_exp("slc", 8)
            attention_exp("win", 8)
            act.wait_ge(dve_step, at("gates free"))
            w2t = part(wide, 6 * T, 4 * T)
            step(act.activation(w2t, tiles[:, 6 * T:10 * T], ACT.Tanh), "tanh za")

            act.wait_ge(small_in, 48)
            step(act.activation(SC["dt"], sm("log_dt"), ACT.Exp), "dt")
            act.wait_ge(dve_step, at("ssm turn"))
            step(act.activation(SC["rho"], SC["rho"], ACT.Exp), "rho")
            step(act.activation(SC["s"], SC["turn"], ACT.Sin, scale=TWO_PI_IN))
            step(act.activation(SC["h"], SC["turn"], ACT.Sin, scale=TWO_PI_IN / 2))
            step(act.activation(SC["c"], SC["turn"], ACT.Abs))
            step(act.activation(SC["c"], SC["c"], ACT.Sin, scale=-TWO_PI_IN, bias=con("misc")[:, 2:3]), "ssm trig")
            for j in range(16):
                act.wait_ge(dve_step, at(f"phases {j}"))
                if j >= 2:
                    act.wait_ge(dve_step, at(f"states {j - 2}"))
                step(act.activation(SIN[j % 2], TURNS[j % 2], ACT.Sin, scale=TWO_PI_IN))
                step(act.activation(TURNS[j % 2], TURNS[j % 2], ACT.Abs))
                step(act.activation(COS[j % 2], TURNS[j % 2], ACT.Sin, scale=-TWO_PI_IN, bias=con("misc")[:, 2:3]), f"waves {j}")
            act.wait_ge(sum_done, at("y 3"))
            step(act.activation(tiles[:, 2 * T:6 * T], tiles[:, 2 * T:6 * T], ACT.Gelu_apprx_tanh), "y gelu")
            step(act.activation(part(wide, 0, 4 * T), tiles[:, 10 * T:14 * T], ACT.Tanh, scale=2.0), "tanh zs")
            for j in range(4):
                drain(1, part(wide, (4 + j) * T, T), f"glu {j}", func=ACT.Tanh, scale=0.5, bias=GLUB[:, j:j + 1])

        @block.vector
        def _(dve):
            def step(ins, name=None, sem_=dve_step):
                n = up(sem_, name)
                ins.then_inc(sem_, 1)
                dve.wait_ge(sem_, n)

            turned = [0]

            def rms_scale(name, gain, out, source=X, shift=None):
                a, y, z = work[:, 0:T], work[:, T:2 * T], work[:, 2 * T:3 * T]
                dve.wait_ge(gemm_done, at(f"mean {name}"))
                dve.wait_ge(act_step, at(f"root {name}"))
                step(dve.reciprocal(y, y))
                step(dve.tensor_tensor(z, y, y, ALU.mult))
                step(dve.tensor_tensor(z, z, a, ALU.mult))
                step(dve.tensor_scalar(z, z, -0.5, 1.5, ALU.mult, ALU.add))
                step(dve.tensor_tensor(y, y, z, ALU.mult), f"rstd {name}")
                for k in range(KD):
                    step(dve.scalar_tensor_tensor(out=out[:, k, :], in0=source[:, k, :], scalar=gain(k), in1=y,
                                                  op0=ALU.mult, op1=ALU.mult),
                         f"normed {name}" if k == KD - 1 and shift is None else None)
                if shift is not None:
                    for k in range(KD):
                        step(dve.tensor_scalar(out[:, k, :], out[:, k, :], shift(k), None, ALU.add),
                             f"normed {name}" if k == KD - 1 else None)

            def squares(name, source=X, out=H):
                for k in range(KD):
                    step(dve.tensor_tensor(out[:, k, :], source[:, k, :], source[:, k, :], ALU.mult),
                         f"squares {name}" if k == KD - 1 else None)

            def take_turn(name, dst, scalar=None, cols=T, rows_=P, view=None, eng=None):
                n = turned[0]
                turned[0] += 1
                dve.wait_ge(turn_full, n + 1)
                src = U[n % 2][0:rows_, 0:cols]
                if view is not None:
                    src = view(src)
                if scalar is None:
                    ins = dve.tensor_copy(dst, src)
                else:
                    ins = dve.tensor_scalar(dst, src, scalar, None, ALU.mult)
                step(ins, name, turn_done)

            def attention_max(name, heads, finish, take_o=None, logits=None):
                items = [(n, h) for n in range(NT) for h in range(heads)]
                last = len(items)
                for i in range(last + 3):
                    if i < last:
                        n, h = items[i]
                        cols = (n + 1) * P
                        dve.wait_ge(score_full, at(f"full {name} score {i}"))
                        src = S[(at(f"full {name} score {i}") - 1) % 2][:, 0:cols]
                        if i >= 2:
                            dve.wait_ge(score_done, at(f"{name} probs {i - 2}"))
                        if logits is not None:
                            src = logits(i, n, h, src)
                        step(dve.tensor_reduce(stat[:, 8 + i % 2:9 + i % 2], src, AX.X, ALU.max, negate=True),
                             f"{name} max {i}")
                    if 1 <= i <= last:
                        n, h = items[i - 1]
                        if i - 1 >= 2:
                            dve.wait_ge(sum_full, at(f"{name} summed {i - 3}"))
                        take_turn(f"{name} probsT {i - 1}", probsT[:, (i - 1) % 2 * T:(i - 1) % 2 * T + (n + 1) * P],
                                  cols=(n + 1) * P)
                    if 2 <= i <= last + 1 and items[i - 2][1] == heads - 1:
                        finish(items[i - 2][0])
                    if take_o is not None and i >= 3 and items[i - 3][1] == heads - 1:
                        take_o(items[i - 3][0])


            def small_rstd(name, mean, n):
                step(dve.tensor_scalar(mean, mean, 1.0 / n, EPS, ALU.mult, ALU.add), f"mean {name}")
                dve.wait_ge(pool_step, at(f"rstd {name}"))

            def tt(out, a, b, op, name=None):
                step(dve.tensor_tensor(out, a, b, op), name)

            def ts(out, a, s1, s2, o1, o2=None, name=None):
                step(dve.tensor_scalar(out, a, s1, s2, o1, *([o2] if o2 is not None else [])), name)

            def stt(out, a, s_, b, o1, o2, name=None, sem_=dve_step):
                step(dve.scalar_tensor_tensor(out=out, in0=a, scalar=s_, in1=b, op0=o1, op1=o2), name, sem_)

            def sum_out(fill, write):
                dve.wait_ge(sum_full, at(fill))
                write(O[0])

            def probs_over_sums(name, dst, heads, gate=None):
                def finish(n):
                    last = (n + 1) * heads - 1
                    dve.wait_ge(score_done, at(f"{name} probs {last}"))
                    r = stat[:, 16 + (n % 2) * 8:16 + (n % 2) * 8 + heads]
                    step(dve.reciprocal(r, r))
                    if gate is not None:
                        tt(r, r, gate(n), ALU.mult)
                    dve.wait_ge(sum_full, at(f"{name} summed {last}"))
                    w = T // heads
                    o3 = O[0][:, :].rearrange("p (h d) -> p h d", h=heads)
                    rb = r.unsqueeze(2).broadcast_to([P, heads, w])
                    if gate is None:
                        if n:
                            dve.wait_ge(turn_full, at(f"full turn {name} o {n - 1}"))
                        step(dve.tensor_tensor(dst(n).rearrange("p (h d) -> p h d", h=heads), o3, rb, ALU.mult),
                             f"{name} o {n}", sum_done)
                    else:
                        t_ = part(wide, 4200, T)
                        step(dve.tensor_tensor(t_.rearrange("p (h d) -> p h d", h=heads), o3, rb, ALU.mult))
                        step(dve.tensor_tensor(dst(n), dst(n), t_, ALU.add), f"{name} o {n}", sum_done)
                return finish

            def o_to_tiles(name, first):
                def take(n):
                    take_turn(f"{name} oT {n}", TL[:, first:first + 4, n * P:(n + 1) * P],
                              view=lambda v: v.rearrange("p (j t) -> p j t", j=4))
                return take

            dve.wait_ge(const_in, 16)
            dve.wait_ge(x_in, 16)
            squares("attn")
            dve.wait_ge(small_in, 48)
            rms_scale("attn", lambda k: sm("g_attn")[:, k:k + 1], H)
            for i in range(24):
                n, h = 1 + i // 8, i % 8
                r, iw = probs[:, i % 2 * T:i % 2 * T + (n + 1) * P], ROW[:, n, 128 + h:129 + h]
                dve.wait_ge(score_done, at(f"index relu {i}"))
                if h == 0:
                    ts(INDEX[n], r, iw, None, ALU.mult, name=f"index added {i}")
                else:
                    stt(INDEX[n], r, iw, INDEX[n], ALU.mult, ALU.add, name=f"index added {i}")
            step(dve.tensor_copy(chosen[:, 0:P], causal))
            for n in range(1, NT):
                a = INDEX[n]
                ts(a, a, (64 ** -0.5) * (8 ** -0.5), None, ALU.mult)
                tt(a[:, n * P:(n + 1) * P], a[:, n * P:(n + 1) * P], causal, ALU.add)
                for _i in range(TOPK // 8):
                    step(dve.max(stat[:, 0:8], a))
                    step(dve.match_replace(out=a, in_to_replace=stat[:, 0:8], in_values=a, imm_value=TAKEN))
                ts(chosen[:, upto(n):upto(n + 1)], a, TAKEN, NEG, ALU.not_equal, ALU.mult, name="chosen" if n == 3 else None)

            f4, k4, w0, w1 = tiles[:, 5 * T:9 * T], tiles[:, 0:4 * T], work[:, 0:4 * T], work[:, 4 * T:8 * T]
            dve.wait_ge(gemm_done, at("have bg"))
            dve.wait_ge(act_step, at("rec u"))
            ts(w1, w0, 1.0, None, ALU.add, name="rec one plus u")
            step(dve.reciprocal(w1, w1))
            dve.wait_ge(act_step, at("rec num"))
            tt(k4, k4, w1, ALU.mult, "keys rec")
            dve.wait_ge(act_step, at("rec ln"))
            stt(f4, f4, 0.0, w0, ALU.min, ALU.subtract, name="rec log sigmoid")
            dve.wait_ge(act_step, at("rec floor"))
            stt(f4, f4, LOG_FLOOR, w0, ALU.max, ALU.add, name="rec log f")
            for h in range(4):
                bt = TL[:, 5 + h, :]
                step(dve.tensor_tensor_scan(bt, con("reset"), bt, 0.0, ALU.mult, ALU.add))
            dve.wait_ge(act_step, at("rec gate"))
            g4 = tiles[:, 18 * T:22 * T]
            stt(g4, w0, 1.0, g4, ALU.add, ALU.mult)
            for h in range(4):
                bt, q, k = TL[:, 5 + h, :], TL[:, 9 + h, :], TL[:, h, :]
                b4 = bt.rearrange("p (c t) -> p c t", c=4)
                e4 = REC_E[1].rearrange("p (c t) -> p c t", c=4)
                tt(e4, b4[:, :, P - 1:P].broadcast_to([P, 4, P]), b4, ALU.subtract, f"rec args {h}")
                dve.wait_ge(act_step, at(f"rec el {h}"))
                tt(REC_QX, q, REC_E[0], ALU.mult)
                tt(REC_KX, k, REC_E[1], ALU.mult)
                end = [REC_E[0][:, (c + 1) * P - 1:(c + 1) * P] for c in range(4)]
                ts(REC_QS[:, 0:P], REC_QX[:, 2 * P:3 * P], end[1], None, ALU.mult)
                ts(REC_QS[:, P:2 * P], REC_QX[:, 3 * P:4 * P], end[2], None, ALU.mult)
                ts(REC_QS[:, 2 * P:3 * P], REC_QS[:, P:2 * P], end[1], None, ALU.mult, name=f"rec cross {h}")
                step(dve.memset(REC_AT, 0.0))
                lev = con("level").rearrange("p (l t) -> p l t", l=LEVELS + 1)

                def take_level(l):
                    m = turned[0]
                    turned[0] += 1
                    dve.wait_ge(turn_full, m + 1)
                    mask = lev[:, l:l + 1, :].bitcast(I32).broadcast_to([P, 4, P])
                    step(dve.copy_predicated(REC_AT.rearrange("p (c t) -> p c t", c=4), mask,
                                             U[m % 2][:, :].rearrange("p (c t) -> p c t", c=4)),
                         f"rec weights {h}" if l == LEVELS else None, turn_done)

                def args(l):
                    m = 1 << l
                    bv = bt.rearrange("p (n t) -> p n t", t=2 * m)
                    ev = REC_E[l % 2].rearrange("p (n t) -> p n t", t=2 * m)
                    ref = bv[:, :, m - 1:m].broadcast_to([P, T // (2 * m), m])
                    tt(ev[:, :, 0:m], ref, bv[:, :, 0:m], ALU.subtract)
                    tt(ev[:, :, m:], bv[:, :, m:], ref, ALU.subtract, f"rec args {h} {l}")

                args(0)
                take_level(0)
                take_turn(None, REC_X[:, 0:4 * P])
                take_turn(None, REC_X[:, 4 * P:6 * P], cols=2 * P)
                for l in range(LEVELS):
                    m = 1 << l
                    if l + 1 < LEVELS:
                        args(l + 1)
                    dve.wait_ge(act_step, at(f"rec e {h} {l}"))
                    ev = REC_E[l % 2].rearrange("p (n t) -> p n t", t=2 * m)
                    ov = REC_QK[l % 2].rearrange("p (n t) -> p n t", t=2 * m)
                    kv_, qv = k.rearrange("p (n t) -> p n t", t=2 * m), q.rearrange("p (n t) -> p n t", t=2 * m)
                    tt(ov[:, :, 0:m], kv_[:, :, 0:m], ev[:, :, 0:m], ALU.mult)
                    tt(ov[:, :, m:], qv[:, :, m:], ev[:, :, m:], ALU.mult, f"rec scaled {h} {l}")
                    if l >= 1:
                        take_level(l)
                take_level(LEVELS)
                dve.wait_ge(sum_full, at(f"full rec o {h}"))
                step(dve.tensor_copy(REC_O[:, :, h * P:(h + 1) * P], O[0][:, :].rearrange("p (c t) -> p c t", c=4)),
                     None, sum_done)
            o16 = part(wide, 2560, 2048, k=16)
            tt(w0, part(wide, 2560, 2048), part(wide, 2560, 2048), ALU.mult)
            r16 = stat[:, 32:48]
            step(dve.tensor_reduce(r16, w0.rearrange("p (k t) -> p k t", k=16), AX.X, ALU.add))
            small_rstd("rec", r16, 128)
            tt(o16, o16, r16.unsqueeze(2).broadcast_to([P, 16, P]), ALU.mult, "rec normed")
            for n in range(NT):
                m = turned[0]
                turned[0] += 1
                dve.wait_ge(turn_full, m + 1)
                stt(TL[:, 9:13, n * P:(n + 1) * P], U[m % 2][:, :].rearrange("p (j t) -> p j t", j=4), sm("g_ob")[:, 0:1],
                    TL[:, 18:22, n * P:(n + 1) * P], ALU.mult, ALU.mult, f"rec oT {n}", turn_done)

            for name, v, wd, c0 in (("cq", CQ, 384, 48), ("ckv", CKV, 256, 52)):
                sq = part(work, 2560, 4 * wd, k=NT)
                tt(sq, v, v, ALU.mult)
                step(dve.tensor_reduce(stat[:, c0:c0 + 4], sq, AX.X, ALU.add))
                small_rstd(name, stat[:, c0:c0 + 4], wd)
                for n in range(NT):
                    ts(v[:, n, :], v[:, n, :], stat[:, c0 + n:c0 + n + 1], None, ALU.mult,
                       name="latents normed" if (name, n) == ("ckv", NT - 1) else None)
            for j in range(3):
                take_turn(None, CQT[:, j, :], scalar=sm("g_cq")[:, j:j + 1])
            for j in range(2):
                take_turn("ckvT" if j else None, CKVT[:, j, :], scalar=sm("g_ckv")[:, j:j + 1])
            pf, ang, kk = stat[:, 56:60], trig[:, 0:P], trig[:, P:2 * P]
            step(dve.tensor_copy(pf, pcol[:, :]))
            for n in range(NT):
                ts(ang[:, n * 32:(n + 1) * 32], con("invf"), pf[:, n:n + 1], None, ALU.mult)
            ts(kk, ang, 1.0 / TWO_PI, ROUND, ALU.mult, ALU.add)
            ts(kk, kk, ROUND, None, ALU.subtract)
            for c_ in PI_PARTS:
                stt(ang, kk, -c_, ang, ALU.mult, ALU.add)
            ts(ang, ang, PI_IN, -PI_IN, ALU.min, ALU.max, name="angles")
            dve.wait_ge(act_step, at("trig"))
            cos1, sin1 = part(trig, 0, P, k=NT), part(trig, P, P, k=NT)

            def rope(x1, x2, c_, s_, a, b, o1=None, o2=None, name=None):
                o1, o2 = x1 if o1 is None else o1, x2 if o2 is None else o2
                tt(a, x1, s_, ALU.mult)
                tt(b, x2, s_, ALU.mult)
                tt(o1, x1, c_, ALU.mult)
                tt(o1, o1, b, ALU.subtract)
                tt(o2, x2, c_, ALU.mult)
                tt(o2, o2, a, ALU.add, name)

            dve.wait_ge(gemm_done, at("have qpe"))
            ta, tb = part(wide, 512, 128), part(wide, 640, 128)
            a3, b3 = ta.rearrange("p (n t) -> p n t", n=4), tb.rearrange("p (n t) -> p n t", n=4)
            rope(ROW[:, :, 136:168], ROW[:, :, 168:200], cos1, sin1, a3, b3, KPE2[:, :, 0:32], KPE2[:, :, 32:64])
            step(dve.tensor_copy(KPE2[:, :, 64:128], KPE2[:, :, 0:64]))
            for n in range(NT):
                qv = QPE[:, n, :].rearrange("p (h t) -> p h t", h=4)
                cb, sb_ = [v[:, n:n + 1, :].broadcast_to([P, 4, 32]) for v in (cos1, sin1)]
                rope(qv[:, :, 0:32], qv[:, :, 32:64], cb, sb_, a3, b3, name="roped" if n == NT - 1 else None)
            take_turn(None, KPET)
            for j in range(2):
                take_turn("qpeT" if j else None, QPET[:, j, :])
            attention_max("mla", 4, probs_over_sums("mla", lambda n: work[:, 0:T], 4), o_to_tiles("mla", 5))

            dl = stat[:, 64:188]
            rel = sm("rel")
            tt(dl, rel[:, 4:128], rel[:, 0:124], ALU.subtract)
            steps = bucket_steps()
            for n in range(NT):
                cols = (n + 1) * P
                dist, ind = part(work, 2 * T, cols), part(work, 3 * T, cols)
                ts(dist, prow[:, 0:cols], -1.0, pf[:, n:n + 1], ALU.mult, ALU.add)
                acc = [BIAS[:, h, upto(n):upto(n + 1)] for h in range(4)]
                for h in range(4):
                    ts(acc[h], dist, 0.0, rel[:, h:h + 1], ALU.mult, ALU.add)
                for i, least in enumerate(steps):
                    ts(ind, dist, float(least), None, ALU.is_ge)
                    for h in range(4):
                        stt(acc[h], ind, dl[:, 4 * i + h:4 * i + h + 1], acc[h], ALU.mult, ALU.add)
                for h in range(4):
                    tt(acc[h], acc[h], chosen[:, upto(n):upto(n + 1)], ALU.add)

            def biased(i, n, h, src):
                out = LOGITS[i % 2][:, 0:(n + 1) * P]
                tt(out, src, BIAS[:, h, upto(n):upto(n + 1)], ALU.add)
                return out

            attention_max("dsa", 4, probs_over_sums("dsa", lambda n: work[:, 0:T], 4), o_to_tiles("dsa", 13), biased)
            step(dve.memset(stat[:, 60:61], 0.0), "dsa done")

            for j in range(8):
                m0, m1 = part(work, 0, T), part(work, T, T)
                for b_ in range(3):
                    dve.wait_ge(gemm_done, at(f"gate {j} {b_}"))
                    m = turned[0]
                    turned[0] += 1
                    dve.wait_ge(turn_full, m + 1)
                    stt(m1 if b_ else m0, GATE[b_], 1.0, U[m % 2][:, :], ALU.add, ALU.mult, None, turn_done)
                    if b_ == 1:
                        tt(m0, m0, m1, ALU.add)
                    if b_ == 2:
                        tt(TL[:, MIX[j], :], m0, m1, ALU.add, f"mixed {j}")
            step(dve.memset(stat[:, 60:61], 0.0), "mixed")

            def add_to_x(scalar):
                for j in range(8):
                    m = turned[0]
                    turned[0] += 1
                    dve.wait_ge(turn_full, m + 1)
                    stt(X[:, j, :], U[m % 2][:, :], scalar(j), X[:, j, :], ALU.mult, ALU.add, None, turn_done)

            add_to_x(lambda j: 0.5)
            squares("ffn")
            rms_scale("ffn", lambda k: sm("g_ffn")[:, k:k + 1], H)
            for j in range(NFF):
                a, hb = part(work, j % 2 * T, T), part(work, (2 + j % 2) * T, T)
                dve.wait_ge(gemm_done, at(f"ff gate {j}"))
                stt(a, a, 1.0, hb, ALU.add, ALU.mult)
                m = turned[0]
                turned[0] += 1
                dve.wait_ge(turn_full, m + 1)
                step(dve.tensor_tensor(TL[:, j, :], a, U[m % 2][:, :], ALU.mult), f"ff {j}", turn_done)
                if j == NFF - 1:
                    tally.named["ff hidden"] = tally.named[f"ff {j}"]
            add_to_x(lambda j: 1.0)
            squares("final")
            rms_scale("final", lambda k: sm("g_final")[:, k:k + 1], X)
            dve.wait_ge(act_step, at("tanh c"))
            stt(SILU_C, SILU_C, 1.0, sm("c2"), ALU.add, ALU.mult)
            ts(GLUB, sm("glu_b"), 0.5, None, ALU.mult)
            ts(SILU_C, SILU_C, 0.5, None, ALU.mult, name="silu c")
            squares("block2")
            dve.wait_ge(gemm_done, at("have mod"))
            tt(MOD, MOD, sm("b_ada"), ALU.add)
            stt(GAIN2, MOD[:, 8:16], 1.0, sm("g_2"), ALU.add, ALU.mult)
            rms_scale("block2", lambda k: GAIN2[:, k:k + 1], H, shift=lambda k: MOD[:, k:k + 1])
            dve.wait_ge(gemm_done, at("have vcmp"))
            kr = KCRAW[0:NCMP, :].rearrange("p (g t) -> p g t", g=2)
            kq = part(work, T, P)[0:NCMP].rearrange("p (g t) -> p g t", g=2)
            tt(kq, kr, kr, ALU.mult)
            step(dve.memset(stat[:, 32:34], 1.0))
            step(dve.tensor_reduce(stat[0:NCMP, 32:34], kq, AX.X, ALU.add))
            small_rstd("kc", stat[:, 32:34], 64)
            tt(kr, kr, stat[0:NCMP, 32:34].unsqueeze(2).broadcast_to([NCMP, 2, 64]), ALU.mult)
            for d in range(2):
                tt(KC2[0:NCMP, :, 64 * d:64 * d + 64], kr,
                   sm("g_kc")[0:NCMP, :].unsqueeze(1).broadcast_to([NCMP, 2, 64]), ALU.mult, "kc normed" if d else None)
            take_turn("kcT", KCT.rearrange("p (g t) -> p g t", g=2)[:, :, 0:NCMP], cols=64,
                      view=lambda v: v.rearrange("p (g t) -> p g t", g=2)[:, :, 0:NCMP])
            dve.wait_ge(gemm_done, at("have rows2"))
            ts(stat[:, 64:128], sm("g_q"), 0.125, None, ALU.mult)
            for name, c0, heads, gain, c1 in (("q", 0, 8, stat[:, 64:128], 128), ("ksl", 512, 2, sm("g_ks"), 160), ("kwn", 768, 2, sm("g_kw"), 168)):
                sq = part(work, 0, NT * heads * 64, k=NT)
                v = R2[:, :, c0:c0 + heads * 64]
                tt(sq, v, v, ALU.mult)
                r = stat[:, c1:c1 + NT * heads]
                step(dve.tensor_reduce(r, sq.rearrange("p n (h d) -> p n h d", h=heads), AX.X, ALU.add))
                small_rstd(name, r, 64)
                for n in range(NT):
                    vn = v[:, n, :].rearrange("p (h d) -> p h d", h=heads)
                    tt(vn, vn, r[:, n * heads:(n + 1) * heads].unsqueeze(2).broadcast_to([P, heads, 64]), ALU.mult)
                    tt(vn, vn, gain.unsqueeze(1).broadcast_to([P, heads, 64]), ALU.mult,
                       "q normed" if (name, n) == ("q", NT - 1) else None)
            for j in range(4):
                take_turn(None, TL[:, 14 + j, :])
            cos2, sin2 = con("cos2").rearrange("p (n t) -> p n t", n=NT), con("sin2").rearrange("p (n t) -> p n t", n=NT)
            ta, tb = [part(wide, 4200 + 256 * z, 256, k=8) for z in range(2)]
            for n in range(NT):
                qv = R2[:, n, 0:512].rearrange("p (h t) -> p h t", h=8)
                cb, sb_ = [v[:, n:n + 1, :].broadcast_to([P, 8, 32]) for v in (cos2, sin2)]
                rope(qv[:, :, 0:32], qv[:, :, 32:64], cb, sb_, ta, tb, name="q roped" if n == NT - 1 else None)
            for j in range(4):
                take_turn(None, TL[:, 18 + j, :])
            for a_, c0 in enumerate((512, 768)):
                for g in range(2):
                    x1, x2 = [R2[:, :, c0 + 64 * g + 32 * z:c0 + 64 * g + 32 * z + 32] for z in range(2)]
                    k2 = K2(2 * a_ + g)
                    aa, bb = [part(wide, 4200 + 256 * z, 128, k=4) for z in range(2)]
                    rope(x1, x2, cos2, sin2, aa, bb, k2[:, :, 0:32], k2[:, :, 32:64])
                    step(dve.tensor_copy(k2[:, :, 64:128], k2[:, :, 0:64]), "k roped" if (a_, g) == (1, 1) else None)
            for i in range(4):
                take_turn("kT 3" if i == 3 else None, KT2[:, i, :])
            for z in range(3):
                step(dve.tensor_copy(GB[z], R2[:, :, 1024 + z:1048:3]), "branch logits" if z == 2 else None)
            dve.wait_ge(act_step, at("branch gates"))
            for z in range(3):
                ts(GB[z], GB[z], 0.5, 0.5, ALU.mult, ALU.add)
            cn = con("cmp_neg").rearrange("p (n t) -> p n t", n=NT)
            ck = con("cmp_ok").rearrange("p (n t) -> p n t", n=NT)
            for i in range(8):
                n, e = divmod(i, 2)
                s3 = CMP_P.rearrange("p (h t) -> p h t", h=4)
                m4 = stat[:, 8:12]
                dve.wait_ge(score_done, at(f"cmp score {i}"))
                tt(s3, s3, cn[:, n:n + 1, :].broadcast_to([P, 4, NCMP]), ALU.add)
                step(dve.tensor_reduce(m4, s3, AX.X, ALU.max))
                tt(s3, s3, m4.unsqueeze(2).broadcast_to([P, 4, NCMP]), ALU.subtract, f"cmp less max {i}")
                dve.wait_ge(act_step, at(f"cmp exp {i}"))
                tt(s3, s3, ck[:, n:n + 1, :].broadcast_to([P, 4, NCMP]), ALU.mult, f"cmp probs {i}")
                rs = stat[:, 16:24].rearrange("p (q e) -> p q e", e=2)[:, :, e:e + 1]
                step(dve.tensor_reduce(rs, s3, AX.X, ALU.add))
                if i:
                    dve.wait_ge(sum_full, at(f"cmp summed {i - 1}"))
                take_turn(f"cmp probsT {i}", probsT[0:NCMP, 0:T], rows_=NCMP)
                if e == 1:
                    r8 = stat[:, 16:24]
                    ts(r8, r8, 1e-30, None, ALU.max)
                    step(dve.reciprocal(r8, r8))
                    tt(r8, r8, GB[0][:, n, :], ALU.mult)
                    dve.wait_ge(sum_full, at(f"cmp summed {i}"))
                    step(dve.tensor_tensor(ATT[:, n, :].rearrange("p (h d) -> p h d", h=8),
                                           O[0][:, :].rearrange("p (h d) -> p h d", h=8),
                                           r8.unsqueeze(2).broadcast_to([P, 8, 64]), ALU.mult), None, sum_done)
            for z, name in ((1, "slc"), (2, "win")):
                attention_max(name, 8, probs_over_sums(name, lambda n: ATT[:, n, :], 8, gate=lambda n: GB[z][:, n, :]))
            step(dve.memset(stat[:, 60:61], 0.0), "gates free")
            dve.wait_ge(act_step, at("tanh za"))
            za4 = tiles[:, 6 * T:10 * T]
            stt(za4, part(wide, 6 * T, 4 * T), 1.0, za4, ALU.add, ALU.mult)
            for n in range(NT):
                m = turned[0]
                turned[0] += 1
                dve.wait_ge(turn_full, m + 1)
                v = TL[:, 6:10, n * P:(n + 1) * P]
                step(dve.tensor_tensor(v, U[m % 2][:, :].rearrange("p (j t) -> p j t", j=4), v, ALU.mult),
                     f"attn T {n}", turn_done)

            c = SC
            dve.wait_ge(act_step, at("dt"))
            tt(c["t"], sm("a_im"), c["dt"], ALU.mult)
            ts(c["t"], c["t"], 1.0 / TWO_PI, None, ALU.mult)
            ts(c["u"], c["t"], ROUND, None, ALU.add)
            ts(c["u"], c["u"], ROUND, None, ALU.subtract)
            tt(c["turn"], c["t"], c["u"], ALU.subtract)
            ts(c["u"], c["turn"], 384.0, None, ALU.add)
            ts(c["hi"], c["u"], 384.0, None, ALU.subtract)
            tt(c["lo"], c["turn"], c["hi"], ALU.subtract)
            tt(c["rho"], sm("a_re"), c["dt"], ALU.mult, "ssm turn")
            dve.wait_ge(act_step, at("ssm trig"))
            ts(c["t"], c["rho"], 1.0, None, ALU.subtract)
            tt(c["x"], c["t"], c["c"], ALU.mult)
            tt(c["u"], c["h"], c["h"], ALU.mult)
            stt(c["x"], c["u"], -2.0, c["x"], ALU.mult, ALU.add)
            tt(c["y"], c["rho"], c["s"], ALU.mult)
            tt(c["t"], sm("a_re"), sm("a_re"), ALU.mult)
            tt(c["u"], sm("a_im"), sm("a_im"), ALU.mult)
            tt(c["den"], c["t"], c["u"], ALU.add)
            step(dve.reciprocal(c["den"], c["den"]))
            tt(c["t"], c["x"], sm("a_re"), ALU.mult)
            tt(c["u"], c["y"], sm("a_im"), ALU.mult)
            tt(c["t"], c["t"], c["u"], ALU.add)
            tt(c["kr"], c["t"], c["den"], ALU.mult)
            tt(c["t"], c["y"], sm("a_re"), ALU.mult)
            tt(c["u"], c["x"], sm("a_im"), ALU.mult)
            tt(c["t"], c["t"], c["u"], ALU.subtract)
            tt(c["ki"], c["t"], c["den"], ALU.mult)
            i_ = chunk_at["ssm"]
            dve.wait_ge(slot_in[i_ % SLOTS], 16 * (i_ // SLOTS + 1))
            wssm = chunk("ssm")
            cr, ci = [wssm[:, 512 + 1024 * z:1024 + 1024 * z].rearrange("p (k t) -> p k t", k=16) for z in range(2)]
            kr_, ki_ = [c[n].unsqueeze(2).broadcast_to([P, 16, 32]) for n in ("kr", "ki")]
            tmp = part(work, 4 * T, T, k=16)
            tt(CC[0], cr, kr_, ALU.mult)
            tt(tmp, ci, ki_, ALU.mult)
            tt(CC[0], CC[0], tmp, ALU.subtract)
            tt(CC[1], cr, ki_, ALU.mult)
            tt(tmp, ci, kr_, ALU.mult)
            tt(CC[1], CC[1], tmp, ALU.add)
            ts(CC[1], CC[1], -1.0, None, ALU.mult)

            def phases(j):
                hi, lo = c["hi"][:, j:j + 1], c["lo"][:, j:j + 1]
                r, t1, t2 = TURNS[j % 2], SSM("t1"), SSM("t2")
                ts(t1, con("time"), hi, None, ALU.mult)
                ts(t2, t1, ROUND, None, ALU.add)
                ts(t2, t2, ROUND, None, ALU.subtract)
                tt(t1, t1, t2, ALU.subtract)
                stt(t1, con("time"), lo, t1, ALU.mult, ALU.add)
                ts(r, t1, 0.5, -0.5, ALU.min, ALU.max, name=f"phases {j}")

            phases(0)
            for j in range(16):
                if j + 1 < 16:
                    phases(j + 1)
                s_, c_ = SIN[j % 2], COS[j % 2]
                dve.wait_ge(act_step, at(f"waves {j}"))
                m = turned[0]
                turned[0] += 2
                dve.wait_ge(turn_full, m + 2)
                br, bi_ = U[m % 2][:, :], U[(m + 1) % 2][:, :]
                t1, t2, zr, zi, sr, si = [SSM(n) for n in ("t1", "t2", "zr", "zi", "sr", "si")]
                if j:
                    dve.wait_ge(sum_full, at(f"full y {j - 1}"))
                tt(sr, br, c_, ALU.mult)
                tt(t1, bi_, s_, ALU.mult)
                tt(sr, sr, t1, ALU.add)
                step(dve.tensor_tensor(t2, br, s_, ALU.mult), None, turn_done)
                step(dve.tensor_tensor(si, bi_, c_, ALU.mult), None, turn_done)
                tt(si, si, t2, ALU.subtract)
                rho = c["rho"][:, j:j + 1].broadcast_to([P, T])
                step(dve.tensor_tensor_scan(zr, rho, sr, 0.0, ALU.mult, ALU.add))
                step(dve.tensor_tensor_scan(zi, rho, si, 0.0, ALU.mult, ALU.add))
                tt(sr, zr, c_, ALU.mult)
                tt(t1, zi, s_, ALU.mult)
                tt(sr, sr, t1, ALU.subtract)
                tt(si, zr, s_, ALU.mult)
                tt(t2, zi, c_, ALU.mult)
                tt(si, si, t2, ALU.add, f"states {j}")
                if j % 4 == 3:
                    ct = j // 4
                    dve.wait_ge(sum_full, at(f"full y {j}"))
                    stt(TL[:, 2 + ct, :], TL[:, 2 + ct, :], sm("ssm_d")[:, ct:ct + 1], O[0][:, :], ALU.mult, ALU.add,
                        f"y {ct}", sum_done)
            dve.wait_ge(act_step, at("tanh zs"))
            zs4 = tiles[:, 10 * T:14 * T]
            stt(zs4, part(wide, 0, 4 * T), 1.0, zs4, ALU.add, ALU.mult)
            tt(zs4, zs4, tiles[:, 2 * T:6 * T], ALU.mult)
            for j in range(4):
                dve.wait_ge(gemm_done, at(f"glu {j}"))
                stt(TL[:, 10 + j, :], part(wide, (4 + j) * T, T), 1.0, TL[:, 10 + j, :], ALU.add, ALU.mult,
                    "ssm out" if j == 3 else None)
            add_to_x(lambda j: MOD[:, 16 + j:17 + j])
            step(dve.memset(stat[:, 60:61], 0.0), "out ready")

        @block.gpsimd
        def _(pool):

            def step(ins, name=None):
                n = up(pool_step, name)
                ins.then_inc(pool_step, 1)
                pool.wait_ge(pool_step, n)

            pool.wait_ge(const_in, 16)
            half = con("misc")[:, 0:1]
            for name, c0, n in (("rec", 32, 16), ("cq", 48, 4), ("ckv", 52, 4), ("kc", 32, 2), ("q", 128, 32),
                                ("ksl", 160, 8), ("kwn", 168, 8)):
                v = stat[:, c0:c0 + n]
                pool.wait_ge(dve_step, at(f"mean {name}"))
                step(pool.tensor_tensor(v, v, half.broadcast_to([P, n]), ALU.pow), f"rstd {name}")
    return tally.named


def declare(nc):
    def din(name, shape, dt=F32):
        return nc.dram_tensor(name, shape, dt, kind="ExternalInput").ap()

    return [din("wstream", (len(plan()), P, CHUNK)), din("xT", (P, KD * T)), din("consts", (P, sum(CONST.values()))),
            din("small", (P, sum(SMALL.values()))), din("pos_row", (P, T), I32), din("pos_col", (P, NT), I32),
            nc.dram_tensor("outT", (P, KD * T), F32, kind="ExternalOutput").ap()]


def kernel(**inputs):
    import concourse.bacc as _bacc
    from concourse.bass_utils import run_bass_kernel_spmd as _run

    a = {n: np.asarray(v) for n, v in inputs.items()}
    xT = a["x"][0].T.reshape(KD, P, T).transpose(1, 0, 2).reshape(P, -1)
    pos = a["positions"][0].astype(np.int32)
    c, s = constants(), small_inputs(a)
    arrays = {
        "wstream": weight_stream(a), "xT": np.ascontiguousarray(xT),
        "consts": np.ascontiguousarray(np.concatenate([c[n] for n in CONST], 1)),
        "small": np.ascontiguousarray(np.concatenate([s[n] for n in SMALL], 1)),
        "pos_row": np.ascontiguousarray(np.broadcast_to(pos, (P, T))),
        "pos_col": np.ascontiguousarray(pos.reshape(NT, P).T),
    }
    trial = _bacc.Bacc("TRN2", target_bir_lowering=False, num_devices=1)
    known = two_blocks_kernel(trial, *declare(trial), None)
    nc = _bacc.Bacc("TRN2", target_bir_lowering=False, num_devices=1)
    two_blocks_kernel(nc, *declare(nc), known)
    r = _run(nc, [arrays], core_ids=[0])
    out = r.results[0]["outT"]
    return np.ascontiguousarray(out.reshape(P, KD, T).transpose(2, 1, 0).reshape(1, T, D))
```

```python
import itertools
import math

import numpy as np

import concourse.bass as bass
from concourse import mybir

F32 = mybir.dt.float32
I32 = mybir.dt.int32
BF16 = mybir.dt.bfloat16
F32R = mybir.dt.float32r
ALU = mybir.AluOpType
ACT = mybir.ActivationFunctionType
AX = mybir.AxisListType

P = 128
T = 512
NT = T // P
D = 1024
KD = D // P
NEG = -1e30
TAKEN = -3e38
EPS = 1e-6
CHUNK = 3072
SLOTS = 4
FF = 2816
NFF = FF // P
TOPK = min(256, T // 4)
NCMP = (T - 32) // 16 + 1
LEVELS = 7
TWO_PI = 2.0 * math.pi
ROUND = 1.5 * 2.0 ** 23
TWO_PI_IN = 6.283184
PI_IN = 3.141592
PI_PARTS = (6.28125, 0.00193500518798828125, 3.019915981956753e-07)
LOG_FLOOR = math.log(1e-30)
MLA_SCALE = 192 ** -0.5
TURN_CHUNKS = ("up_", "ff_", "dow", "wou")


def bucket_steps():
    d = np.arange(0, 2048)
    dl = np.maximum(d, 16).astype(np.float32)
    large = 16 + (np.log(dl / np.float32(16)) / np.float32(math.log(8)) * np.float32(16)).astype(np.int32)
    b = np.where(d < 16, d, np.minimum(large, 31))
    return [int(np.argmax(b >= n)) for n in range(1, 32)]


def constants():
    p = np.arange(P)[:, None]
    c = {}
    c["ident"] = (p == np.arange(P)).astype(np.float32)
    c["ones"] = np.ones((P, P), np.float32)
    c["causal"] = np.where(np.arange(P) <= p, 0.0, NEG).astype(np.float32)
    s, t = p, np.arange(P)[None]
    lev = [(s == t)]
    for l in range(LEVELS):
        m = 1 << l
        lev.append((s // (2 * m) == t // (2 * m)) & (s % (2 * m) < m) & (t % (2 * m) >= m))
    c["level"] = np.stack(lev, 1).astype(np.float32).reshape(P, -1)
    c["reset"] = np.broadcast_to((np.arange(T) % P != 0).astype(np.float32), (P, T))
    c["time"] = np.broadcast_to(np.arange(T, dtype=np.float32), (P, T))
    c["invf"] = np.broadcast_to((np.float32(10000.0) ** (-np.arange(0, 64, 2, dtype=np.float32) / np.float32(64))).astype(np.float32), (P, 32))
    inv = (1.0 / (np.float32(10000.0) ** (np.arange(0, 64, 2, dtype=np.float32) / np.float32(64)))).astype(np.float32)
    ang = np.arange(T, dtype=np.float32)[:, None] * inv[None]
    c["cos2"] = np.cos(ang).astype(np.float32).reshape(NT, P, 32).transpose(1, 0, 2).reshape(P, -1)
    c["sin2"] = np.sin(ang).astype(np.float32).reshape(NT, P, 32).transpose(1, 0, 2).reshape(P, -1)
    tt = np.arange(T).reshape(NT, P).T[:, :, None]
    ok = (np.arange(NCMP) * 16 + 31)[None, None] <= tt
    c["cmp_neg"] = np.where(ok, 0.0, NEG).astype(np.float32).reshape(P, -1)
    c["cmp_ok"] = ok.astype(np.float32).reshape(P, -1)
    c["least"] = np.tile(np.array([-2.0 ** 30] + bucket_steps(), np.float32), 4)[:, None]
    c["misc"] = np.tile(np.array([-0.5, EPS, math.pi / 2, -LOG_FLOOR], np.float32), (P, 1))
    return c


def tiles_of(w, cols):
    w = w[:, cols]
    return w.reshape(w.shape[0] // P, P, w.shape[1]).transpose(1, 0, 2).reshape(P, -1)


SPLITS = [512, 128, 128, 512, 64, 8, 512, 512, 512, 512, 384, 256, 64, 3072]
NAMES = ["aq", "ak", "av", "iq", "ik", "iw", "bq", "bf", "bi", "bg", "cq", "ckv", "ckpe", "gate"]
AT1 = dict(zip(NAMES, np.cumsum([0] + SPLITS[:-1]).tolist()))
SPLITS2 = [512] + [128] * 6 + [512, 24, 512, 512]
NAMES2 = ["q", "kcr", "vcr", "ksl", "vsl", "kwn", "vwn", "za", "gbr", "u", "zs"]
AT2 = dict(zip(NAMES2, np.cumsum([0] + SPLITS2[:-1]).tolist()))

PROJ1 = [("iq", 0), ("iq", 1), ("iq", 2), ("iq", 3), ("ik", 0), ("bf", 0)]
PROJ1B = ([("bf", 1), ("bf", 2), ("bf", 3)] + [("bq", i) for i in range(4)] + [("aq", i) for i in range(4)]
          + [("ak", 0)] + [("bg", i) for i in range(4)])
PROJ2 = [("u", i) for i in range(4)] + [("kcr", 0), ("vcr", 0)] + [("za", i) for i in range(4)] + [("zs", i) for i in range(4)]


def columns(name, i, at):
    if name == "ik":
        one = np.arange(at["ik"], at["ik"] + 64)
        return np.concatenate([one, one])
    return np.arange(at[name] + P * i, at[name] + P * (i + 1))


def by_threes(tiles):
    return [tiles[i:i + 3] for i in range(0, len(tiles), 3)]


def span(at, *parts):
    return np.concatenate([np.arange(at[n] + a, at[n] + b) for n, a, b in parts])


ROWS1 = [("av", [("av", 0, 128), ("iw", 0, 8), ("ckpe", 0, 64)])]
ROWS1B = [("bi0", [("bi", 0, 384)]), ("bi1", [("bi", 384, 512), ("ckv", 0, 256)]), ("cq", [("cq", 0, 384)])]
ROWS2 = [("q0", [("q", 0, 384)]), ("q1", [("q", 384, 512), ("ksl", 0, 128), ("vsl", 0, 128)]),
         ("w", [("kwn", 0, 128), ("vwn", 0, 128), ("gbr", 0, 24)])]


def plan():
    out = [(f"proj1_{i}", len(c) * KD * P) for i, c in enumerate(by_threes(PROJ1))]
    out += [("rows1_av", KD * 200)]
    out += [(f"proj1b_{i}", len(c) * KD * P) for i, c in enumerate(by_threes(PROJ1B))]
    out += [(f"rows1_{n}", KD * 384) for n, _ in ROWS1B]
    out += [("qb", 3 * 768), ("kvb", 2 * 1024)]
    for j in range(8):
        out.append((f"gate_{j}", 3 * KD * P))
        if j % 2 == 0:
            out.append((f"up_{j // 2}", 2 * 3 * 4 * P))
    out += [(f"wout_{i}", len(c) * KD * P) for i, c in enumerate(by_threes(range(8)))]
    out += [(f"ff_{j}", 2 * KD * P) for j in range(NFF)]
    out += [(f"down_{j}", NFF * P) for j in range(8)]
    out += [(f"ada_{i}", 3 * KD * P) for i in range(8)]
    out += [(f"proj2_{i}", len(c) * KD * P) for i, c in enumerate(by_threes(PROJ2))]
    out += [(f"rows2_{n}", KD * sum(b - a for _, a, b in parts)) for n, parts in ROWS2]
    out += [("glu", 4 * 512)]
    out += [(f"cmp_{kv}{i}", 256 * n) for kv in "kv" for i, n in enumerate((12, 12, 8))]
    out += [(f"wout2_{i}", len(c) * KD * P) for i, c in enumerate(by_threes(range(8)))]
    return out


def weight_stream(a):
    out = np.zeros((len(plan()), P, CHUNK), np.float32)
    at = {n: i for i, (n, _) in enumerate(plan())}

    def put(name, block):
        out[at[name], :, :block.shape[1]] = block

    w = a["w_in"][0]
    for tag, tiles in (("proj1", PROJ1), ("proj1b", PROJ1B)):
        for i, c in enumerate(by_threes(tiles)):
            put(f"{tag}_{i}", np.concatenate([tiles_of(w, columns(n, k, AT1)) for n, k in c], 1))
    for n, parts in ROWS1 + ROWS1B:
        put(f"rows1_{n}", tiles_of(w, span(AT1, *parts)))
    h = np.arange(4)[:, None]
    put("qb", tiles_of(a["mla_w_qb"][0], np.concatenate([(h * 192 + np.arange(128)).ravel(), (h * 192 + 128 + np.arange(64)).ravel()])))
    put("kvb", tiles_of(a["mla_w_kvb"][0], np.concatenate([(h * 256 + np.arange(128)).ravel(), (h * 256 + 128 + np.arange(128)).ravel()])))
    for j in range(8):
        put(f"gate_{j}", np.concatenate([tiles_of(w, AT1["gate"] + D * b + P * j + np.arange(P)) for b in range(3)], 1))
        if j % 2 == 0:
            put(f"up_{j // 2}", np.concatenate([tiles_of(a[f"w_up_{b}"][0], P * (j + e) + np.arange(P)) for e in range(2) for b in "abc"], 1))
    for i, c in enumerate(by_threes(range(8))):
        put(f"wout_{i}", np.concatenate([tiles_of(a["w_out"][0], P * j + np.arange(P)) for j in c], 1))
        put(f"wout2_{i}", np.concatenate([tiles_of(a["w_out_2"][0], P * j + np.arange(P)) for j in c], 1))
    for j in range(NFF):
        put(f"ff_{j}", np.concatenate([tiles_of(a[n][0], P * j + np.arange(P)) for n in ("w_ffn_gate", "w_ffn_up")], 1))
    for j in range(8):
        put(f"down_{j}", tiles_of(a["w_ffn_down"][0], P * j + np.arange(P)))
        put(f"ada_{j}", np.concatenate([tiles_of(a["w_ada_2"][0], P * (3 * j + e) + np.arange(P)) for e in range(3)], 1))
    w2 = a["w_in_2"][0]
    for i, c in enumerate(by_threes(PROJ2)):
        put(f"proj2_{i}", np.concatenate([tiles_of(w2, columns(n, k, AT2)) for n, k in c], 1))
    for n, parts in ROWS2:
        put(f"rows2_{n}", tiles_of(w2, span(AT2, *parts)))
    for kv in "kv":
        m = a[f"cmp_w1_{kv}_2"][0].reshape(32, 64, 256).transpose(1, 0, 2).reshape(64, -1)
        m = np.concatenate([m, m], 0)
        for i, (lo, n) in enumerate(((0, 12), (12, 12), (24, 8))):
            put(f"cmp_{kv}{i}", m[:, lo * 256:(lo + n) * 256])
    put("glu", tiles_of(a["glu_w_2"][0], np.arange(512)))
    return out


def small_inputs(a):
    def col(v):
        return v.reshape(-1, P).T

    def row(v):
        return np.broadcast_to(v.reshape(1, -1), (P, v.size))

    c = {
        "g_attn": col(a["attn_norm"][0]), "g_ffn": col(a["ffn_norm"][0]), "g_final": col(a["final_norm"]),
        "g_cq": col(a["mla_q_norm"][0]), "g_ckv": col(a["mla_kv_norm"][0]), "g_ob": col(a["hgrn_out_norm"][0]),
        "g_2": col(a["norm_g_2"][0]), "b_ada": col(a["b_ada_2"][0]), "c2": col(a["c_2"][0]),
        "glu_b": col(a["glu_b_2"][0]), "ssm_d": col(a["ssm_d_2"][0]), 
        "g_q": row(a["q_norm_g_2"][0]), "g_kc": row(a["k_cmp_norm_g_2"][0]), "g_ks": row(a["k_slc_norm_g_2"][0]),
        "g_kw": row(a["k_win_norm_g_2"][0]),
    }
    for name, shift in (("rel", 0), ("rel_before", 1)):
        m = np.zeros((4, 32, 4, 4), np.float32)
        for j in range(4):
            m[j, shift:, j, :] = a["rel_bias"][0:32 - shift]
        c[name] = m.reshape(P, 16)
    for kv in "kv":
        pos = a[f"cmp_pos_{kv}_2"][0].T
        c[f"pos_{kv}"] = np.concatenate([pos, pos], 0)
        c[f"w2_{kv}"] = tiles_of(a[f"cmp_w2_{kv}_2"][0], np.arange(64))
    c["a_re"] = a["ssm_a_re_2"][0].reshape(16, P).T
    c["a_im"] = a["ssm_a_im_2"][0].reshape(16, P).T
    c["log_dt"] = np.repeat(a["ssm_log_dt_2"][0].reshape(16, 2), 64, axis=1).T
    return c


def state_space_matrices(a):
    parts = []
    for z in ("re", "im"):
        b = a[f"ssm_b_{z}_2"][0]
        m = np.zeros((P, 4, P), np.float32)
        for g in range(32):
            ct, r = divmod(g, 8)
            m[16 * r:16 * r + 16, ct, 64 * (g % 2):64 * (g % 2) + 64] = b[g].T
        parts.append(m.reshape(P, -1))
        cc = a[f"ssm_c_{z}_2"][0]
        m = np.zeros((P, 16, 32), np.float32)
        for g in range(32):
            m[64 * (g % 2):64 * (g % 2) + 64, g // 2, 16 * (g % 2):16 * (g % 2) + 16] = cc[g].T
        parts.append(m.reshape(P, -1))
    return np.concatenate(parts, 1)


SMALL = {"g_attn": 8, "g_ffn": 8, "g_final": 8, "g_cq": 3, "g_ckv": 2, "g_ob": 1, "g_2": 8, "b_ada": 24, "c2": 8,
         "glu_b": 4, "ssm_d": 4, "rel": 16, "rel_before": 16, "g_q": 64, "g_kc": 64, "g_ks": 64, "g_kw": 64, "pos_k": 32, "w2_k": 128,
         "pos_v": 32, "w2_v": 128, "a_re": 16, "a_im": 16, "log_dt": 16}
CONST = {"ident": P, "ones": P, "causal": P, "level": (LEVELS + 1) * P, "reset": T, "time": T, "invf": 32,
         "cos2": P, "sin2": P, "cmp_neg": NT * NCMP, "cmp_ok": NT * NCMP, "least": 1, "misc": 4}


def offsets(sizes):
    at, out = 0, {}
    for n, k in sizes.items():
        out[n] = (at, at + k)
        at += k
    return out, at


class Tally:

    def __init__(self, known):
        self.count, self.known, self.named = {}, known, {}

    def up(self, sem, name=None, by=1):
        n = self.count[sem.name] = self.count.get(sem.name, 0) + by
        if name is not None:
            assert name not in self.named, name
            self.named[name] = n
        return n

    def at(self, name):
        return self.known[name] if self.known is not None else 1


def two_blocks_kernel(nc, wstream, ssm, xT, consts, small, pos_row, pos_col, pos_key, outT, known):
    tally = Tally(known)
    up, at = tally.up, tally.at

    base = {}

    def sb(name, cols, dt=F32):
        base[name] = -(-nc.sbuf_base // 32) * 32
        return nc.alloc_sbuf_tensor(name, [P, cols], dt)

    def rounded(name, cols):
        return nc.alloc_sbuf_tensor_at(f"{name}_r", [P, cols], F32R, offset=base[name])

    ring = sb("ring", SLOTS * CHUNK)
    x_sb = sb("x_sb", KD * T)
    h_sb = sb("h_sb", KD * T)
    tiles = sb("tiles", 22 * T)
    rows = sb("rows", 24 * P)
    wide = sb("wide", 5760)
    work = sb("work", 4608)
    probs = sb("probs", 2 * T)
    probsT = sb("probsT", 2 * T)
    cst = sb("cst", sum(CONST.values()))
    sml = sb("sml", sum(SMALL.values()))
    chosen = sb("chosen", NT * (NT + 1) // 2 * P, BF16)
    prow = sb("prow", T, I32)
    pcol = sb("pcol", NT, I32)
    pkey = sb("pkey", P, I32)
    stat = sb("stat", 512)
    trig = sb("trig", 2 * NT * 32)

    ring_r, h_r, wide_r = rounded("ring", SLOTS * CHUNK), rounded("h_sb", KD * T), rounded("wide", 5760)
    rows_r, work_r = rounded("rows", 24 * P), rounded("work", 4608)
    X = x_sb[:, :].rearrange("p (k t) -> p k t", k=KD)
    H = h_sb[:, :].rearrange("p (k t) -> p k t", k=KD)
    TL = tiles[:, :].rearrange("p (k t) -> p k t", k=22)
    ROW = rows[:, 0:NT * 712].rearrange("p (n c) -> p n c", n=NT)
    coff, _ = offsets(CONST)
    soff, _ = offsets(SMALL)

    def con(name):
        a, b = coff[name]
        return cst[:, a:b]

    def sm(name):
        a, b = soff[name]
        return sml[:, a:b]

    ident, ones, causal = con("ident"), con("ones"), con("causal")
    G = [nc.alloc_psum_tensor(f"gemm{i}", [P, T], F32) for i in range(3)]
    S = [nc.alloc_psum_tensor(f"score{i}", [P, T], F32) for i in range(2)]
    U = [nc.alloc_psum_tensor(f"turn{i}", [P, T], F32) for i in range(2)]
    O = [nc.alloc_psum_tensor("sum0", [P, T], F32)]

    def part(t, a, n, **shape):
        v = t[:, a:a + n]
        return v.rearrange("p (k t) -> p k t", **shape) if shape else v

    REC_E = [part(work, 0, T), part(work, T, T)]
    REC_QK = [part(work, 2 * T, T), part(work, 3 * T, T)]
    REC_QX, REC_KX, REC_AT = part(work, 4 * T, T), part(work, 5 * T, T), part(work, 6 * T, T)
    REC_X = part(work, 7 * T, 6 * P)
    REC_O, REC_QS = part(wide, 2560, 4 * T, k=NT), part(wide, 4608, 3 * P)

    def REC_FAR(a, c):
        i = {(0, 1): 0, (1, 2): 1, (2, 3): 2, (0, 2): 3, (1, 3): 4, (0, 3): 5}[a, c]
        return REC_X[:, i * P:(i + 1) * P]

    CQ, CKV = part(wide, 0, 1536, k=NT), part(wide, 1536, 1024, k=NT)
    VC, QPE = part(wide, 2560, 2048, k=NT), part(wide, 4608, 1024, k=NT)
    KPE2 = part(wide, 0, 512, k=NT)
    CQT, CKVT = part(work, 0, 1536, k=3), part(work, 1536, 1024, k=2)
    QPET, KPET = part(work, 2560, 1024, k=2), part(work, 3584, T)
    BIAS = part(wide, 0, 5120, k=4)
    INDEX = [None] + [part(work, n * T, (n + 1) * P) for n in range(1, NT)]
    REL = [part(work, 6 * T + 8 * z, 8).bitcast(BF16) for z in range(3)]
    KEYSTEP = part(work, 6 * T + 64, P)

    def STEPS(g, cols):
        return part(work, 2 * T + g % 8 * P, P).bitcast(BF16)[:, 0:cols]

    BIAS_PARTS = [(0, (0, 1)), (0, (2, 3)), (1, (1, 2)), (1, (3,)), (2, (2, 3)), (3, (3,))]
    LOGITS = [part(work, 4 * T, T), part(work, 5 * T, T)]

    def upto(n):
        return n * (n + 1) // 2 * P

    H_HEAD = part(wide_r, 0, KD * T, k=KD)
    H_REST = h_r[:, :].rearrange("p (k t) -> p k t", k=KD)
    FF_HEAD = [part(rows_r, 0, 2 * KD * P), part(work_r, 4 * T, 2 * KD * P)]
    SIDE = [2, 1, 1] * 5 + [2]
    MODROW = rows
    MIX = [0, 1, 2, 3, 4, 18, 19, 20]
    GATE = [part(work, (6 + b) * T, T) for b in range(3)]
    SILU_C, MOD, GAIN2, POSB = stat[:, 192:200], stat[:, 200:224], stat[:, 224:232], stat[:, 232:240]
    R2 = part(wide, 0, NT * 1048, k=NT)
    KT2 = part(rows, 0, 4 * T, k=4)

    def HID(kv):
        return part(rows, 2048 + 128 * (kv == "v"), P, k=2)

    def HROW(kv):
        return part(work, 2 * T + 256 * (kv == "v"), 256)

    CB = part(work, 4 * T, 32 * 2 * NCMP, k=32)
    KC2, VCMP, KCT = part(rows, 2304, 256, k=2), part(rows, 2560, 128), part(rows, 2688, 64)
    CMP_P = part(probs, 0, 4 * NCMP)
    ATT = part(work, 0, 4 * T, k=NT)

    def K2(i):
        return part(work, 4 * T + i * T, T, k=NT)

    GB = [part(wide, 4712 + 32 * z, 32, k=NT) for z in range(3)]
    KCRAW = part(work, 0, P)
    GLUB = stat[:, 236:240]
    SSM_W = tiles[:, 14 * T:18 * T]
    BB = [SSM_W[:, 1024 * z:1024 * z + 512].rearrange("p (c n) -> p c n", c=4) for z in range(2)]
    CC = [SSM_W[:, 1024 * z + 512:1024 * z + 1024].rearrange("p (k t) -> p k t", k=16) for z in range(2)]

    def SSM(name, j=0):
        name = name + str(j % 2) if name in ("sr", "si", "sin", "cos", "br", "bi") else name
        i = ["t1", "t2", "wr", "wi", "sr0", "sr1", "si0", "si1", "turns", "sin0", "sin1", "cos0", "cos1",
             "br0", "br1", "bi0", "bi1"].index(name)
        return part(work, i * T, T) if i < 9 else part(rows, (i - 9) * T, T) if i < 15 else TL[:, i + 3, :]

    SC = {n: stat[:, 240 + 16 * i:256 + 16 * i] for i, n in enumerate(
        ("dt", "turn", "hi", "lo", "rho", "t", "u", "s", "c", "h", "x", "y", "den", "kr", "ki", "v"))}

    def sem(name):
        return nc.alloc_semaphore(name)

    const_in, small_in, x_in = sem("const_in"), sem("small_in"), sem("x_in")
    slot_in = [sem(f"slot{i}_in") for i in range(SLOTS)]
    gemm_full, gemm_done = sem("gemm_full"), sem("gemm_done")
    score_full, score_done = sem("score_full"), sem("score_done")
    turn_full, turn_done = sem("turn_full"), sem("turn_done")
    sum_full, sum_done = sem("sum_full"), sem("sum_done")
    steps_used = sem("steps_used")
    act_step, dve_step, pool_step = sem("act_step"), sem("dve_step"), sem("pool_step")
    ssm_in, stored = sem("ssm_in"), sem("stored")

    chunks = plan()
    chunk_at = {n: i for i, (n, _) in enumerate(chunks)}

    def chunk(name, t=ring):
        i = chunk_at[name]
        return t[:, (i % SLOTS) * CHUNK:(i % SLOTS) * CHUNK + chunks[i][1]]

    block = nc.Block()
    with block:
        @block.sync
        def _(sp):
            sp.dma_start(cst[:, :], consts).then_inc(const_in, 16)
            sp.dma_start(sml[:, :], small).then_inc(small_in, 16)
            sp.dma_start(x_sb[:, :], xT).then_inc(x_in, 16)
            sp.dma_start(prow[:, :], pos_row).then_inc(small_in, 16)
            sp.dma_start(pcol[:, :], pos_col).then_inc(small_in, 16)
            sp.dma_start(pkey[:, :], pos_key).then_inc(small_in, 16)
            for i, (name, cols) in enumerate(chunks):
                if name == "proj2_0":
                    sp.wait_ge(turn_full, at("used down_7"))
                    sp.dma_start(SSM_W, ssm).then_inc(ssm_in, 16)
                if i >= SLOTS:
                    last = chunks[i - SLOTS][0]
                    sp.wait_ge(turn_full if last[:3] in TURN_CHUNKS else gemm_full, at(f"used {last}"))
                sp.dma_start(ring[:, (i % SLOTS) * CHUNK:(i % SLOTS) * CHUNK + cols],
                             wstream[i, :, 0:cols]).then_inc(slot_in[i % SLOTS], 16)
            sp.wait_ge(dve_step, at("out ready"))
            sp.dma_start(outT, x_sb[:, :]).then_inc(stored, 16)
            sp.wait_ge(stored, 16)

        @block.tensor
        def _(pe):
            seen, sums = set(), [0]

            def have(name):
                if name not in seen:
                    seen.add(name)
                    i = chunk_at[name]
                    pe.wait_ge(slot_in[i % SLOTS], 16 * (i // SLOTS + 1))
                return chunk(name)

            def gemm_bank():
                n = tally.count.get("gemm_full", 0)
                if n >= 3:
                    pe.wait_ge(gemm_done, n - 2)
                return G[n % 3]

            def score_bank():
                n = tally.count.get("score_full", 0)
                if n >= 2:
                    pe.wait_ge(score_done, n - 1)
                return S[n % 2]

            def turn_bank():
                n = tally.count.get("turn_full", 0)
                if n >= 2:
                    pe.wait_ge(turn_done, n - 1)
                return U[n % 2]

            def sum_bank():
                n = sums[0]
                sums[0] += 1
                if n >= 1:
                    pe.wait_ge(sum_done, n)
                return O[0]

            def product(out, pairs):
                for i, (l, r) in enumerate(pairs):
                    mm = pe.matmul(out, l, r, start=(i == 0), stop=(i == len(pairs) - 1))
                return mm

            def split_product(out, weights, acts, ready=()):
                last = len(weights) - 1
                for k, ((wh, wr), (ah, ar)) in enumerate(zip(weights, acts)):
                    if ready:
                        pe.wait_ge(dve_step, at(ready[k]))
                    pe.matmul(out, wh, ah, start=(k == 0), stop=False)
                    pe.matmul(out, wh, ar, start=False, stop=False)
                    mm = pe.matmul(out, wr, ah, start=False, stop=(k == last))
                return mm

            def feature_units(tag, tiles_, acts, to_turn=False):
                full = turn_full if to_turn else gemm_full
                for i, c in enumerate(by_threes(tiles_)):
                    w = have(f"{tag}_{i}").rearrange("p (c k n) -> p c k n", c=len(c), k=KD)
                    for e in range(len(c)):
                        b = turn_bank() if to_turn else gemm_bank()
                        mm = product(b[:, :], [(w[:, e, k, :], acts(k)) for k in range(KD)])
                        mm.then_inc(full, 1)
                        up(full)
                        if e == len(c) - 1:
                            tally.named[f"used {tag}_{i}"] = tally.count[full.name]
                        yield

            def row_units(chunk_name, cols, acts, kt=KD):
                w = have(chunk_name).rearrange("p (k n) -> p k n", k=kt)
                for n in range(NT):
                    b = gemm_bank()
                    mm = product(b[:, 0:cols], [(acts[:, k, n * P:(n + 1) * P], w[:, k, :]) for k in range(kt)])
                    mm.then_inc(gemm_full, 1)
                    up(gemm_full, f"full {chunk_name} {n}")
                    if n == NT - 1:
                        tally.named[f"used {chunk_name}"] = tally.count["gemm_full"]
                    yield

            def feature_tiles(*a, **k):
                for _ in feature_units(*a, **k):
                    pass

            def row_tiles(*a, **k):
                for _ in row_units(*a, **k):
                    pass

            def square_sums(name, src):
                pe.wait_ge(dve_step, at(f"squares {name}"))
                b = gemm_bank()
                product(b[:, :], [(ones, src[:, k, :]) for k in range(KD)]).then_inc(gemm_full, 1)
                up(gemm_full, f"full sums {name}")

            def turn(name, blocks, ready):
                b = turn_bank()
                pe.wait_ge(*ready)
                for src, r, dst in blocks:
                    mm = pe.transpose(b[0:src.shape[1], dst:dst + r], src, ident[0:r, 0:r])
                mm.then_inc(turn_full, 1)
                up(turn_full, f"full turn {name}")

            def attention(name, heads, query, key, value, width, before, turn_o=True):
                items = [(n, h) for n in range(NT) for h in range(heads)]
                last = len(items)
                for i in range(last + 3):
                    if i < last:
                        n, h = items[i]
                        cols = (n + 1) * P
                        b = score_bank()
                        if h == 0:
                            before(n)
                        pairs = [(q[:, n * P:(n + 1) * P], k[:, 0:cols]) for q, k in zip(query(h), key(h))]
                        for j, (l, r) in enumerate(pairs):
                            mm = pe.matmul(b[:, 0:cols], l, r, start=(j == 0), stop=False)
                        mm = pe.matmul(b[:, n * P:cols], ident, causal, start=False, stop=True)
                        mm.then_inc(score_full, 1)
                        up(score_full, f"full {name} score {i}")
                    if 1 <= i <= last:
                        n, h = items[i - 1]
                        b = turn_bank()
                        pe.wait_ge(score_done, at(f"{name} probs {i - 1}"))
                        for j in range(n + 1):
                            mm = pe.transpose(b[:, j * P:(j + 1) * P],
                                              probs[:, (i - 1) % 2 * T + j * P:(i - 1) % 2 * T + (j + 1) * P], ident)
                        mm.then_inc(turn_full, 1)
                        up(turn_full, f"full {name} turn {i - 1}")
                    if 2 <= i <= last + 1:
                        n, h = items[i - 2]
                        if h == 0:
                            b = sum_bank()
                        pe.wait_ge(turn_done, at(f"{name} probsT {i - 2}"))
                        for j in range(n + 1):
                            mm = pe.matmul(O[0][:, h * width:(h + 1) * width],
                                           probsT[:, (i - 2) % 2 * T + j * P:(i - 2) % 2 * T + (j + 1) * P],
                                           value(h, j), start=(j == 0), stop=(j == n))
                        mm.then_inc(sum_full, 1)
                        up(sum_full, f"{name} summed {i - 2}")
                    if i >= 3 and items[i - 3][1] == heads - 1:
                        n = items[i - 3][0]
                        if turn_o:
                            turn(f"{name} o {n}", [(work[:, j * P:(j + 1) * P], P, j * P) for j in range(4)],
                                 (sum_done, at(f"{name} o {n}")))


            def rows_out(name, cols, acts, w, kt, used):
                for n in range(NT):
                    b = gemm_bank()
                    product(b[:, 0:cols], [(acts(k)[:, n * P:(n + 1) * P], w(k)) for k in range(kt)]).then_inc(gemm_full, 1)
                    up(gemm_full)

            pe.wait_ge(const_in, 16)
            square_sums("attn", H)
            pe.wait_ge(dve_step, at("normed attn"))
            feature_tiles("proj1", PROJ1, lambda k: H[:, k, :])
            row_tiles("rows1_av", 200, H)
            pe.wait_ge(gemm_done, at("have ik"))
            for i in range(3 * 8):
                n, h = 1 + i // 8, i % 8
                b, r = score_bank(), slice(64 * (h % 2), 64 * (h % 2) + 64)
                pe.matmul(b[:, 0:(n + 1) * P], TL[r, h // 2, n * P:(n + 1) * P], TL[r, 4, 0:(n + 1) * P],
                          start=True, stop=True).then_inc(score_full, 1)
                up(score_full, f"full index {i}")
            feature_tiles("proj1b", PROJ1B, lambda k: H[:, k, :])
            for n_ in ("bi0", "bi1", "cq"):
                row_tiles(f"rows1_{n_}", 384, H)

            V = ROW[:, :, 200:712]
            for h in range(4):
                q, k = TL[:, 9 + h, :], TL[:, h, :]
                pe.wait_ge(gemm_done, at("have bg"))
                pe.wait_ge(dve_step, at("keys rec"))

                def blocks(name, pairs, ready):
                    b = turn_bank()
                    pe.wait_ge(dve_step, at(ready))
                    for j, (l, r) in enumerate(pairs):
                        mm = pe.matmul(b[:, j * P:(j + 1) * P], l, r, start=True, stop=True)
                    mm.then_inc(turn_full, 1)
                    up(turn_full, name)

                def ch(a, c):
                    return a[:, c * P:(c + 1) * P]

                blocks(f"full rec diag {h}", [(ch(k, c), ch(q, c)) for c in range(4)], "keys rec")
                blocks(f"full rec near {h}", [(ch(REC_KX, 0), ch(REC_QX, 1)), (ch(REC_KX, 1), ch(REC_QX, 2)),
                                              (ch(REC_KX, 2), ch(REC_QX, 3)), (ch(REC_KX, 0), ch(REC_QS, 0))], f"rec cross {h}")
                blocks(f"full rec far {h}", [(ch(REC_KX, 1), ch(REC_QS, 1)), (ch(REC_KX, 0), ch(REC_QS, 2))], f"rec cross {h}")
                for l in range(LEVELS):
                    qk = REC_QK[l % 2]
                    blocks(f"full rec level {h} {l}", [(ch(qk, c), ch(qk, c)) for c in range(4)], f"rec scaled {h} {l}")
                b = sum_bank()
                pe.wait_ge(turn_done, at(f"rec weights {h}"))
                for c in range(4):
                    parts = [(REC_FAR(a, c), V[:, a, h * P:(h + 1) * P]) for a in range(c)] + [(ch(REC_AT, c), V[:, c, h * P:(h + 1) * P])]
                    mm = product(b[:, c * P:(c + 1) * P], parts)
                mm.then_inc(sum_full, 1)
                up(sum_full, f"full rec o {h}")
            for n in range(NT):
                turn(f"rec o {n}", [(REC_O[:, n, j * P:(j + 1) * P], P, j * P) for j in range(4)], (dve_step, at("rec normed")))

            for j in range(3):
                turn(f"cq {j}", [(CQ[:, n, j * P:(j + 1) * P], P, n * P) for n in range(NT)], (dve_step, at("latents normed")))
            for j in range(2):
                turn(f"ckv {j}", [(CKV[:, n, j * P:(j + 1) * P], P, n * P) for n in range(NT)], (dve_step, at("latents normed")))
            pe.wait_ge(turn_done, at("ckvT"))
            w = have("qb").rearrange("p (k n) -> p k n", k=3)
            for j in range(4):
                b = gemm_bank()
                product(b[:, :], [(w[:, k, j * P:(j + 1) * P], CQT[:, k, :]) for k in range(3)]).then_inc(gemm_full, 1)
                up(gemm_full)
            rows_out("qpe", 256, lambda k: CQT[:, k, :], lambda k: w[:, k, 512:768], 3, "qb")
            tally.named["used qb"] = tally.count["gemm_full"]
            w2 = have("kvb").rearrange("p (k n) -> p k n", k=2)
            for j in range(4):
                b = gemm_bank()
                product(b[:, :], [(w2[:, k, j * P:(j + 1) * P], CKVT[:, k, :]) for k in range(2)]).then_inc(gemm_full, 1)
                up(gemm_full)
            rows_out("vc", 512, lambda k: CKVT[:, k, :], lambda k: w2[:, k, 512:1024], 2, "kvb")
            tally.named["used kvb"] = tally.count["gemm_full"]
            turn("kpe", [(KPE2[:, n, :], P, n * P) for n in range(NT)], (dve_step, at("roped")))
            for j in range(2):
                turn(f"qpe {j}", [(QPE[:, n, j * P:(j + 1) * P], P, n * P) for n in range(NT)], (dve_step, at("roped")))
            pe.wait_ge(turn_done, at("qpeT"))
            pe.wait_ge(gemm_done, at("have vc"))

            def half(t, h):
                return t[64 * (h % 2):64 * (h % 2) + 64]

            attention("mla", 4, lambda h: [TL[:, 5 + h, :], half(QPET[:, h // 2, :], h)],
                      lambda h: [TL[:, h, :], half(KPET, h)],
                      lambda h, j: VC[:, j, h * P:(h + 1) * P], P, lambda n: None)
            pe.wait_ge(dve_step, at("increments"))
            for c_, (key, queries) in enumerate(BIAS_PARTS):
                banks = [turn_bank()]
                if len(queries) == 2:
                    n_ = tally.count["turn_full"] + 1
                    pe.wait_ge(turn_done, n_ - 1)
                    banks.append(U[n_ % 2])
                for g in range(32):
                    pe.wait_ge(dve_step, at(f"steps {c_} {g}"))
                    for e, b in enumerate(banks):
                        for z in range(3):
                            mm = pe.matmul(b[:, 16 * g:16 * g + 16], STEPS(g, P * len(banks))[:, e * P:(e + 1) * P], REL[z],
                                           start=(z == 0), stop=(z == 2))
                        if g == 31:
                            mm.then_inc(turn_full, 1)
                            up(turn_full)
                    if g < 31:
                        mm.then_inc(steps_used, 1)
                        up(steps_used, f"bias {c_} {g}")
            attention("dsa", 4, lambda h: [TL[:, 13 + h, :]], lambda h: [TL[:, 17, :]],
                      lambda h, j: ROW[:, j, 0:128], P, lambda n: None)

            branch = {0: 13, 1: 9, 2: 5}
            for j in range(8):
                w = have(f"gate_{j}").rearrange("p (b k n) -> p b k n", b=3, k=KD)
                for b_ in range(3):
                    b = gemm_bank()
                    product(b[:, :], [(w[:, b_, k, :], H[:, k, :]) for k in range(KD)]).then_inc(gemm_full, 1)
                    up(gemm_full)
                tally.named[f"used gate_{j}"] = tally.count["gemm_full"]
                w = have(f"up_{j // 2}").rearrange("p (e b k n) -> p e b k n", e=2, b=3, k=4)
                if j == 0:
                    pe.wait_ge(turn_done, at("dsa oT 3"))
                for b_ in range(3):
                    b = turn_bank()
                    product(b[:, :], [(w[:, j % 2, b_, k, :], TL[:, branch[b_] + k, :]) for k in range(4)]).then_inc(turn_full, 1)
                    up(turn_full)
                if j % 2:
                    tally.named[f"used up_{j // 2}"] = tally.count["turn_full"]
            pe.wait_ge(dve_step, at("mixed"))
            feature_tiles("wout", range(8), lambda k: TL[:, MIX[k], :], to_turn=True)

            square_sums("ffn", H)
            acts = [(H_HEAD[:, k, :], H_REST[:, k, :]) for k in range(KD)]
            for j in range(NFF):
                pe.wait_ge(dve_step, at(f"split ff_{j}"))
                head = FF_HEAD[j % 2].rearrange("p (b k n) -> p b k n", b=2, k=KD)
                rest = chunk(f"ff_{j}", ring_r).rearrange("p (b k n) -> p b k n", b=2, k=KD)
                b = gemm_bank()
                split_product(b[:, :], [(head[:, 0, k, :], rest[:, 0, k, :]) for k in range(KD)], acts,
                              () if j else [f"split ffn {k}" for k in range(KD)]).then_inc(gemm_full, 1)
                up(gemm_full)
                b = turn_bank()
                split_product(b[:, :], [(head[:, 1, k, :], rest[:, 1, k, :]) for k in range(KD)], acts).then_inc(turn_full, 1)
                up(turn_full)
                tally.named[f"used ff_{j}"] = tally.count["turn_full"]
            pe.wait_ge(dve_step, at("silu c"))
            pe.wait_ge(turn_done, at("ff hidden"))
            for j in range(8):
                w = have(f"down_{j}").rearrange("p (k n) -> p k n", k=NFF)
                b = turn_bank()
                product(b[:, :], [(w[:, k, :], TL[:, k, :]) for k in range(NFF)]).then_inc(turn_full, 1)
                up(turn_full)
                tally.named[f"used down_{j}"] = tally.count["turn_full"]
            for i in range(8):
                b = gemm_bank()
                w = have(f"ada_{i}").rearrange("p (c k n) -> p c k n", c=3, k=KD)
                product(b[0:1, 0:384].rearrange("p (c n) -> p c n", c=3),
                        [(SILU_C[:, k:k + 1], w[:, :, k, :]) for k in range(KD)]).then_inc(gemm_full, 1)
                up(gemm_full, f"used ada_{i}")
            square_sums("final", H)

            for i in range(24):
                if i == 0:
                    b = turn_bank()
                    pe.wait_ge(gemm_done, at("have mod"))
                mm = pe.transpose(b[:, i:i + 1], MODROW[0:1, i * P:(i + 1) * P], ident[0:1, 0:1])
            mm.then_inc(turn_full, 1)
            up(turn_full)
            square_sums("block2", H)
            pe.wait_ge(dve_step, at("normed block2"))
            units = itertools.chain(feature_units("proj2", PROJ2, lambda k: H[:, k, :]), row_units("rows2_q0", 384, H),
                                    row_units("rows2_q1", 384, H), row_units("rows2_w", 280, H))
            for _ in range(4):
                next(units)
            pe.wait_ge(ssm_in, 16)
            for j in range(17):
                if j < 16:
                    if j == 0:
                        pe.wait_ge(gemm_done, at("have u"))
                    r = slice(32 * (j % 4), 32 * (j % 4) + 32)
                    for z in range(2):
                        b = gemm_bank()
                        pe.matmul(b[:, :], BB[z][r, j // 4, :], TL[r, 2 + j // 4, :], start=True, stop=True)\
                            .then_inc(gemm_full, 1)
                        up(gemm_full)
                    for _ in range(SIDE[j]):
                        next(units)
                if j >= 1:
                    i = j - 1
                    if i % 4 == 0:
                        b = sum_bank()
                    pe.wait_ge(dve_step, at(f"states {i}"))
                    q_ = slice(32 * (i % 4), 32 * (i % 4) + 32)
                    pe.matmul(O[0][q_, :], CC[0][:, i, :], SSM("sr", i), start=True, stop=False)
                    mm = pe.matmul(O[0][q_, :], CC[1][:, i, :], SSM("si", i), start=False, stop=True)
                    mm.then_inc(sum_full, 1)
                    up(sum_full, f"full y {i}")
            for _ in units:
                pass
            w = have("glu").rearrange("p (k n) -> p k n", k=4)
            pe.wait_ge(act_step, at("y gelu"))
            for j in range(4):
                b = gemm_bank()
                product(b[:, :], [(w[:, k, j * P:(j + 1) * P], TL[:, 2 + k, :]) for k in range(4)]).then_inc(gemm_full, 1)
                up(gemm_full)
            tally.named["used glu"] = tally.count["gemm_full"]

            pe.wait_ge(gemm_done, at("have zs"))
            for kv, tile in (("k", 0), ("v", 1)):
                parts = [(have(f"cmp_{kv}{i}").rearrange("p (l n) -> p l n", n=256), lo, n)
                         for i, (lo, n) in enumerate(((0, 12), (12, 12), (24, 8)))]
                b = gemm_bank()
                pe.wait_ge(dve_step, at(f"blocks {kv}"))
                product(b[0:2 * NCMP, 0:256], [(CB[:, lo + l, :], w[:, l, :]) for w, lo, n in parts for l in range(n)])\
                    .then_inc(gemm_full, 1)
                up(gemm_full)
                for i in range(3):
                    tally.named[f"used cmp_{kv}{i}"] = tally.count["gemm_full"]
            for kv in "kv":
                turn(f"hidden {kv}", [(HROW(kv)[0:2 * NCMP, k * P:(k + 1) * P], 2 * NCMP, 64 * k) for k in range(2)],
                     (gemm_done, at(f"hidden {kv}")))
            for kv in "kv":
                b = gemm_bank()
                pe.wait_ge(turn_done, at(f"hidden T {kv}"))
                w2_ = sm(f"w2_{kv}").rearrange("p (k n) -> p k n", k=2)
                for g in range(2):
                    mm = product(b[0:NCMP, 64 * g:64 * g + 64], [(HID(kv)[:, k, g * NCMP:(g + 1) * NCMP], w2_[:, k, :]) for k in range(2)])
                mm.then_inc(gemm_full, 1)
                up(gemm_full)
            turn("kc", [(KC2[0:NCMP, g, :], NCMP, 32 * g) for g in range(2)], (dve_step, at("kc normed")))
            for j in range(4):
                turn(f"q {j}", [(R2[:, n, j * P:(j + 1) * P], P, n * P) for n in range(NT)], (dve_step, at("q normed")))
            for j in range(4):
                turn(f"qr {j}", [(R2[:, n, j * P:(j + 1) * P], P, n * P) for n in range(NT)], (dve_step, at("q roped")))
            for i in range(4):
                turn(f"k2 {i}", [(K2(i)[:, n, :], P, n * P) for n in range(NT)], (dve_step, at("k roped")))
            pe.wait_ge(turn_done, at("kT 3"))
            def cmp_scores(i):
                n, e = divmod(i, 2)
                b = score_bank()
                for q_ in range(4):
                    h = 2 * q_ + e
                    r = slice(64 * e, 64 * e + 64)
                    mm = pe.matmul(b[:, q_ * NCMP:(q_ + 1) * NCMP], TL[r, 14 + h // 2, n * P:(n + 1) * P],
                                   KCT[r, 32 * (h // 4):32 * (h // 4) + NCMP], start=True, stop=True)
                mm.then_inc(score_full, 1)
                up(score_full, f"full cmp {i}")

            for i in range(8):
                cmp_scores(i)
                n, e = divmod(i, 2)
                b = turn_bank()
                pe.wait_ge(dve_step, at(f"cmp probs {i}"))
                for q_ in range(4):
                    mm = pe.transpose(b[0:NCMP, q_ * P:(q_ + 1) * P], CMP_P[:, q_ * NCMP:(q_ + 1) * NCMP], ident)
                mm.then_inc(turn_full, 1)
                up(turn_full)
                if e == 0:
                    b = sum_bank()
                pe.wait_ge(turn_done, at(f"cmp probsT {i}"))
                for q_ in range(4):
                    h = 2 * q_ + e
                    mm = pe.matmul(O[0][:, 64 * h:64 * h + 64], probsT[0:NCMP, q_ * P:(q_ + 1) * P],
                                   VCMP[0:NCMP, 64 * (h // 4):64 * (h // 4) + 64], start=True, stop=True)
                mm.then_inc(sum_full, 1)
                up(sum_full, f"cmp summed {i}")

            def both(t, h):
                return t[64 * (h % 2):64 * (h % 2) + 64, :]

            for a_, name in enumerate(("slc", "win")):
                attention(name, 8, lambda h: [both(TL[:, 18 + h // 2, :], h)],
                          lambda h: [both(KT2[:, 2 * a_ + h // 4, :], h)],
                          lambda h, j: R2[:, j, (640 if a_ == 0 else 896) + 64 * (h // 4):(640 if a_ == 0 else 896) + 64 * (h // 4) + 64],
                          64, lambda n: None, turn_o=False)
            for n in range(NT):
                turn(f"attn {n}", [(ATT[:, n, j * P:(j + 1) * P], P, j * P) for j in range(4)], (sum_done, at("win o 3")))

            pe.wait_ge(dve_step, at("ssm out"))
            pe.wait_ge(turn_done, at("attn T 3"))
            feature_tiles("wout2", range(8), lambda k: TL[:, 6 + k, :], to_turn=True)

        @block.scalar
        def _(act):
            def step(ins, name=None, sem_=act_step):
                n = up(sem_, name)
                ins.then_inc(sem_, 1)
                act.wait_ge(sem_, n)

            drained = [0]

            def drain(fills, out, name=None, func=ACT.Identity, bias=0.0, scale=1.0, cols=T, rows_=P, src=None):
                n = drained[0]
                drained[0] += 1
                act.wait_ge(gemm_full, n + 1)
                b = G[n % 3][0:rows_, 0:cols] if src is None else src(G[n % 3])
                step(act.activation(out, b, func, bias=bias, scale=scale), name, gemm_done)

            def attention_exp(name, heads, logits=None):
                for i in range(NT * heads):
                    n, h = divmod(i, heads)
                    cols = (n + 1) * P
                    act.wait_ge(dve_step, at(f"{name} max {i}"))
                    if i >= 2:
                        act.wait_ge(turn_full, at(f"full {name} turn {i - 2}"))
                    if h == 0 and n >= 2:
                        act.wait_ge(sum_done, at(f"{name} o {n - 2}"))
                    src = S[(at(f"full {name} score {i}") - 1) % 2][:, 0:cols] if logits is None else logits(i, cols)
                    step(act.activation(probs[:, i % 2 * T:i % 2 * T + cols], src, ACT.Exp,
                                        bias=stat[:, 8 + i % 2:9 + i % 2], scale=1.0,
                                        accum_out=stat[:, 16 + (n % 2) * 8 + h:17 + (n % 2) * 8 + h]),
                         f"{name} probs {i}", score_done)


            def weights_head(name, dst):
                i = chunk_at[name]
                act.wait_ge(slot_in[i % SLOTS], 16 * (i // SLOTS + 1))
                step(act.activation(dst, chunk(name), ACT.Identity), f"head {name}")

            def sums_out(name):
                drain(1, work[:, 0:T], f"mean {name}", bias=con("misc")[:, 1:2], scale=1.0 / D)
                step(act.activation(work[:, T:2 * T], work[:, 0:T], ACT.Sqrt), f"root {name}")

            act.wait_ge(const_in, 16)
            act.wait_ge(small_in, 64)
            sums_out("attn")
            dest = {"iq": 0, "ik": 4, "bf": 5, "bq": 9, "aq": 13, "ak": 17, "bg": 18}
            scales = {"bq": P ** -0.5, "aq": P ** -0.5, "bg": 0.5}

            def project(tiles_, names=()):
                for n, i in tiles_:
                    drain(1, TL[:, dest[n] + i, :], f"tile {n} {i}", scale=scales.get(n, 1.0))

            project(PROJ1)
            for n in range(NT):
                drain(1, ROW[:, n, 0:200], "have ik" if n == NT - 1 else None, cols=200)
            for i in range(24):
                n = 1 + i // 8
                act.wait_ge(score_full, at(f"full index {i}"))
                if i >= 2:
                    act.wait_ge(dve_step, at(f"index added {i - 2}"))
                step(act.activation(probs[:, i % 2 * T:i % 2 * T + (n + 1) * P], S[i % 2][:, 0:(n + 1) * P], ACT.Relu),
                     f"index relu {i}", score_done)
            project(PROJ1B)
            for n in range(NT):
                drain(1, ROW[:, n, 200:584], cols=384)
            for n in range(NT):
                k = drained[0]
                drained[0] += 1
                act.wait_ge(gemm_full, k + 1)
                step(act.activation(ROW[:, n, 584:712], G[k % 3][:, 0:128], ACT.Identity))
                step(act.activation(CKV[:, n, :], G[k % 3][:, 128:384], ACT.Identity), None, gemm_done)
            for n in range(NT):
                drain(1, CQ[:, n, :], "have bg" if n == NT - 1 else None, cols=384)

            f4, k4, w0 = tiles[:, 5 * T:9 * T], tiles[:, 0:4 * T], work[:, 0:4 * T]
            act.wait_ge(dve_step, at("chosen"))
            step(act.activation(k4, f4, ACT.Abs))
            step(act.activation(w0, k4, ACT.Exp, scale=-1.0), "rec u")
            step(act.activation(k4, f4, ACT.Relu))
            step(act.activation(k4, k4, ACT.Exp, scale=-1.0), "rec num")
            act.wait_ge(dve_step, at("rec one plus u"))
            step(act.activation(w0, w0, ACT.Ln, bias=1.0), "rec ln")
            act.wait_ge(dve_step, at("rec log sigmoid"))
            step(act.activation(w0, f4, ACT.Abs, bias=con("misc")[:, 3:4], scale=1.0))
            step(act.activation(w0, w0, ACT.Exp, scale=-1.0))
            step(act.activation(w0, w0, ACT.Ln, bias=1.0), "rec floor")
            act.wait_ge(dve_step, at("rec log f"))
            step(act.activation(w0, tiles[:, 18 * T:22 * T], ACT.Tanh), "rec gate")
            for h in range(4):
                bt = TL[:, 5 + h, :]
                act.wait_ge(dve_step, at(f"rec args {h}"))
                step(act.activation(REC_E[0], bt, ACT.Exp), f"rec eb {h}")
                step(act.activation(REC_E[1], REC_E[1], ACT.Exp), f"rec el {h}")
                for l in range(LEVELS):
                    act.wait_ge(dve_step, at(f"rec args {h} {l}"))
                    step(act.activation(REC_E[l % 2], REC_E[l % 2], ACT.Exp), f"rec e {h} {l}")

            for j in range(4):
                drain(1, TL[:, 5 + j, :], scale=MLA_SCALE)
            for n in range(NT):
                drain(1, QPE[:, n, :], "have qpe" if n == NT - 1 else None, scale=MLA_SCALE, cols=256)
            for j in range(4):
                drain(1, TL[:, j, :])
            for n in range(NT):
                drain(1, VC[:, n, :], "have vc" if n == NT - 1 else None)
            act.wait_ge(dve_step, at("angles"))
            step(act.activation(trig[:, P:2 * P], trig[:, 0:P], ACT.Sin))
            step(act.activation(trig[:, 0:P], trig[:, 0:P], ACT.Abs))
            step(act.activation(trig[:, 0:P], trig[:, 0:P], ACT.Sin, bias=con("misc")[:, 2:3], scale=-1.0), "trig")
            attention_exp("mla", 4)
            attention_exp("dsa", 4, lambda i, cols: LOGITS[i % 2][:, 0:cols])

            for j in range(8):
                for b_ in range(3):
                    if j >= 1 or b_ == 0:
                        act.wait_ge(dve_step, at(f"mixed {j - 1}") if j else at("dsa done"))
                    drain(1, GATE[b_], f"gate {j} {b_}", func=ACT.Tanh, scale=0.5)

            step(act.activation(SILU_C, sm("c2"), ACT.Tanh, scale=0.5), "tanh c")
            act.wait_ge(dve_step, at("mixed"))
            for j in range(2):
                weights_head(f"ff_{j}", FF_HEAD[j])
            sums_out("ffn")
            for k in range(KD):
                act.wait_ge(dve_step, at(f"normed ffn {k}"))
                step(act.activation(H_HEAD[:, k, :], H[:, k, :], ACT.Identity), f"head ffn {k}")
            for j in range(NFF):
                if j >= 2:
                    act.wait_ge(turn_done, at(f"ff {j - 2}"))
                k = drained[0]
                drained[0] += 1
                act.wait_ge(gemm_full, k + 1)
                step(act.activation(part(work, j % 2 * T, T), G[k % 3][:, :], ACT.Tanh, scale=0.5))
                step(act.activation(part(work, (2 + j % 2) * T, T), G[k % 3][:, :], ACT.Identity, scale=0.5),
                     f"ff gate {j}", gemm_done)
                if j + 2 < NFF:
                    act.wait_ge(turn_full, at(f"used ff_{j}"))
                    weights_head(f"ff_{j + 2}", FF_HEAD[j % 2])
            for i in range(8):
                drain(1, MODROW[0:1, 384 * i:384 * i + 384], "have mod" if i == 7 else None, cols=384, rows_=1)
            sums_out("final")
            sums_out("block2")
            scale2 = {"za": 0.5, "zs": 0.25}
            dest2 = {"kcr": 0, "vcr": 1, "u": 2, "za": 6, "zs": 10}
            def drains2():
                for n, i in PROJ2:
                    drain(1, TL[:, dest2[n] + i, :], f"have {n}" if i == 3 else f"have {n} {i}", scale=scale2.get(n, 1.0))
                    yield
                for a_, c_ in ((0, 384), (384, 384), (768, 280)):
                    for n in range(NT):
                        drain(1, R2[:, n, a_:a_ + c_], "have rows2" if (a_, n) == (768, NT - 1) else None, cols=c_)
                        yield

            units = drains2()
            step(act.activation(SC["dt"], sm("log_dt"), ACT.Exp), "dt")
            act.wait_ge(dve_step, at("ssm turn"))
            step(act.activation(SC["rho"], SC["rho"], ACT.Exp), "rho")
            step(act.activation(SC["s"], SC["turn"], ACT.Sin, scale=TWO_PI_IN))
            step(act.activation(SC["h"], SC["turn"], ACT.Sin, scale=TWO_PI_IN / 2))
            step(act.activation(SC["c"], SC["turn"], ACT.Abs))
            step(act.activation(SC["c"], SC["c"], ACT.Sin, scale=-TWO_PI_IN, bias=con("misc")[:, 2:3]), "ssm trig")
            for _ in range(4):
                next(units)
            for j in range(16):
                act.wait_ge(dve_step, at(f"phases {j}"))
                if j >= 2:
                    act.wait_ge(dve_step, at(f"states {j - 2}"))
                step(act.activation(SSM("sin", j), SSM("turns"), ACT.Sin, scale=TWO_PI_IN))
                step(act.activation(SSM("turns"), SSM("turns"), ACT.Abs))
                step(act.activation(SSM("cos", j), SSM("turns"), ACT.Sin, scale=-TWO_PI_IN, bias=con("misc")[:, 2:3]), f"waves {j}")
                drain(1, SSM("br", j))
                drain(1, SSM("bi", j), f"bu {j}")
                for _ in range(SIDE[j]):
                    next(units)
            for _ in units:
                pass
            act.wait_ge(sum_done, at("y 3"))
            step(act.activation(tiles[:, 2 * T:6 * T], tiles[:, 2 * T:6 * T], ACT.Gelu_apprx_tanh), "y gelu")
            step(act.activation(part(work, 0, 4 * T), tiles[:, 10 * T:14 * T], ACT.Tanh, scale=2.0), "tanh zs")
            for j in range(4):
                drain(1, part(work, (4 + j) * T, T), f"glu {j}", func=ACT.Tanh, scale=0.5, bias=GLUB[:, j:j + 1])
            act.wait_ge(dve_step, at("ssm out"))
            for kv in "kv":
                drain(1, HROW(kv)[0:2 * NCMP, :], f"hidden {kv}", func=ACT.Gelu_apprx_tanh, cols=256, rows_=2 * NCMP)
            drain(1, KCRAW[0:NCMP, :], "have kc", cols=P, rows_=NCMP)
            drain(1, VCMP[0:NCMP, :], "have vcmp", cols=P, rows_=NCMP)
            act.wait_ge(dve_step, at("branch logits"))
            for z in range(3):
                step(act.activation(GB[z], GB[z], ACT.Tanh, scale=0.5), "branch gates" if z == 2 else None)
            for i in range(8):
                n, e = divmod(i, 2)
                act.wait_ge(score_full, at(f"full cmp {i}"))
                if i >= 1:
                    act.wait_ge(turn_done, at(f"cmp probsT {i - 1}"))
                step(act.activation(CMP_P, S[(at(f"full cmp {i}") - 1) % 2][:, 0:4 * NCMP], ACT.Identity),
                     f"cmp score {i}", score_done)
                act.wait_ge(dve_step, at(f"cmp less max {i}"))
                step(act.activation(CMP_P, CMP_P, ACT.Exp), f"cmp exp {i}")
            attention_exp("slc", 8)
            attention_exp("win", 8)
            act.wait_ge(dve_step, at("gates free"))
            w2t = part(wide, 6 * T, 4 * T)
            step(act.activation(w2t, tiles[:, 6 * T:10 * T], ACT.Tanh), "tanh za")

        @block.vector
        def _(dve):
            def step(ins, name=None, sem_=dve_step):
                n = up(sem_, name)
                ins.then_inc(sem_, 1)
                dve.wait_ge(sem_, n)

            turned = [0]

            def split(name, x, head, rest):
                dve.wait_ge(act_step, at(f"head {name}"))
                tt(rest, x, head.bitcast(F32), ALU.subtract, f"split {name}")

            def rms_scale(name, gain, out, source=X, shift=None, heads=None):
                a, y, z = work[:, 0:T], work[:, T:2 * T], work[:, 2 * T:3 * T]
                dve.wait_ge(gemm_done, at(f"mean {name}"))
                dve.wait_ge(act_step, at(f"root {name}"))
                step(dve.reciprocal(y, y))
                step(dve.tensor_tensor(z, y, y, ALU.mult))
                step(dve.tensor_tensor(z, z, a, ALU.mult))
                step(dve.tensor_scalar(z, z, -0.5, 1.5, ALU.mult, ALU.add))
                step(dve.tensor_tensor(y, y, z, ALU.mult), f"rstd {name}")
                for k in range(KD):
                    step(dve.scalar_tensor_tensor(out=out[:, k, :], in0=source[:, k, :], scalar=gain(k), in1=y,
                                                  op0=ALU.mult, op1=ALU.mult),
                         f"normed {name} {k}" if heads is not None else
                         f"normed {name}" if k == KD - 1 and shift is None else None)
                    if heads is not None and k >= 2:
                        split(f"{name} {k - 2}", out[:, k - 2, :], heads[:, k - 2, :], H_REST[:, k - 2, :])
                if heads is not None:
                    for k in (KD - 2, KD - 1):
                        split(f"{name} {k}", out[:, k, :], heads[:, k, :], H_REST[:, k, :])
                if shift is not None:
                    for k in range(KD):
                        step(dve.tensor_scalar(out[:, k, :], out[:, k, :], shift(k), None, ALU.add),
                             f"normed {name}" if k == KD - 1 else None)

            def squares(name, source=X, out=H):
                for k in range(KD):
                    step(dve.tensor_tensor(out[:, k, :], source[:, k, :], source[:, k, :], ALU.mult),
                         f"squares {name}" if k == KD - 1 else None)

            def take_turn(name, dst, scalar=None, cols=T, rows_=P, view=None, eng=None):
                n = turned[0]
                turned[0] += 1
                dve.wait_ge(turn_full, n + 1)
                src = U[n % 2][0:rows_, 0:cols]
                if view is not None:
                    src = view(src)
                if scalar is None:
                    ins = dve.tensor_copy(dst, src)
                else:
                    ins = dve.tensor_scalar(dst, src, scalar, None, ALU.mult)
                step(ins, name, turn_done)

            def attention_max(name, heads, finish, take_o=None, logits=None):
                items = [(n, h) for n in range(NT) for h in range(heads)]
                last = len(items)
                for i in range(last + 3):
                    if i < last:
                        n, h = items[i]
                        cols = (n + 1) * P
                        dve.wait_ge(score_full, at(f"full {name} score {i}"))
                        src = S[(at(f"full {name} score {i}") - 1) % 2][:, 0:cols]
                        if i >= 2:
                            dve.wait_ge(score_done, at(f"{name} probs {i - 2}"))
                        if logits is not None:
                            src = logits(i, n, h, src)
                        step(dve.tensor_reduce(stat[:, 8 + i % 2:9 + i % 2], src, AX.X, ALU.max, negate=True),
                             f"{name} max {i}")
                    if 1 <= i <= last:
                        n, h = items[i - 1]
                        if i - 1 >= 2:
                            dve.wait_ge(sum_full, at(f"{name} summed {i - 3}"))
                        take_turn(f"{name} probsT {i - 1}", probsT[:, (i - 1) % 2 * T:(i - 1) % 2 * T + (n + 1) * P],
                                  cols=(n + 1) * P)
                    if 2 <= i <= last + 1 and items[i - 2][1] == heads - 1:
                        finish(items[i - 2][0])
                    if take_o is not None and i >= 3 and items[i - 3][1] == heads - 1:
                        take_o(items[i - 3][0])


            def small_rstd(name, mean, n):
                step(dve.tensor_scalar(mean, mean, 1.0 / n, EPS, ALU.mult, ALU.add), f"mean {name}")
                dve.wait_ge(pool_step, at(f"rstd {name}"))

            def tt(out, a, b, op, name=None):
                step(dve.tensor_tensor(out, a, b, op), name)

            def ts(out, a, s1, s2, o1, o2=None, name=None):
                step(dve.tensor_scalar(out, a, s1, s2, o1, *([o2] if o2 is not None else [])), name)

            def stt(out, a, s_, b, o1, o2, name=None, sem_=dve_step):
                step(dve.scalar_tensor_tensor(out=out, in0=a, scalar=s_, in1=b, op0=o1, op1=o2), name, sem_)

            def sum_out(fill, write):
                dve.wait_ge(sum_full, at(fill))
                write(O[0])

            def probs_over_sums(name, dst, heads, gate=None):
                def finish(n):
                    last = (n + 1) * heads - 1
                    dve.wait_ge(score_done, at(f"{name} probs {last}"))
                    r = stat[:, 16 + (n % 2) * 8:16 + (n % 2) * 8 + heads]
                    step(dve.reciprocal(r, r))
                    if gate is not None:
                        tt(r, r, gate(n), ALU.mult)
                    dve.wait_ge(sum_full, at(f"{name} summed {last}"))
                    w = T // heads
                    o3 = O[0][:, :].rearrange("p (h d) -> p h d", h=heads)
                    rb = r.unsqueeze(2).broadcast_to([P, heads, w])
                    if gate is None:
                        if n:
                            dve.wait_ge(turn_full, at(f"full turn {name} o {n - 1}"))
                        step(dve.tensor_tensor(dst(n).rearrange("p (h d) -> p h d", h=heads), o3, rb, ALU.mult),
                             f"{name} o {n}", sum_done)
                    else:
                        t_ = part(wide, 4200, T)
                        step(dve.tensor_tensor(t_.rearrange("p (h d) -> p h d", h=heads), o3, rb, ALU.mult))
                        step(dve.tensor_tensor(dst(n), dst(n), t_, ALU.add), f"{name} o {n}", sum_done)
                return finish

            def o_to_tiles(name, first):
                def take(n):
                    take_turn(f"{name} oT {n}", TL[:, first:first + 4, n * P:(n + 1) * P],
                              view=lambda v: v.rearrange("p (j t) -> p j t", j=4))
                return take

            dve.wait_ge(const_in, 16)
            dve.wait_ge(x_in, 16)
            squares("attn")
            dve.wait_ge(small_in, 64)
            rms_scale("attn", lambda k: sm("g_attn")[:, k:k + 1], H)
            for i in range(24):
                n, h = 1 + i // 8, i % 8
                r, iw = probs[:, i % 2 * T:i % 2 * T + (n + 1) * P], ROW[:, n, 128 + h:129 + h]
                dve.wait_ge(score_done, at(f"index relu {i}"))
                if h == 0:
                    ts(INDEX[n], r, iw, None, ALU.mult, name=f"index added {i}")
                else:
                    stt(INDEX[n], r, iw, INDEX[n], ALU.mult, ALU.add, name=f"index added {i}")
            step(dve.tensor_copy(chosen[:, 0:P], causal))
            for n in range(1, NT):
                a = INDEX[n]
                ts(a, a, (64 ** -0.5) * (8 ** -0.5), None, ALU.mult)
                tt(a[:, n * P:(n + 1) * P], a[:, n * P:(n + 1) * P], causal, ALU.add)
                for _i in range(TOPK // 8):
                    step(dve.max(stat[:, 0:8], a))
                    step(dve.match_replace(out=a, in_to_replace=stat[:, 0:8], in_values=a, imm_value=TAKEN))
                ts(chosen[:, upto(n):upto(n + 1)], a, TAKEN, NEG, ALU.not_equal, ALU.mult, name="chosen" if n == 3 else None)

            f4, k4, w0, w1 = tiles[:, 5 * T:9 * T], tiles[:, 0:4 * T], work[:, 0:4 * T], work[:, 4 * T:8 * T]
            dve.wait_ge(gemm_done, at("have bg"))
            dve.wait_ge(act_step, at("rec u"))
            ts(w1, w0, 1.0, None, ALU.add, name="rec one plus u")
            step(dve.reciprocal(w1, w1))
            dve.wait_ge(act_step, at("rec num"))
            tt(k4, k4, w1, ALU.mult, "keys rec")
            dve.wait_ge(act_step, at("rec ln"))
            stt(f4, f4, 0.0, w0, ALU.min, ALU.subtract, name="rec log sigmoid")
            dve.wait_ge(act_step, at("rec floor"))
            stt(f4, f4, LOG_FLOOR, w0, ALU.max, ALU.add, name="rec log f")
            for h in range(4):
                bt = TL[:, 5 + h, :]
                step(dve.tensor_tensor_scan(bt, con("reset"), bt, 0.0, ALU.mult, ALU.add))
            dve.wait_ge(act_step, at("rec gate"))
            g4 = tiles[:, 18 * T:22 * T]
            stt(g4, w0, 1.0, g4, ALU.add, ALU.mult)
            for h in range(4):
                bt, q, k = TL[:, 5 + h, :], TL[:, 9 + h, :], TL[:, h, :]
                b4 = bt.rearrange("p (c t) -> p c t", c=4)
                e4 = REC_E[1].rearrange("p (c t) -> p c t", c=4)
                tt(e4, b4[:, :, P - 1:P].broadcast_to([P, 4, P]), b4, ALU.subtract, f"rec args {h}")
                dve.wait_ge(act_step, at(f"rec el {h}"))
                tt(REC_QX, q, REC_E[0], ALU.mult)
                tt(REC_KX, k, REC_E[1], ALU.mult)
                end = [REC_E[0][:, (c + 1) * P - 1:(c + 1) * P] for c in range(4)]
                ts(REC_QS[:, 0:P], REC_QX[:, 2 * P:3 * P], end[1], None, ALU.mult)
                ts(REC_QS[:, P:2 * P], REC_QX[:, 3 * P:4 * P], end[2], None, ALU.mult)
                ts(REC_QS[:, 2 * P:3 * P], REC_QS[:, P:2 * P], end[1], None, ALU.mult, name=f"rec cross {h}")
                step(dve.memset(REC_AT, 0.0))
                lev = con("level").rearrange("p (l t) -> p l t", l=LEVELS + 1)

                def take_level(l):
                    m = turned[0]
                    turned[0] += 1
                    dve.wait_ge(turn_full, m + 1)
                    mask = lev[:, l:l + 1, :].bitcast(I32).broadcast_to([P, 4, P])
                    step(dve.copy_predicated(REC_AT.rearrange("p (c t) -> p c t", c=4), mask,
                                             U[m % 2][:, :].rearrange("p (c t) -> p c t", c=4)),
                         f"rec weights {h}" if l == LEVELS else None, turn_done)

                def args(l):
                    m = 1 << l
                    bv = bt.rearrange("p (n t) -> p n t", t=2 * m)
                    ev = REC_E[l % 2].rearrange("p (n t) -> p n t", t=2 * m)
                    ref = bv[:, :, m - 1:m].broadcast_to([P, T // (2 * m), m])
                    tt(ev[:, :, 0:m], ref, bv[:, :, 0:m], ALU.subtract)
                    tt(ev[:, :, m:], bv[:, :, m:], ref, ALU.subtract, f"rec args {h} {l}")

                args(0)
                take_level(0)
                take_turn(None, REC_X[:, 0:4 * P])
                take_turn(None, REC_X[:, 4 * P:6 * P], cols=2 * P)
                for l in range(LEVELS):
                    m = 1 << l
                    if l + 1 < LEVELS:
                        args(l + 1)
                    dve.wait_ge(act_step, at(f"rec e {h} {l}"))
                    ev = REC_E[l % 2].rearrange("p (n t) -> p n t", t=2 * m)
                    ov = REC_QK[l % 2].rearrange("p (n t) -> p n t", t=2 * m)
                    kv_, qv = k.rearrange("p (n t) -> p n t", t=2 * m), q.rearrange("p (n t) -> p n t", t=2 * m)
                    tt(ov[:, :, 0:m], kv_[:, :, 0:m], ev[:, :, 0:m], ALU.mult)
                    tt(ov[:, :, m:], qv[:, :, m:], ev[:, :, m:], ALU.mult, f"rec scaled {h} {l}")
                    if l >= 1:
                        take_level(l)
                take_level(LEVELS)
                dve.wait_ge(sum_full, at(f"full rec o {h}"))
                step(dve.tensor_copy(REC_O[:, :, h * P:(h + 1) * P], O[0][:, :].rearrange("p (c t) -> p c t", c=4)),
                     None, sum_done)
            o16 = part(wide, 2560, 2048, k=16)
            tt(w0, part(wide, 2560, 2048), part(wide, 2560, 2048), ALU.mult)
            r16 = stat[:, 32:48]
            step(dve.tensor_reduce(r16, w0.rearrange("p (k t) -> p k t", k=16), AX.X, ALU.add))
            small_rstd("rec", r16, 128)
            tt(o16, o16, r16.unsqueeze(2).broadcast_to([P, 16, P]), ALU.mult, "rec normed")
            for n in range(NT):
                m = turned[0]
                turned[0] += 1
                dve.wait_ge(turn_full, m + 1)
                stt(TL[:, 9:13, n * P:(n + 1) * P], U[m % 2][:, :].rearrange("p (j t) -> p j t", j=4), sm("g_ob")[:, 0:1],
                    TL[:, 18:22, n * P:(n + 1) * P], ALU.mult, ALU.mult, f"rec oT {n}", turn_done)

            for name, v, wd, c0 in (("cq", CQ, 384, 48), ("ckv", CKV, 256, 52)):
                sq = part(work, 2560, 4 * wd, k=NT)
                tt(sq, v, v, ALU.mult)
                step(dve.tensor_reduce(stat[:, c0:c0 + 4], sq, AX.X, ALU.add))
                small_rstd(name, stat[:, c0:c0 + 4], wd)
                for n in range(NT):
                    ts(v[:, n, :], v[:, n, :], stat[:, c0 + n:c0 + n + 1], None, ALU.mult,
                       name="latents normed" if (name, n) == ("ckv", NT - 1) else None)
            for j in range(3):
                take_turn(None, CQT[:, j, :], scalar=sm("g_cq")[:, j:j + 1])
            for j in range(2):
                take_turn("ckvT" if j else None, CKVT[:, j, :], scalar=sm("g_ckv")[:, j:j + 1])
            pf, ang, kk = stat[:, 56:60], trig[:, 0:P], trig[:, P:2 * P]
            step(dve.tensor_copy(pf, pcol[:, :]))
            for n in range(NT):
                ts(ang[:, n * 32:(n + 1) * 32], con("invf"), pf[:, n:n + 1], None, ALU.mult)
            ts(kk, ang, 1.0 / TWO_PI, ROUND, ALU.mult, ALU.add)
            ts(kk, kk, ROUND, None, ALU.subtract)
            for c_ in PI_PARTS:
                stt(ang, kk, -c_, ang, ALU.mult, ALU.add)
            ts(ang, ang, PI_IN, -PI_IN, ALU.min, ALU.max, name="angles")
            dve.wait_ge(act_step, at("trig"))
            cos1, sin1 = part(trig, 0, P, k=NT), part(trig, P, P, k=NT)

            def rope(x1, x2, c_, s_, a, b, o1=None, o2=None, name=None):
                o1, o2 = x1 if o1 is None else o1, x2 if o2 is None else o2
                tt(a, x1, s_, ALU.mult)
                tt(b, x2, s_, ALU.mult)
                tt(o1, x1, c_, ALU.mult)
                tt(o1, o1, b, ALU.subtract)
                tt(o2, x2, c_, ALU.mult)
                tt(o2, o2, a, ALU.add, name)

            dve.wait_ge(gemm_done, at("have qpe"))
            ta, tb = part(wide, 512, 128), part(wide, 640, 128)
            a3, b3 = ta.rearrange("p (n t) -> p n t", n=4), tb.rearrange("p (n t) -> p n t", n=4)
            rope(ROW[:, :, 136:168], ROW[:, :, 168:200], cos1, sin1, a3, b3, KPE2[:, :, 0:32], KPE2[:, :, 32:64])
            step(dve.tensor_copy(KPE2[:, :, 64:128], KPE2[:, :, 0:64]))
            for n in range(NT):
                qv = QPE[:, n, :].rearrange("p (h t) -> p h t", h=4)
                cb, sb_ = [v[:, n:n + 1, :].broadcast_to([P, 4, 32]) for v in (cos1, sin1)]
                rope(qv[:, :, 0:32], qv[:, :, 32:64], cb, sb_, a3, b3, name="roped" if n == NT - 1 else None)
            take_turn(None, KPET)
            for j in range(2):
                take_turn("qpeT" if j else None, QPET[:, j, :])
            attention_max("mla", 4, probs_over_sums("mla", lambda n: work[:, 0:T], 4), o_to_tiles("mla", 5))

            inc, rest = stat[:, 64:80], stat[:, 80:96]
            tt(inc, sm("rel"), sm("rel_before"), ALU.subtract)
            for z in range(3):
                step(dve.tensor_copy(REL[z], inc), "increments" if z == 2 else None)
                step(dve.tensor_copy(rest, REL[z]))
                tt(inc, inc, rest, ALU.subtract)
            ts(KEYSTEP, pkey[:, :], con("least"), None, ALU.add)
            for c_, (key, queries) in enumerate(BIAS_PARTS):
                t0, t1 = queries[0] * P, (queries[-1] + 1) * P
                for g in range(32):
                    if g >= 8:
                        dve.wait_ge(steps_used, at(f"bias {c_} {g - 8}"))
                    ts(STEPS(g, t1 - t0), prow[:, t0:t1], KEYSTEP[:, 32 * key + g:32 * key + g + 1], None, ALU.is_ge,
                       name=f"steps {c_} {g}")
                for n in queries:
                    m = turned[0]
                    turned[0] += 1
                    dve.wait_ge(turn_full, m + 1)
                    lo = upto(n) + key * P
                    step(dve.tensor_tensor(BIAS[:, :, lo:lo + P], U[m % 2][:, :].rearrange("p (s h) -> p h s", h=4),
                                           chosen[:, lo:lo + P].unsqueeze(1).broadcast_to([P, 4, P]), ALU.add), None, turn_done)

            def biased(i, n, h, src):
                out = LOGITS[i % 2][:, 0:(n + 1) * P]
                tt(out, src, BIAS[:, h, upto(n):upto(n + 1)], ALU.add)
                return out

            attention_max("dsa", 4, probs_over_sums("dsa", lambda n: work[:, 0:T], 4), o_to_tiles("dsa", 13), biased)
            step(dve.memset(stat[:, 60:61], 0.0), "dsa done")

            for j in range(8):
                m0, m1 = part(work, 0, T), part(work, T, T)
                for b_ in range(3):
                    dve.wait_ge(gemm_done, at(f"gate {j} {b_}"))
                    m = turned[0]
                    turned[0] += 1
                    dve.wait_ge(turn_full, m + 1)
                    stt(m1 if b_ else m0, GATE[b_], 1.0, U[m % 2][:, :], ALU.add, ALU.mult, None, turn_done)
                    if b_ == 1:
                        tt(m0, m0, m1, ALU.add)
                    if b_ == 2:
                        tt(TL[:, MIX[j], :], m0, m1, ALU.add, f"mixed {j}")
            step(dve.memset(stat[:, 60:61], 0.0), "mixed")

            def add_to_x(scalar):
                for j in range(8):
                    m = turned[0]
                    turned[0] += 1
                    dve.wait_ge(turn_full, m + 1)
                    stt(X[:, j, :], U[m % 2][:, :], scalar(j), X[:, j, :], ALU.mult, ALU.add, None, turn_done)

            dve.wait_ge(act_step, at("tanh c"))
            stt(SILU_C, SILU_C, 1.0, sm("c2"), ALU.add, ALU.mult)
            ts(GLUB, sm("glu_b"), 0.5, None, ALU.mult)
            ts(SILU_C, SILU_C, 0.5, None, ALU.mult, name="silu c")
            add_to_x(lambda j: 0.5)
            squares("ffn")
            for j in range(2):
                split(f"ff_{j}", chunk(f"ff_{j}"), FF_HEAD[j], chunk(f"ff_{j}", ring_r))
            rms_scale("ffn", lambda k: sm("g_ffn")[:, k:k + 1], H, heads=H_HEAD)
            for j in range(NFF):
                a, hb = part(work, j % 2 * T, T), part(work, (2 + j % 2) * T, T)
                dve.wait_ge(gemm_done, at(f"ff gate {j}"))
                stt(a, a, 1.0, hb, ALU.add, ALU.mult)
                m = turned[0]
                turned[0] += 1
                dve.wait_ge(turn_full, m + 1)
                step(dve.tensor_tensor(TL[:, j, :], a, U[m % 2][:, :], ALU.mult), f"ff {j}", turn_done)
                if j == NFF - 1:
                    tally.named["ff hidden"] = tally.named[f"ff {j}"]
                if j + 2 < NFF:
                    split(f"ff_{j + 2}", chunk(f"ff_{j + 2}"), FF_HEAD[j % 2], chunk(f"ff_{j + 2}", ring_r))
            add_to_x(lambda j: 1.0)
            squares("final")
            rms_scale("final", lambda k: sm("g_final")[:, k:k + 1], X)
            squares("block2")
            m = turned[0]
            turned[0] += 1
            dve.wait_ge(turn_full, m + 1)
            step(dve.tensor_tensor(MOD, U[m % 2][:, 0:24], sm("b_ada"), ALU.add), None, turn_done)
            stt(GAIN2, MOD[:, 8:16], 1.0, sm("g_2"), ALU.add, ALU.mult)
            rms_scale("block2", lambda k: GAIN2[:, k:k + 1], H, shift=lambda k: MOD[:, k:k + 1])
            c = SC
            dve.wait_ge(act_step, at("dt"))
            tt(c["t"], sm("a_im"), c["dt"], ALU.mult)
            ts(c["t"], c["t"], 1.0 / TWO_PI, None, ALU.mult)
            ts(c["u"], c["t"], ROUND, None, ALU.add)
            ts(c["u"], c["u"], ROUND, None, ALU.subtract)
            tt(c["turn"], c["t"], c["u"], ALU.subtract)
            ts(c["u"], c["turn"], 384.0, None, ALU.add)
            ts(c["hi"], c["u"], 384.0, None, ALU.subtract)
            tt(c["lo"], c["turn"], c["hi"], ALU.subtract)
            tt(c["rho"], sm("a_re"), c["dt"], ALU.mult, "ssm turn")
            dve.wait_ge(act_step, at("ssm trig"))
            ts(c["t"], c["rho"], 1.0, None, ALU.subtract)
            tt(c["x"], c["t"], c["c"], ALU.mult)
            tt(c["u"], c["h"], c["h"], ALU.mult)
            stt(c["x"], c["u"], -2.0, c["x"], ALU.mult, ALU.add)
            tt(c["y"], c["rho"], c["s"], ALU.mult)
            tt(c["t"], sm("a_re"), sm("a_re"), ALU.mult)
            tt(c["u"], sm("a_im"), sm("a_im"), ALU.mult)
            tt(c["den"], c["t"], c["u"], ALU.add)
            step(dve.reciprocal(c["den"], c["den"]))
            tt(c["t"], c["x"], sm("a_re"), ALU.mult)
            tt(c["u"], c["y"], sm("a_im"), ALU.mult)
            tt(c["t"], c["t"], c["u"], ALU.add)
            tt(c["kr"], c["t"], c["den"], ALU.mult)
            tt(c["t"], c["y"], sm("a_re"), ALU.mult)
            tt(c["u"], c["x"], sm("a_im"), ALU.mult)
            tt(c["t"], c["t"], c["u"], ALU.subtract)
            tt(c["ki"], c["t"], c["den"], ALU.mult)
            dve.wait_ge(ssm_in, 16)
            kr_, ki_ = [c[n].unsqueeze(2).broadcast_to([P, 16, 32]) for n in ("kr", "ki")]
            t1, t2 = [SSM(n).rearrange("p (k t) -> p k t", k=16) for n in ("t1", "t2")]
            tt(t1, CC[1], ki_, ALU.mult)
            tt(t2, CC[0], ki_, ALU.mult)
            tt(CC[0], CC[0], kr_, ALU.mult)
            tt(CC[0], CC[0], t1, ALU.subtract)
            tt(CC[1], CC[1], kr_, ALU.mult)
            tt(CC[1], CC[1], t2, ALU.add)
            ts(CC[1], CC[1], -1.0, None, ALU.mult)

            def phases(j):
                hi, lo = c["hi"][:, j:j + 1], c["lo"][:, j:j + 1]
                r, t1, t2 = SSM("turns"), SSM("t1"), SSM("t2")
                ts(t1, con("time"), hi, None, ALU.mult)
                ts(t2, t1, ROUND, None, ALU.add)
                ts(t2, t2, ROUND, None, ALU.subtract)
                tt(t1, t1, t2, ALU.subtract)
                stt(t1, con("time"), lo, t1, ALU.mult, ALU.add)
                ts(r, t1, 0.5, -0.5, ALU.min, ALU.max, name=f"phases {j}")

            def drain_y(ct):
                dve.wait_ge(sum_full, at(f"full y {4 * ct + 3}"))
                stt(TL[:, 2 + ct, :], TL[:, 2 + ct, :], sm("ssm_d")[:, ct:ct + 1], O[0][:, :], ALU.mult, ALU.add,
                    f"y {ct}", sum_done)

            phases(0)
            for j in range(16):
                s_, c_ = SSM("sin", j), SSM("cos", j)
                dve.wait_ge(act_step, at(f"waves {j}"))
                if j + 1 < 16:
                    phases(j + 1)
                dve.wait_ge(gemm_done, at(f"bu {j}"))
                t1, t2, wr, wi, br, bi_, sr, si = [SSM(n, j) for n in ("t1", "t2", "wr", "wi", "br", "bi", "sr", "si")]
                tt(wr, br, c_, ALU.mult)
                tt(t1, bi_, s_, ALU.mult)
                tt(wr, wr, t1, ALU.add)
                tt(t2, br, s_, ALU.mult)
                tt(wi, bi_, c_, ALU.mult)
                tt(wi, wi, t2, ALU.subtract)
                rho = c["rho"][:, j:j + 1].broadcast_to([P, T])
                step(dve.tensor_tensor_scan(br, rho, wr, 0.0, ALU.mult, ALU.add))
                step(dve.tensor_tensor_scan(bi_, rho, wi, 0.0, ALU.mult, ALU.add))
                if j >= 2:
                    dve.wait_ge(sum_full, at(f"full y {j - 2}"))
                tt(sr, br, c_, ALU.mult)
                tt(t1, bi_, s_, ALU.mult)
                tt(sr, sr, t1, ALU.subtract)
                tt(si, br, s_, ALU.mult)
                tt(t2, bi_, c_, ALU.mult)
                tt(si, si, t2, ALU.add, f"states {j}")
                if j % 4 == 0 and j:
                    drain_y(j // 4 - 1)
            drain_y(3)
            dve.wait_ge(act_step, at("tanh zs"))
            zs4 = tiles[:, 10 * T:14 * T]
            stt(zs4, part(work, 0, 4 * T), 1.0, zs4, ALU.add, ALU.mult)
            tt(zs4, zs4, tiles[:, 2 * T:6 * T], ALU.mult)
            for j in range(4):
                dve.wait_ge(gemm_done, at(f"glu {j}"))
                stt(TL[:, 10 + j, :], part(work, (4 + j) * T, T), 1.0, TL[:, 10 + j, :], ALU.add, ALU.mult,
                    "ssm out" if j == 3 else None)
            dve.wait_ge(gemm_done, at("have zs"))
            step(dve.memset(CB, 0.0))
            for i, kv in enumerate("kv"):
                if i:
                    dve.wait_ge(gemm_done, at("hidden k"))
                pos = sm(f"pos_{kv}")
                for g in range(2):
                    r = slice(64 * g, 64 * g + 64)
                    src = TL[r, i, :].rearrange("p (n l) -> p l n", l=16)
                    for hf in range(2):
                        tt(CB[r, 16 * hf:16 * hf + 16, g * NCMP:(g + 1) * NCMP], src[:, :, hf:hf + NCMP],
                           pos[r, 16 * hf:16 * hf + 16].unsqueeze(2).broadcast_to([64, 16, NCMP]), ALU.add,
                           f"blocks {kv}" if g and hf else None)
            for kv in "kv":
                take_turn(f"hidden T {kv}", HID(kv)[:, :, 0:2 * NCMP], cols=P, view=lambda v: v.rearrange("p (k t) -> p k t", k=2)[:, :, 0:2 * NCMP])
            dve.wait_ge(gemm_done, at("have vcmp"))
            kr = KCRAW[0:NCMP, :].rearrange("p (g t) -> p g t", g=2)
            kq = part(work, T, P)[0:NCMP].rearrange("p (g t) -> p g t", g=2)
            tt(kq, kr, kr, ALU.mult)
            step(dve.memset(stat[:, 32:34], 1.0))
            step(dve.tensor_reduce(stat[0:NCMP, 32:34], kq, AX.X, ALU.add))
            small_rstd("kc", stat[:, 32:34], 64)
            tt(kr, kr, stat[0:NCMP, 32:34].unsqueeze(2).broadcast_to([NCMP, 2, 64]), ALU.mult)
            for d in range(2):
                tt(KC2[0:NCMP, :, 64 * d:64 * d + 64], kr,
                   sm("g_kc")[0:NCMP, :].unsqueeze(1).broadcast_to([NCMP, 2, 64]), ALU.mult, "kc normed" if d else None)
            take_turn("kcT", KCT.rearrange("p (g t) -> p g t", g=2)[:, :, 0:NCMP], cols=64,
                      view=lambda v: v.rearrange("p (g t) -> p g t", g=2)[:, :, 0:NCMP])
            dve.wait_ge(gemm_done, at("have rows2"))
            ts(stat[:, 64:128], sm("g_q"), 0.125, None, ALU.mult)
            for name, c0, heads, gain, c1 in (("q", 0, 8, stat[:, 64:128], 128), ("ksl", 512, 2, sm("g_ks"), 160), ("kwn", 768, 2, sm("g_kw"), 168)):
                sq = part(work, 0, NT * heads * 64, k=NT)
                v = R2[:, :, c0:c0 + heads * 64]
                tt(sq, v, v, ALU.mult)
                r = stat[:, c1:c1 + NT * heads]
                step(dve.tensor_reduce(r, sq.rearrange("p n (h d) -> p n h d", h=heads), AX.X, ALU.add))
                small_rstd(name, r, 64)
                for n in range(NT):
                    vn = v[:, n, :].rearrange("p (h d) -> p h d", h=heads)
                    tt(vn, vn, r[:, n * heads:(n + 1) * heads].unsqueeze(2).broadcast_to([P, heads, 64]), ALU.mult)
                    tt(vn, vn, gain.unsqueeze(1).broadcast_to([P, heads, 64]), ALU.mult,
                       "q normed" if (name, n) == ("q", NT - 1) else None)
            for j in range(4):
                take_turn(None, TL[:, 14 + j, :])
            cos2, sin2 = con("cos2").rearrange("p (n t) -> p n t", n=NT), con("sin2").rearrange("p (n t) -> p n t", n=NT)
            ta, tb = [part(wide, 4200 + 256 * z, 256, k=8) for z in range(2)]
            for n in range(NT):
                qv = R2[:, n, 0:512].rearrange("p (h t) -> p h t", h=8)
                cb, sb_ = [v[:, n:n + 1, :].broadcast_to([P, 8, 32]) for v in (cos2, sin2)]
                rope(qv[:, :, 0:32], qv[:, :, 32:64], cb, sb_, ta, tb, name="q roped" if n == NT - 1 else None)
            for j in range(4):
                take_turn(None, TL[:, 18 + j, :])
            for a_, c0 in enumerate((512, 768)):
                for g in range(2):
                    x1, x2 = [R2[:, :, c0 + 64 * g + 32 * z:c0 + 64 * g + 32 * z + 32] for z in range(2)]
                    k2 = K2(2 * a_ + g)
                    aa, bb = [part(wide, 4200 + 256 * z, 128, k=4) for z in range(2)]
                    rope(x1, x2, cos2, sin2, aa, bb, k2[:, :, 0:32], k2[:, :, 32:64])
                    step(dve.tensor_copy(k2[:, :, 64:128], k2[:, :, 0:64]), "k roped" if (a_, g) == (1, 1) else None)
            for i in range(4):
                take_turn("kT 3" if i == 3 else None, KT2[:, i, :])
            for z in range(3):
                step(dve.tensor_copy(GB[z], R2[:, :, 1024 + z:1048:3]), "branch logits" if z == 2 else None)
            dve.wait_ge(act_step, at("branch gates"))
            for z in range(3):
                ts(GB[z], GB[z], 0.5, 0.5, ALU.mult, ALU.add)
            cn = con("cmp_neg").rearrange("p (n t) -> p n t", n=NT)
            ck = con("cmp_ok").rearrange("p (n t) -> p n t", n=NT)
            for i in range(8):
                n, e = divmod(i, 2)
                s3 = CMP_P.rearrange("p (h t) -> p h t", h=4)
                m4 = stat[:, 8:12]
                dve.wait_ge(score_done, at(f"cmp score {i}"))
                tt(s3, s3, cn[:, n:n + 1, :].broadcast_to([P, 4, NCMP]), ALU.add)
                step(dve.tensor_reduce(m4, s3, AX.X, ALU.max))
                tt(s3, s3, m4.unsqueeze(2).broadcast_to([P, 4, NCMP]), ALU.subtract, f"cmp less max {i}")
                dve.wait_ge(act_step, at(f"cmp exp {i}"))
                tt(s3, s3, ck[:, n:n + 1, :].broadcast_to([P, 4, NCMP]), ALU.mult, f"cmp probs {i}")
                rs = stat[:, 16:24].rearrange("p (q e) -> p q e", e=2)[:, :, e:e + 1]
                step(dve.tensor_reduce(rs, s3, AX.X, ALU.add))
                if i:
                    dve.wait_ge(sum_full, at(f"cmp summed {i - 1}"))
                take_turn(f"cmp probsT {i}", probsT[0:NCMP, 0:T], rows_=NCMP)
                if e == 1:
                    r8 = stat[:, 16:24]
                    ts(r8, r8, 1e-30, None, ALU.max)
                    step(dve.reciprocal(r8, r8))
                    tt(r8, r8, GB[0][:, n, :], ALU.mult)
                    dve.wait_ge(sum_full, at(f"cmp summed {i}"))
                    step(dve.tensor_tensor(ATT[:, n, :].rearrange("p (h d) -> p h d", h=8),
                                           O[0][:, :].rearrange("p (h d) -> p h d", h=8),
                                           r8.unsqueeze(2).broadcast_to([P, 8, 64]), ALU.mult), None, sum_done)
            for z, name in ((1, "slc"), (2, "win")):
                attention_max(name, 8, probs_over_sums(name, lambda n: ATT[:, n, :], 8, gate=lambda n: GB[z][:, n, :]))
            step(dve.memset(stat[:, 60:61], 0.0), "gates free")
            dve.wait_ge(act_step, at("tanh za"))
            za4 = tiles[:, 6 * T:10 * T]
            stt(za4, part(wide, 6 * T, 4 * T), 1.0, za4, ALU.add, ALU.mult)
            for n in range(NT):
                m = turned[0]
                turned[0] += 1
                dve.wait_ge(turn_full, m + 1)
                v = TL[:, 6:10, n * P:(n + 1) * P]
                step(dve.tensor_tensor(v, U[m % 2][:, :].rearrange("p (j t) -> p j t", j=4), v, ALU.mult),
                     f"attn T {n}", turn_done)

            add_to_x(lambda j: MOD[:, 16 + j:17 + j])
            step(dve.memset(stat[:, 60:61], 0.0), "out ready")

        @block.gpsimd
        def _(pool):

            def step(ins, name=None):
                n = up(pool_step, name)
                ins.then_inc(pool_step, 1)
                pool.wait_ge(pool_step, n)

            pool.wait_ge(const_in, 16)
            half = con("misc")[:, 0:1]
            for name, c0, n in (("rec", 32, 16), ("cq", 48, 4), ("ckv", 52, 4), ("kc", 32, 2), ("q", 128, 32),
                                ("ksl", 160, 8), ("kwn", 168, 8)):
                v = stat[:, c0:c0 + n]
                pool.wait_ge(dve_step, at(f"mean {name}"))
                step(pool.tensor_tensor(v, v, half.broadcast_to([P, n]), ALU.pow), f"rstd {name}")
    return tally.named


def declare(nc):
    def din(name, shape, dt=F32):
        return nc.dram_tensor(name, shape, dt, kind="ExternalInput").ap()

    return [din("wstream", (len(plan()), P, CHUNK)), din("ssm", (P, 4 * T)), din("xT", (P, KD * T)), din("consts", (P, sum(CONST.values()))),
            din("small", (P, sum(SMALL.values()))), din("pos_row", (P, T), I32), din("pos_col", (P, NT), I32),
            din("pos_key", (P, P), I32),
            nc.dram_tensor("outT", (P, KD * T), F32, kind="ExternalOutput").ap()]


def kernel(**inputs):
    import concourse.bacc as _bacc
    from concourse.bass_utils import run_bass_kernel_spmd as _run

    a = {n: np.asarray(v) for n, v in inputs.items()}
    xT = a["x"][0].T.reshape(KD, P, T).transpose(1, 0, 2).reshape(P, -1)
    pos = a["positions"][0].astype(np.int32)
    c, s = constants(), small_inputs(a)
    arrays = {
        "wstream": weight_stream(a), "ssm": state_space_matrices(a), "xT": np.ascontiguousarray(xT),
        "consts": np.ascontiguousarray(np.concatenate([c[n] for n in CONST], 1)),
        "small": np.ascontiguousarray(np.concatenate([s[n] for n in SMALL], 1)),
        "pos_row": np.ascontiguousarray(np.broadcast_to(pos, (P, T))),
        "pos_col": np.ascontiguousarray(pos.reshape(NT, P).T),
        "pos_key": np.ascontiguousarray(np.repeat(pos.reshape(P, 4).T, 32, axis=0)),
    }
    trial = _bacc.Bacc("TRN2", target_bir_lowering=False, num_devices=1)
    known = two_blocks_kernel(trial, *declare(trial), None)
    nc = _bacc.Bacc("TRN2", target_bir_lowering=False, num_devices=1)
    two_blocks_kernel(nc, *declare(nc), known)
    r = _run(nc, [arrays], core_ids=[0])
    out = r.results[0]["outT"]
    return np.ascontiguousarray(out.reshape(P, KD, T).transpose(2, 1, 0).reshape(1, T, D))
```

```python
import itertools
import math

import numpy as np

from concourse import mybir

F32 = mybir.dt.float32
I32 = mybir.dt.int32
BF16 = mybir.dt.bfloat16
F32R = mybir.dt.float32r
ALU = mybir.AluOpType
ACT = mybir.ActivationFunctionType
AX = mybir.AxisListType

P = 128
T = 512
NT = T // P
D = 1024
KD = D // P
NEG = -1e30
TAKEN = -3e38
EPS = 1e-6
CHUNK = 3072
SLOTS = 4
FF = 2816
NFF = FF // P
TOPK = min(256, T // 4)
NCMP = (T - 32) // 16 + 1
LEVELS = 7
TWO_PI = 2.0 * math.pi
ROUND = 1.5 * 2.0 ** 23
TWO_PI_IN = 6.283184
PI_IN = 3.141592
PI_PARTS = (6.28125, 0.00193500518798828125, 3.019915981956753e-07)
LOG_FLOOR = math.log(1e-30)
MLA_SCALE = 192 ** -0.5
TURN_CHUNKS = ("up_", "ff_", "dow", "wou")


def bucket_steps():
    d = np.arange(0, 2048)
    dl = np.maximum(d, 16).astype(np.float32)
    large = 16 + (np.log(dl / np.float32(16)) / np.float32(math.log(8)) * np.float32(16)).astype(np.int32)
    b = np.where(d < 16, d, np.minimum(large, 31))
    return [int(np.argmax(b >= n)) for n in range(1, 32)]


def constants():
    p = np.arange(P)[:, None]
    c = {}
    c["ident"] = (p == np.arange(P)).astype(np.float32)
    c["ones"] = np.ones((P, P), np.float32)
    c["causal"] = np.where(np.arange(P) <= p, 0.0, NEG).astype(np.float32)
    s, t = p, np.arange(P)[None]
    lev = [(s == t)]
    for l in range(LEVELS):
        m = 1 << l
        lev.append((s // (2 * m) == t // (2 * m)) & (s % (2 * m) < m) & (t % (2 * m) >= m))
    c["level"] = np.stack(lev, 1).astype(np.float32).reshape(P, -1)
    c["reset"] = np.broadcast_to((np.arange(T) % P != 0).astype(np.float32), (P, T))
    c["time"] = np.broadcast_to(np.arange(T, dtype=np.float32), (P, T))
    c["invf"] = np.broadcast_to((np.float32(10000.0) ** (-np.arange(0, 64, 2, dtype=np.float32) / np.float32(64))).astype(np.float32), (P, 32))
    inv = (1.0 / (np.float32(10000.0) ** (np.arange(0, 64, 2, dtype=np.float32) / np.float32(64)))).astype(np.float32)
    ang = np.arange(T, dtype=np.float32)[:, None] * inv[None]
    c["cos2"] = np.cos(ang).astype(np.float32).reshape(NT, P, 32).transpose(1, 0, 2).reshape(P, -1)
    c["sin2"] = np.sin(ang).astype(np.float32).reshape(NT, P, 32).transpose(1, 0, 2).reshape(P, -1)
    tt = np.arange(T).reshape(NT, P).T[:, :, None]
    ok = (np.arange(NCMP) * 16 + 31)[None, None] <= tt
    c["cmp_neg"] = np.where(ok, 0.0, NEG).astype(np.float32).reshape(P, -1)
    c["cmp_ok"] = ok.astype(np.float32).reshape(P, -1)
    c["least"] = np.tile(np.array([-2.0 ** 30] + bucket_steps(), np.float32), 4)[:, None]
    c["misc"] = np.tile(np.array([-0.5, EPS, math.pi / 2, -LOG_FLOOR], np.float32), (P, 1))
    return c


def tiles_of(w, cols):
    w = w[:, cols]
    return w.reshape(w.shape[0] // P, P, w.shape[1]).transpose(1, 0, 2).reshape(P, -1)


SPLITS = [512, 128, 128, 512, 64, 8, 512, 512, 512, 512, 384, 256, 64, 3072]
NAMES = ["aq", "ak", "av", "iq", "ik", "iw", "bq", "bf", "bi", "bg", "cq", "ckv", "ckpe", "gate"]
AT1 = dict(zip(NAMES, np.cumsum([0] + SPLITS[:-1]).tolist()))
SPLITS2 = [512] + [128] * 6 + [512, 24, 512, 512]
NAMES2 = ["q", "kcr", "vcr", "ksl", "vsl", "kwn", "vwn", "za", "gbr", "u", "zs"]
AT2 = dict(zip(NAMES2, np.cumsum([0] + SPLITS2[:-1]).tolist()))

PROJ1 = [("iq", 0), ("iq", 1), ("iq", 2), ("iq", 3), ("ik", 0), ("bf", 0)]
PROJ1B = ([("bf", 1), ("bf", 2), ("bf", 3)] + [("bq", i) for i in range(4)] + [("bg", i) for i in range(4)])
PROJ1C = [("ak", 0)] + [("aq", i) for i in range(4)]
PROJ2 = [("u", i) for i in range(4)] + [("kcr", 0), ("vcr", 0)] + [("za", i) for i in range(4)] + [("zs", i) for i in range(4)]


def columns(name, i, at):
    if name == "ik":
        one = np.arange(at["ik"], at["ik"] + 64)
        return np.concatenate([one, one])
    return np.arange(at[name] + P * i, at[name] + P * (i + 1))


def by_threes(tiles):
    return [tiles[i:i + 3] for i in range(0, len(tiles), 3)]


def span(at, *parts):
    return np.concatenate([np.arange(at[n] + a, at[n] + b) for n, a, b in parts])


ROWS1 = [("av", [("av", 0, 128), ("iw", 0, 8), ("ckpe", 0, 64)])]
ROWS1B = [("bi0", [("bi", 0, 384)]), ("bi1", [("bi", 384, 512), ("ckv", 0, 256)]), ("cq", [("cq", 0, 384)])]
ROWS2 = [("q0", [("q", 0, 384)]), ("q1", [("q", 384, 512), ("ksl", 0, 128), ("vsl", 0, 128)]),
         ("w", [("kwn", 0, 128), ("vwn", 0, 128), ("gbr", 0, 24)])]


def plan():
    out = [(f"proj1_{i}", len(c) * KD * P) for i, c in enumerate(by_threes(PROJ1))]
    out += [("rows1_av", KD * 200)]
    out += [(f"proj1b_{i}", len(c) * KD * P) for i, c in enumerate(by_threes(PROJ1B))]
    out += [(f"rows1_{n}", KD * 384) for n in ("bi0", "bi1")]
    out += [(f"proj1c_{i}", len(c) * KD * P) for i, c in enumerate(by_threes(PROJ1C))]
    out += [("rows1_cq", KD * 384)]
    out += [("qb", 3 * 768), ("kvb", 2 * 1024)]
    out += [(f"ada_{i}", 3 * KD * P) for i in range(8)]
    for j in range(8):
        out.append((f"gate_{j}", 3 * KD * P))
        if j % 2 == 0:
            out.append((f"up_{j // 2}", 2 * 3 * 4 * P))
    out += [(f"wout_{i}", len(c) * KD * P) for i, c in enumerate(by_threes(range(8)))]
    out += [(f"ff_{j}", 2 * KD * P) for j in range(NFF)]
    out += [(f"down_{j}", NFF * P) for j in range(8)]
    out += [(f"proj2_{i}", len(c) * KD * P) for i, c in enumerate(by_threes(PROJ2))]
    out += [(f"rows2_{n}", KD * sum(b - a for _, a, b in parts)) for n, parts in ROWS2]
    out += [("glu", 4 * 512)]
    out += [(f"cmp_{kv}{i}", 256 * n) for kv in "kv" for i, n in enumerate((12, 12, 8))]
    out += [(f"wout2_{i}", len(c) * KD * P) for i, c in enumerate(by_threes(range(8)))]
    return out


def weight_stream(a):
    out = np.zeros((len(plan()), P, CHUNK), np.float32)
    at = {n: i for i, (n, _) in enumerate(plan())}

    def put(name, block):
        out[at[name], :, :block.shape[1]] = block

    w = a["w_in"][0]
    for tag, tiles in (("proj1", PROJ1), ("proj1b", PROJ1B), ("proj1c", PROJ1C)):
        for i, c in enumerate(by_threes(tiles)):
            put(f"{tag}_{i}", np.concatenate([tiles_of(w, columns(n, k, AT1)) for n, k in c], 1))
    for n, parts in ROWS1 + ROWS1B:
        put(f"rows1_{n}", tiles_of(w, span(AT1, *parts)))
    h = np.arange(4)[:, None]
    put("qb", tiles_of(a["mla_w_qb"][0], np.concatenate([(h * 192 + np.arange(128)).ravel(), (h * 192 + 128 + np.arange(64)).ravel()])))
    put("kvb", tiles_of(a["mla_w_kvb"][0], np.concatenate([(h * 256 + np.arange(128)).ravel(), (h * 256 + 128 + np.arange(128)).ravel()])))
    for j in range(8):
        put(f"gate_{j}", np.concatenate([tiles_of(w, AT1["gate"] + D * b + P * j + np.arange(P)) for b in range(3)], 1))
        if j % 2 == 0:
            put(f"up_{j // 2}", np.concatenate([tiles_of(a[f"w_up_{b}"][0], P * (j + e) + np.arange(P)) for e in range(2) for b in "abc"], 1))
    for i, c in enumerate(by_threes(range(8))):
        put(f"wout_{i}", np.concatenate([tiles_of(a["w_out"][0], P * j + np.arange(P)) for j in c], 1))
        put(f"wout2_{i}", np.concatenate([tiles_of(a["w_out_2"][0], P * j + np.arange(P)) for j in c], 1))
    for j in range(NFF):
        put(f"ff_{j}", np.concatenate([tiles_of(a[n][0], P * j + np.arange(P)) for n in ("w_ffn_gate", "w_ffn_up")], 1))
    for j in range(8):
        put(f"down_{j}", tiles_of(a["w_ffn_down"][0], P * j + np.arange(P)))
        put(f"ada_{j}", np.concatenate([tiles_of(a["w_ada_2"][0], P * (3 * j + e) + np.arange(P)) for e in range(3)], 1))
    w2 = a["w_in_2"][0]
    for i, c in enumerate(by_threes(PROJ2)):
        put(f"proj2_{i}", np.concatenate([tiles_of(w2, columns(n, k, AT2)) for n, k in c], 1))
    for n, parts in ROWS2:
        put(f"rows2_{n}", tiles_of(w2, span(AT2, *parts)))
    for kv in "kv":
        m = a[f"cmp_w1_{kv}_2"][0].reshape(32, 64, 256).transpose(1, 0, 2).reshape(64, -1)
        m = np.concatenate([m, m], 0)
        for i, (lo, n) in enumerate(((0, 12), (12, 12), (24, 8))):
            put(f"cmp_{kv}{i}", m[:, lo * 256:(lo + n) * 256])
    put("glu", tiles_of(a["glu_w_2"][0], np.arange(512)))
    return out


def small_inputs(a):
    def col(v):
        return v.reshape(-1, P).T

    def row(v):
        return np.broadcast_to(v.reshape(1, -1), (P, v.size))

    c = {
        "g_attn": col(a["attn_norm"][0]), "g_ffn": col(a["ffn_norm"][0]), "g_final": col(a["final_norm"]),
        "g_cq": col(a["mla_q_norm"][0]), "g_ckv": col(a["mla_kv_norm"][0]), "g_ob": col(a["hgrn_out_norm"][0]),
        "g_2": col(a["norm_g_2"][0]), "b_ada": col(a["b_ada_2"][0]), "c2": col(a["c_2"][0]),
        "glu_b": col(a["glu_b_2"][0]), "ssm_d": col(a["ssm_d_2"][0]), 
        "g_q": row(a["q_norm_g_2"][0]), "g_kc": row(a["k_cmp_norm_g_2"][0]), "g_ks": row(a["k_slc_norm_g_2"][0]),
        "g_kw": row(a["k_win_norm_g_2"][0]),
    }
    for name, shift in (("rel", 0), ("rel_before", 1)):
        m = np.zeros((4, 32, 4, 4), np.float32)
        for j in range(4):
            m[j, shift:, j, :] = a["rel_bias"][0:32 - shift]
        c[name] = m.reshape(P, 16)
    for kv in "kv":
        pos = a[f"cmp_pos_{kv}_2"][0].T
        c[f"pos_{kv}"] = np.concatenate([pos, pos], 0)
        c[f"w2_{kv}"] = tiles_of(a[f"cmp_w2_{kv}_2"][0], np.arange(64))
    c["a_re"] = a["ssm_a_re_2"][0].reshape(16, P).T
    c["a_im"] = a["ssm_a_im_2"][0].reshape(16, P).T
    c["log_dt"] = np.repeat(a["ssm_log_dt_2"][0].reshape(16, 2), 64, axis=1).T
    return c


def state_space_matrices(a):
    parts = []
    for z in ("re", "im"):
        b = a[f"ssm_b_{z}_2"][0]
        m = np.zeros((P, 4, P), np.float32)
        for g in range(32):
            ct, r = divmod(g, 8)
            m[16 * r:16 * r + 16, ct, 64 * (g % 2):64 * (g % 2) + 64] = b[g].T
        parts.append(m.reshape(P, -1))
        cc = a[f"ssm_c_{z}_2"][0]
        m = np.zeros((P, 16, 32), np.float32)
        for g in range(32):
            m[64 * (g % 2):64 * (g % 2) + 64, g // 2, 16 * (g % 2):16 * (g % 2) + 16] = cc[g].T
        parts.append(m.reshape(P, -1))
    return np.concatenate(parts, 1)


SMALL = {"g_attn": 8, "g_ffn": 8, "g_final": 8, "g_cq": 3, "g_ckv": 2, "g_ob": 1, "g_2": 8, "b_ada": 24, "c2": 8,
         "glu_b": 4, "ssm_d": 4, "rel": 16, "rel_before": 16, "g_q": 64, "g_kc": 64, "g_ks": 64, "g_kw": 64, "pos_k": 32, "w2_k": 128,
         "pos_v": 32, "w2_v": 128, "a_re": 16, "a_im": 16, "log_dt": 16}
CONST = {"ident": P, "ones": P, "causal": P, "level": (LEVELS + 1) * P, "reset": T, "time": T, "invf": 32,
         "cos2": P, "sin2": P, "cmp_neg": NT * NCMP, "cmp_ok": NT * NCMP, "least": 1, "misc": 4}


def offsets(sizes):
    at, out = 0, {}
    for n, k in sizes.items():
        out[n] = (at, at + k)
        at += k
    return out, at


class Tally:

    def __init__(self, known):
        self.count, self.known, self.named = {}, known, {}

    def up(self, sem, name=None, by=1):
        n = self.count[sem.name] = self.count.get(sem.name, 0) + by
        if name is not None:
            assert name not in self.named, name
            self.named[name] = n
        return n

    def at(self, name):
        return self.known[name] if self.known is not None else 1


def two_blocks_kernel(nc, wstream, ssm, xT, consts, small, pos_row, pos_col, pos_key, outT, known):
    tally = Tally(known)
    up, at = tally.up, tally.at

    base = {}

    def sb(name, cols, dt=F32):
        base[name] = -(-nc.sbuf_base // 32) * 32
        return nc.alloc_sbuf_tensor(name, [P, cols], dt)

    def rounded(name, cols):
        return nc.alloc_sbuf_tensor_at(f"{name}_r", [P, cols], F32R, offset=base[name])

    ring = sb("ring", SLOTS * CHUNK)
    x_sb = sb("x_sb", KD * T)
    h_sb = sb("h_sb", KD * T)
    tiles = sb("tiles", 22 * T)
    rows = sb("rows", 24 * P)
    wide = sb("wide", 5760)
    work = sb("work", 4608)
    probs = sb("probs", 2 * T)
    probsT = sb("probsT", 2 * T)
    cst = sb("cst", sum(CONST.values()))
    sml = sb("sml", sum(SMALL.values()))
    chosen = sb("chosen", NT * (NT + 1) // 2 * P, BF16)
    prow = sb("prow", T, I32)
    pcol = sb("pcol", NT, I32)
    pkey = sb("pkey", P, I32)
    stat = sb("stat", 512)
    trig = sb("trig", 2 * NT * 32)

    ring_r, h_r, wide_r = rounded("ring", SLOTS * CHUNK), rounded("h_sb", KD * T), rounded("wide", 5760)
    rows_r, work_r, tiles_r = rounded("rows", 24 * P), rounded("work", 4608), rounded("tiles", 22 * T)
    X = x_sb[:, :].rearrange("p (k t) -> p k t", k=KD)
    H = h_sb[:, :].rearrange("p (k t) -> p k t", k=KD)
    TL = tiles[:, :].rearrange("p (k t) -> p k t", k=22)
    ROW = rows[:, 0:NT * 712].rearrange("p (n c) -> p n c", n=NT)
    coff, _ = offsets(CONST)
    soff, _ = offsets(SMALL)

    def con(name):
        a, b = coff[name]
        return cst[:, a:b]

    def sm(name):
        a, b = soff[name]
        return sml[:, a:b]

    ident, ones, causal = con("ident"), con("ones"), con("causal")
    G = [nc.alloc_psum_tensor(f"gemm{i}", [P, T], F32) for i in range(3)]
    S = [nc.alloc_psum_tensor(f"score{i}", [P, T], F32) for i in range(2)]
    U = [nc.alloc_psum_tensor(f"turn{i}", [P, T], F32) for i in range(2)]
    O = [nc.alloc_psum_tensor("sum0", [P, T], F32)]

    def part(t, a, n, **shape):
        v = t[:, a:a + n]
        return v.rearrange("p (k t) -> p k t", **shape) if shape else v

    REC_E = [part(work, 0, T), part(work, T, T)]
    REC_QK = [part(work, 2 * T, T), part(work, 3 * T, T)]
    REC_QX, REC_KX, REC_AT = part(work, 4 * T, T), part(work, 5 * T, T), part(work, 6 * T, T)
    REC_X = part(work, 7 * T, 6 * P)
    REC_O, REC_QS = part(wide, 2560, 4 * T, k=NT), part(wide, 4608, 3 * P)

    def REC_FAR(a, c):
        i = {(0, 1): 0, (1, 2): 1, (2, 3): 2, (0, 2): 3, (1, 3): 4, (0, 3): 5}[a, c]
        return REC_X[:, i * P:(i + 1) * P]

    CQ, CKV = part(wide, 0, 1536, k=NT), part(wide, 1536, 1024, k=NT)
    VC, QPE = part(wide, 2560, 2048, k=NT), part(wide, 4608, 1024, k=NT)
    KPE2 = part(wide, 0, 512, k=NT)
    CQT, CKVT = part(work, 0, 1536, k=3), part(work, 1536, 1024, k=2)
    QPET, KPET = part(work, 2560, 1024, k=2), part(work, 3584, T)
    BIAS = part(wide, 0, 5120, k=4)
    INDEX = [None] + [part(work, n * T, (n + 1) * P) for n in range(1, NT)]
    REL = [part(work, 6 * T + 8 * z, 8).bitcast(BF16) for z in range(3)]
    KEYSTEP = part(work, 6 * T + 64, P)

    def STEPS(g, cols):
        return part(work, 2 * T + g % 8 * P, P).bitcast(BF16)[:, 0:cols]

    BIAS_PARTS = [(0, (0, 1)), (0, (2, 3)), (1, (1, 2)), (1, (3,)), (2, (2, 3)), (3, (3,))]
    LOGITS = [part(work, 4 * T, T), part(work, 5 * T, T)]

    def upto(n):
        return n * (n + 1) // 2 * P

    H_HEAD = part(wide_r, 0, KD * T, k=KD)
    H_REST = h_r[:, :].rearrange("p (k t) -> p k t", k=KD)
    HEADS = [[part(rows_r, z * KD * P, KD * P) for z in range(3)],
             [part(wide_r, 8 * T, KD * P), part(work_r, 4 * T, KD * P), part(work_r, 2 * T, KD * P)]]
    HIDDEN_HEAD = [part(work_r, (6 + z) * T, T) for z in range(3)] + [part(wide_r, 10 * T, T)]
    HIDDEN_HEAD += [H_HEAD[:, k, :] for k in range(KD)] + [H_REST[:, k, :] for k in range(KD)]
    HIDDEN_HEAD += [part(work_r, z * T, T) for z in range(2)]
    TL_REST = tiles_r[:, :].rearrange("p (k t) -> p k t", k=22)
    SPLIT = [f"gate_{j}" for j in range(8)] + [f"wout_{i}" for i in range(3)] + [f"ff_{j}" for j in range(NFF)] + \
            [f"down_{j}" for j in range(8)]

    def head_of(name, q, n=1):
        return HEADS[(SPLIT.index(name) + 1) % 2][q // KD][:, q % KD * P:(q % KD + n) * P]

    def parts_of(name):
        cols = chunks[chunk_at[name]][1]
        return [(z, c, min(KD * P, cols - c)) for z, c in enumerate(range(0, cols, KD * P))]

    SIDE = [2, 1, 1] * 5 + [2]
    MODROW = [tiles[0:1, a_:a_ + 384] for a_ in [384 * i for i in range(6)] + [18 * T, 18 * T + 384]]
    MIX = [0, 1, 2, 3, 4, 18, 19, 20]
    GATE = [part(work, (6 + b) * T, T) for b in range(3)]
    SQUARES = [part(rows, k * T, T) for k in range(6)] + [H[:, 6, :], H[:, 7, :]]
    SILU_C, MOD, GAIN2, POSB = stat[:, 192:200], stat[:, 200:224], stat[:, 224:232], stat[:, 232:240]
    R2 = part(wide, 0, NT * 1048, k=NT)
    KT2 = part(rows, 0, 4 * T, k=4)

    def HID(kv):
        return part(rows, 2048 + 128 * (kv == "v"), P, k=2)

    def HROW(kv):
        return part(work, 8 * T + 256 * (kv == "v"), 256)

    CB = part(tiles, 2 * T, 32 * 2 * NCMP, k=32)
    KC2, VCMP, KCT = part(rows, 2304, 256, k=2), part(rows, 2560, 128), part(rows, 2688, 64)
    CMP_P = part(probs, 0, 4 * NCMP)
    ATT = part(work, 0, 4 * T, k=NT)

    def K2(i):
        return part(work, 4 * T + i * T, T, k=NT)

    GB = [part(wide, 4712 + 32 * z, 32, k=NT) for z in range(3)]
    KCRAW = part(work, 0, P)
    GLUB = stat[:, 236:240]
    SSM_W = tiles[:, 14 * T:18 * T]
    BB = [SSM_W[:, 1024 * z:1024 * z + 512].rearrange("p (c n) -> p c n", c=4) for z in range(2)]
    CC = [SSM_W[:, 1024 * z + 512:1024 * z + 1024].rearrange("p (k t) -> p k t", k=16) for z in range(2)]

    def SSM(name, j=0):
        name = name + str(j % 2) if name in ("sr", "si", "sin", "cos", "br", "bi") else name
        i = ["t1", "t2", "wr", "wi", "sr0", "sr1", "si0", "si1", "turns", "sin0", "sin1", "cos0", "cos1",
             "br0", "br1", "bi0", "bi1"].index(name)
        return part(work, i * T, T) if i < 9 else part(rows, (i - 9) * T, T) if i < 15 else TL[:, i + 3, :]

    SC = {n: stat[:, 240 + 16 * i:256 + 16 * i] for i, n in enumerate(
        ("dt", "turn", "hi", "lo", "rho", "t", "u", "s", "c", "h", "x", "y", "den", "kr", "ki", "v"))}

    def sem(name):
        return nc.alloc_semaphore(name)

    const_in, small_in, x_in = sem("const_in"), sem("small_in"), [sem(f"x{i}_in") for i in range(4)]
    slot_in = [sem(f"slot{i}_in") for i in range(SLOTS)]
    gemm_full, gemm_done = sem("gemm_full"), sem("gemm_done")
    score_full, score_done = sem("score_full"), sem("score_done")
    turn_full, turn_done = sem("turn_full"), sem("turn_done")
    sum_full, sum_done = sem("sum_full"), sem("sum_done")
    steps_used = sem("steps_used")
    act_step, dve_step, pool_step = sem("act_step"), sem("dve_step"), sem("pool_step")
    ssm_in, stored = sem("ssm_in"), sem("stored")

    chunks = plan()
    chunk_at = {n: i for i, (n, _) in enumerate(chunks)}

    def chunk(name, t=ring):
        i = chunk_at[name]
        return t[:, (i % SLOTS) * CHUNK:(i % SLOTS) * CHUNK + chunks[i][1]]

    def used(name):
        return turn_full if name[:3] in TURN_CHUNKS else gemm_full, at(f"used {name}")

    block = nc.Block()
    with block:
        @block.sync
        def _(sp):
            for i in range(4):
                sp.dma_start(x_sb[:, 2 * T * i:2 * T * (i + 1)], xT[:, 2 * T * i:2 * T * (i + 1)]).then_inc(x_in[i], 16)
            sp.dma_start(cst[:, :], consts).then_inc(const_in, 16)
            sp.dma_start(sml[:, :], small).then_inc(small_in, 16)
            sp.dma_start(prow[:, :], pos_row).then_inc(small_in, 16)
            sp.dma_start(pcol[:, :], pos_col).then_inc(small_in, 16)
            sp.dma_start(pkey[:, :], pos_key).then_inc(small_in, 16)
            for i, (name, cols) in enumerate(chunks):
                if name == "proj2_0":
                    sp.wait_ge(turn_full, at("used down_7"))
                    sp.dma_start(SSM_W, ssm).then_inc(ssm_in, 16)
                if i >= SLOTS:
                    last = chunks[i - SLOTS][0]
                    sp.wait_ge(*used(last))
                sp.dma_start(ring[:, (i % SLOTS) * CHUNK:(i % SLOTS) * CHUNK + cols],
                             wstream[i, :, 0:cols]).then_inc(slot_in[i % SLOTS], 16)
            sp.wait_ge(dve_step, at("out ready"))
            sp.dma_start(outT, x_sb[:, :]).then_inc(stored, 16)
            sp.wait_ge(stored, 16)

        @block.tensor
        def _(pe):
            seen, sums = set(), [0]

            def have(name):
                if name not in seen:
                    seen.add(name)
                    i = chunk_at[name]
                    pe.wait_ge(slot_in[i % SLOTS], 16 * (i // SLOTS + 1))
                return chunk(name)

            def gemm_bank():
                n = tally.count.get("gemm_full", 0)
                if n >= 3:
                    pe.wait_ge(gemm_done, n - 2)
                return G[n % 3]

            def score_bank():
                n = tally.count.get("score_full", 0)
                if n >= 2:
                    pe.wait_ge(score_done, n - 1)
                return S[n % 2]

            def turn_bank():
                n = tally.count.get("turn_full", 0)
                if n >= 2:
                    pe.wait_ge(turn_done, n - 1)
                return U[n % 2]

            def sum_bank():
                n = sums[0]
                sums[0] += 1
                if n >= 1:
                    pe.wait_ge(sum_done, n)
                return O[0]

            def product(out, pairs, ready=None):
                for i, (l, r) in enumerate(pairs):
                    if ready:
                        pe.wait_ge(ready[0], at(ready[1][i]))
                    mm = pe.matmul(out, l, r, start=(i == 0), stop=(i == len(pairs) - 1))
                return mm

            def split_product(out, name, q0, acts, ready=None):
                last = len(acts) - 1
                for k, (ah, ar) in enumerate(acts):
                    q = q0 + k
                    if q % KD == 0:
                        pe.wait_ge(dve_step, at(f"split {name} {q // KD}"))
                    if ready:
                        pe.wait_ge(dve_step, at(ready[k]))
                    wh, wr = head_of(name, q), chunk(name, ring_r)[:, q * P:(q + 1) * P]
                    pe.matmul(out, wh, ah, start=(k == 0), stop=False)
                    pe.matmul(out, wh, ar, start=False, stop=False)
                    mm = pe.matmul(out, wr, ah, start=False, stop=(k == last))
                return mm

            def feature_units(tag, tiles_, acts, to_turn=False, ready=None):
                full = turn_full if to_turn else gemm_full
                for i, c in enumerate(by_threes(tiles_)):
                    w = have(f"{tag}_{i}").rearrange("p (c k n) -> p c k n", c=len(c), k=KD)
                    for e in range(len(c)):
                        b = turn_bank() if to_turn else gemm_bank()
                        mm = product(b[:, :], [(w[:, e, k, :], acts(k)) for k in range(KD)],
                                     ready if i + e == 0 else None)
                        mm.then_inc(full, 1)
                        up(full)
                        if e == len(c) - 1:
                            tally.named[f"used {tag}_{i}"] = tally.count[full.name]
                        yield

            def row_units(chunk_name, cols, acts, kt=KD):
                w = have(chunk_name).rearrange("p (k n) -> p k n", k=kt)
                for n in range(NT):
                    b = gemm_bank()
                    mm = product(b[:, 0:cols], [(acts[:, k, n * P:(n + 1) * P], w[:, k, :]) for k in range(kt)])
                    mm.then_inc(gemm_full, 1)
                    up(gemm_full, f"full {chunk_name} {n}")
                    if n == NT - 1:
                        tally.named[f"used {chunk_name}"] = tally.count["gemm_full"]
                    yield

            def feature_tiles(*a, **k):
                for _ in feature_units(*a, **k):
                    pass

            def row_tiles(*a, **k):
                for _ in row_units(*a, **k):
                    pass

            def square_sums(name, src, by=dve_step):
                b = gemm_bank()
                product(b[:, :], [(ones, src(k)) for k in range(KD)],
                        (by, [f"squares {name} {k}" for k in range(KD)])).then_inc(gemm_full, 1)
                up(gemm_full, f"full sums {name}")

            def turn(name, blocks, ready):
                b = turn_bank()
                pe.wait_ge(*ready)
                for src, r, dst in blocks:
                    mm = pe.transpose(b[0:src.shape[1], dst:dst + r], src, ident[0:r, 0:r])
                mm.then_inc(turn_full, 1)
                up(turn_full, f"full turn {name}")

            def attention(name, heads, query, key, value, width, before, turn_o=True):
                items = [(n, h) for n in range(NT) for h in range(heads)]
                last = len(items)
                for i in range(last + 3):
                    if i < last:
                        n, h = items[i]
                        cols = (n + 1) * P
                        b = score_bank()
                        if h == 0:
                            before(n)
                        pairs = [(q[:, n * P:(n + 1) * P], k[:, 0:cols]) for q, k in zip(query(h), key(h))]
                        for j, (l, r) in enumerate(pairs):
                            mm = pe.matmul(b[:, 0:cols], l, r, start=(j == 0), stop=False)
                        mm = pe.matmul(b[:, n * P:cols], ident, causal, start=False, stop=True)
                        mm.then_inc(score_full, 1)
                        up(score_full, f"full {name} score {i}")
                    if 1 <= i <= last:
                        n, h = items[i - 1]
                        b = turn_bank()
                        pe.wait_ge(score_done, at(f"{name} probs {i - 1}"))
                        for j in range(n + 1):
                            mm = pe.transpose(b[:, j * P:(j + 1) * P],
                                              probs[:, (i - 1) % 2 * T + j * P:(i - 1) % 2 * T + (j + 1) * P], ident)
                        mm.then_inc(turn_full, 1)
                        up(turn_full, f"full {name} turn {i - 1}")
                    if 2 <= i <= last + 1:
                        n, h = items[i - 2]
                        if h == 0:
                            b = sum_bank()
                        pe.wait_ge(turn_done, at(f"{name} probsT {i - 2}"))
                        for j in range(n + 1):
                            mm = pe.matmul(O[0][:, h * width:(h + 1) * width],
                                           probsT[:, (i - 2) % 2 * T + j * P:(i - 2) % 2 * T + (j + 1) * P],
                                           value(h, j), start=(j == 0), stop=(j == n))
                        mm.then_inc(sum_full, 1)
                        up(sum_full, f"{name} summed {i - 2}")
                    if i >= 3 and items[i - 3][1] == heads - 1:
                        n = items[i - 3][0]
                        if turn_o:
                            turn(f"{name} o {n}", [(work[:, j * P:(j + 1) * P], P, j * P) for j in range(4)],
                                 (sum_done, at(f"{name} o {n}")))


            def rows_out(name, cols, acts, w, kt, used):
                for n in range(NT):
                    b = gemm_bank()
                    product(b[:, 0:cols], [(acts(k)[:, n * P:(n + 1) * P], w(k)) for k in range(kt)]).then_inc(gemm_full, 1)
                    up(gemm_full)

            pe.wait_ge(const_in, 16)
            square_sums("attn", lambda k: H[:, k, :])
            feature_tiles("proj1", PROJ1, lambda k: H[:, k, :], ready=(dve_step, [f"normed attn {k}" for k in range(KD)]))
            row_tiles("rows1_av", 200, H)
            pe.wait_ge(gemm_done, at("have ik"))
            for i in range(3 * 8):
                n, h = 1 + i // 8, i % 8
                b, r = score_bank(), slice(64 * (h % 2), 64 * (h % 2) + 64)
                pe.matmul(b[:, 0:(n + 1) * P], TL[r, h // 2, n * P:(n + 1) * P], TL[r, 4, 0:(n + 1) * P],
                          start=True, stop=True).then_inc(score_full, 1)
                up(score_full, f"full index {i}")
            feature_tiles("proj1b", PROJ1B, lambda k: H[:, k, :])
            for n_ in ("bi0", "bi1"):
                row_tiles(f"rows1_{n_}", 384, H)
            beside = itertools.chain(feature_units("proj1c", PROJ1C, lambda k: H[:, k, :]), row_units("rows1_cq", 384, H))
            for _ in range(5):
                next(beside)

            V = ROW[:, :, 200:712]
            for h in range(4):
                q, k = TL[:, 9 + h, :], TL[:, h, :]
                pe.wait_ge(gemm_done, at("have bg"))
                pe.wait_ge(dve_step, at("keys rec"))

                def blocks(name, pairs, ready):
                    b = turn_bank()
                    pe.wait_ge(dve_step, at(ready))
                    for j, (l, r) in enumerate(pairs):
                        mm = pe.matmul(b[:, j * P:(j + 1) * P], l, r, start=True, stop=True)
                    mm.then_inc(turn_full, 1)
                    up(turn_full, name)

                def ch(a, c):
                    return a[:, c * P:(c + 1) * P]

                blocks(f"full rec diag {h}", [(ch(k, c), ch(q, c)) for c in range(4)], "keys rec")
                blocks(f"full rec near {h}", [(ch(REC_KX, 0), ch(REC_QX, 1)), (ch(REC_KX, 1), ch(REC_QX, 2)),
                                              (ch(REC_KX, 2), ch(REC_QX, 3)), (ch(REC_KX, 0), ch(REC_QS, 0))], f"rec cross {h}")
                blocks(f"full rec far {h}", [(ch(REC_KX, 1), ch(REC_QS, 1)), (ch(REC_KX, 0), ch(REC_QS, 2))], f"rec cross {h}")
                for l in range(LEVELS):
                    qk = REC_QK[l % 2]
                    blocks(f"full rec level {h} {l}", [(ch(qk, c), ch(qk, c)) for c in range(4)], f"rec scaled {h} {l}")
                    if l == 1:
                        next(beside)
                b = sum_bank()
                pe.wait_ge(turn_done, at(f"rec weights {h}"))
                for c in range(4):
                    parts = [(REC_FAR(a, c), V[:, a, h * P:(h + 1) * P]) for a in range(c)] + [(ch(REC_AT, c), V[:, c, h * P:(h + 1) * P])]
                    mm = product(b[:, c * P:(c + 1) * P], parts)
                mm.then_inc(sum_full, 1)
                up(sum_full, f"full rec o {h}")
            for n in range(NT):
                turn(f"rec o {n}", [(REC_O[:, n, j * P:(j + 1) * P], P, j * P) for j in range(4)], (dve_step, at("rec normed")))

            for j in range(3):
                turn(f"cq {j}", [(CQ[:, n, j * P:(j + 1) * P], P, n * P) for n in range(NT)], (dve_step, at("latents normed")))
            for j in range(2):
                turn(f"ckv {j}", [(CKV[:, n, j * P:(j + 1) * P], P, n * P) for n in range(NT)], (dve_step, at("latents normed")))
            pe.wait_ge(turn_done, at("ckvT"))
            w = have("qb").rearrange("p (k n) -> p k n", k=3)
            for j in range(4):
                b = gemm_bank()
                product(b[:, :], [(w[:, k, j * P:(j + 1) * P], CQT[:, k, :]) for k in range(3)]).then_inc(gemm_full, 1)
                up(gemm_full)
            rows_out("qpe", 256, lambda k: CQT[:, k, :], lambda k: w[:, k, 512:768], 3, "qb")
            tally.named["used qb"] = tally.count["gemm_full"]
            w2 = have("kvb").rearrange("p (k n) -> p k n", k=2)
            for j in range(4):
                b = gemm_bank()
                product(b[:, :], [(w2[:, k, j * P:(j + 1) * P], CKVT[:, k, :]) for k in range(2)]).then_inc(gemm_full, 1)
                up(gemm_full)
            rows_out("vc", 512, lambda k: CKVT[:, k, :], lambda k: w2[:, k, 512:1024], 2, "kvb")
            tally.named["used kvb"] = tally.count["gemm_full"]
            turn("kpe", [(KPE2[:, n, :], P, n * P) for n in range(NT)], (dve_step, at("roped")))
            for j in range(2):
                turn(f"qpe {j}", [(QPE[:, n, j * P:(j + 1) * P], P, n * P) for n in range(NT)], (dve_step, at("roped")))
            pe.wait_ge(turn_done, at("qpeT"))
            pe.wait_ge(gemm_done, at("have vc"))

            def half(t, h):
                return t[64 * (h % 2):64 * (h % 2) + 64]

            attention("mla", 4, lambda h: [TL[:, 5 + h, :], half(QPET[:, h // 2, :], h)],
                      lambda h: [TL[:, h, :], half(KPET, h)],
                      lambda h, j: VC[:, j, h * P:(h + 1) * P], P, lambda n: None)
            def modulation():
                for i in range(8):
                    w = have(f"ada_{i}").rearrange("p (c k n) -> p c k n", c=3, k=KD)
                    b = gemm_bank()
                    for k in range(KD):
                        mm = pe.matmul(b[0:1, 0:384].rearrange("p (c n) -> p c n", c=3), SILU_C[:, k:k + 1], w[:, :, k, :],
                                       start=(k == 0), stop=(k == KD - 1))
                        if k == KD - 1:
                            mm.then_inc(gemm_full, 1)
                            up(gemm_full, f"used ada_{i}")
                        yield

            between = modulation()
            pe.wait_ge(dve_step, at("silu c"))
            pe.wait_ge(dve_step, at("increments"))
            for c_, (key, queries) in enumerate(BIAS_PARTS):
                banks = [turn_bank()]
                if len(queries) == 2:
                    n_ = tally.count["turn_full"] + 1
                    pe.wait_ge(turn_done, n_ - 1)
                    banks.append(U[n_ % 2])
                for g in range(32):
                    pe.wait_ge(dve_step, at(f"steps {c_} {g}"))
                    for e, b in enumerate(banks):
                        for z in range(3):
                            mm = pe.matmul(b[:, 16 * g:16 * g + 16], STEPS(g, P * len(banks))[:, e * P:(e + 1) * P], REL[z],
                                           start=(z == 0), stop=(z == 2))
                        if g == 31:
                            mm.then_inc(turn_full, 1)
                            up(turn_full)
                    if g < 31:
                        mm.then_inc(steps_used, 1)
                        up(steps_used, f"bias {c_} {g}")
                    if (32 * c_ + g) % 3 == 2:
                        next(between)
            attention("dsa", 4, lambda h: [TL[:, 13 + h, :]], lambda h: [TL[:, 17, :]],
                      lambda h, j: ROW[:, j, 0:128], P, lambda n: None)

            b = turn_bank()
            pe.wait_ge(gemm_done, at("have mod"))
            for i in range(24):
                mm = pe.transpose(b[:, i:i + 1], MODROW[i // 3][:, i % 3 * P:(i % 3 + 1) * P], ident[0:1, 0:1])
            mm.then_inc(turn_full, 1)
            up(turn_full)

            branch = {0: 13, 1: 9, 2: 5}
            acts = [(H_HEAD[:, k, :], H_REST[:, k, :]) for k in range(KD)]
            for j in range(8):
                for b_ in range(3):
                    b = gemm_bank()
                    split_product(b[:, :], f"gate_{j}", b_ * KD, acts,
                                  None if j or b_ else [f"split attn {k}" for k in range(KD)]).then_inc(gemm_full, 1)
                    up(gemm_full)
                tally.named[f"used gate_{j}"] = tally.count["gemm_full"]
                w = have(f"up_{j // 2}").rearrange("p (e b k n) -> p e b k n", e=2, b=3, k=4)
                if j == 0:
                    pe.wait_ge(turn_done, at("dsa oT 3"))
                for b_ in range(3):
                    b = turn_bank()
                    product(b[:, :], [(w[:, j % 2, b_, k, :], TL[:, branch[b_] + k, :]) for k in range(4)]).then_inc(turn_full, 1)
                    up(turn_full)
                if j % 2:
                    tally.named[f"used up_{j // 2}"] = tally.count["turn_full"]
            mixed = [(H_HEAD[:, k, :], TL_REST[:, MIX[k], :]) for k in range(KD)]
            for j in range(8):
                b = turn_bank()
                split_product(b[:, :], f"wout_{j // 3}", j % 3 * KD, mixed,
                              None if j else [f"split mixed {k}" for k in range(KD)]).then_inc(turn_full, 1)
                up(turn_full)
                if j % 3 == 2 or j == 7:
                    tally.named[f"used wout_{j // 3}"] = tally.count["turn_full"]

            square_sums("ffn", lambda k: H[:, k, :])
            for j in range(NFF):
                b = gemm_bank()
                split_product(b[:, :], f"ff_{j}", 0, acts,
                              None if j else [f"split ffn {k}" for k in range(KD)]).then_inc(gemm_full, 1)
                up(gemm_full)
                b = turn_bank()
                split_product(b[:, :], f"ff_{j}", KD, acts).then_inc(turn_full, 1)
                up(turn_full)
                tally.named[f"used ff_{j}"] = tally.count["turn_full"]
            hidden = [(HIDDEN_HEAD[k], TL_REST[:, k, :]) for k in range(NFF)]
            for j in range(8):
                b = turn_bank()
                split_product(b[:, :], f"down_{j}", 0, hidden,
                              None if j else [f"split hidden {k}" for k in range(NFF)]).then_inc(turn_full, 1)
                up(turn_full)
                tally.named[f"used down_{j}"] = tally.count["turn_full"]
            square_sums("final", lambda k: SQUARES[k])

            square_sums("block2", lambda k: H[:, k, :], act_step)
            units = itertools.chain(feature_units("proj2", PROJ2, lambda k: H[:, k, :],
                                                  ready=(act_step, [f"normed block2 {k}" for k in range(KD)])), row_units("rows2_q0", 384, H),
                                    row_units("rows2_q1", 384, H), row_units("rows2_w", 280, H))
            for _ in range(4):
                next(units)
            pe.wait_ge(ssm_in, 16)
            for j in range(17):
                if j < 16:
                    if j == 0:
                        pe.wait_ge(gemm_done, at("have u"))
                    r = slice(32 * (j % 4), 32 * (j % 4) + 32)
                    for z in range(2):
                        b = gemm_bank()
                        pe.matmul(b[:, :], BB[z][r, j // 4, :], TL[r, 2 + j // 4, :], start=True, stop=True)\
                            .then_inc(gemm_full, 1)
                        up(gemm_full)
                    for _ in range(SIDE[j]):
                        next(units)
                if j >= 1:
                    i = j - 1
                    if i % 4 == 0:
                        b = sum_bank()
                    pe.wait_ge(dve_step, at(f"states {i}"))
                    q_ = slice(32 * (i % 4), 32 * (i % 4) + 32)
                    pe.matmul(O[0][q_, :], CC[0][:, i, :], SSM("sr", i), start=True, stop=False)
                    mm = pe.matmul(O[0][q_, :], CC[1][:, i, :], SSM("si", i), start=False, stop=True)
                    mm.then_inc(sum_full, 1)
                    up(sum_full, f"full y {i}")
            for _ in units:
                pass
            w = have("glu").rearrange("p (k n) -> p k n", k=4)
            pe.wait_ge(act_step, at("y gelu"))
            for j in range(4):
                b = gemm_bank()
                product(b[:, :], [(w[:, k, j * P:(j + 1) * P], TL[:, 2 + k, :]) for k in range(4)]).then_inc(gemm_full, 1)
                up(gemm_full)
            tally.named["used glu"] = tally.count["gemm_full"]

            pe.wait_ge(gemm_done, at("have zs"))
            def compress(kv):
                parts = [(have(f"cmp_{kv}{i}").rearrange("p (l n) -> p l n", n=256), lo, n)
                         for i, (lo, n) in enumerate(((0, 12), (12, 12), (24, 8)))]
                b = gemm_bank()
                pe.wait_ge(dve_step, at(f"blocks {kv}"))
                product(b[0:2 * NCMP, 0:256], [(CB[:, lo + l, :], w[:, l, :]) for w, lo, n in parts for l in range(n)])\
                    .then_inc(gemm_full, 1)
                up(gemm_full)
                for i in range(3):
                    tally.named[f"used cmp_{kv}{i}"] = tally.count["gemm_full"]

            compress("k")
            for j in range(4):
                turn(f"q {j}", [(R2[:, n, j * P:(j + 1) * P], P, n * P) for n in range(NT)], (dve_step, at("q normed")))
            compress("v")
            for j in range(4):
                turn(f"qr {j}", [(R2[:, n, j * P:(j + 1) * P], P, n * P) for n in range(NT)], (dve_step, at("q roped")))
            for kv in "kv":
                turn(f"hidden {kv}", [(HROW(kv)[0:2 * NCMP, k * P:(k + 1) * P], 2 * NCMP, 64 * k) for k in range(2)],
                     (gemm_done, at(f"hidden {kv}")))
            for kv in "kv":
                b = gemm_bank()
                pe.wait_ge(turn_done, at(f"hidden T {kv}"))
                w2_ = sm(f"w2_{kv}").rearrange("p (k n) -> p k n", k=2)
                for g in range(2):
                    mm = product(b[0:NCMP, 64 * g:64 * g + 64], [(HID(kv)[:, k, g * NCMP:(g + 1) * NCMP], w2_[:, k, :]) for k in range(2)])
                mm.then_inc(gemm_full, 1)
                up(gemm_full)
            for i in range(4):
                turn(f"k2 {i}", [(K2(i)[:, n, :], P, n * P) for n in range(NT)], (dve_step, at("k roped")))
            turn("kc", [(KC2[0:NCMP, g, :], NCMP, 32 * g) for g in range(2)], (dve_step, at("kc normed")))
            pe.wait_ge(turn_done, at("kcT"))
            def cmp_scores(i):
                n, e = divmod(i, 2)
                b = score_bank()
                for q_ in range(4):
                    h = 2 * q_ + e
                    r = slice(64 * e, 64 * e + 64)
                    mm = pe.matmul(b[:, q_ * NCMP:(q_ + 1) * NCMP], TL[r, 14 + h // 2, n * P:(n + 1) * P],
                                   KCT[r, 32 * (h // 4):32 * (h // 4) + NCMP], start=True, stop=True)
                mm.then_inc(score_full, 1)
                up(score_full, f"full cmp {i}")

            for i in range(8):
                cmp_scores(i)
                n, e = divmod(i, 2)
                b = turn_bank()
                pe.wait_ge(dve_step, at(f"cmp probs {i}"))
                for q_ in range(4):
                    mm = pe.transpose(b[0:NCMP, q_ * P:(q_ + 1) * P], CMP_P[:, q_ * NCMP:(q_ + 1) * NCMP], ident)
                mm.then_inc(turn_full, 1)
                up(turn_full)
                if e == 0:
                    b = sum_bank()
                pe.wait_ge(turn_done, at(f"cmp probsT {i}"))
                for q_ in range(4):
                    h = 2 * q_ + e
                    mm = pe.matmul(O[0][:, 64 * h:64 * h + 64], probsT[0:NCMP, q_ * P:(q_ + 1) * P],
                                   VCMP[0:NCMP, 64 * (h // 4):64 * (h // 4) + 64], start=True, stop=True)
                mm.then_inc(sum_full, 1)
                up(sum_full, f"cmp summed {i}")

            def both(t, h):
                return t[64 * (h % 2):64 * (h % 2) + 64, :]

            for a_, name in enumerate(("slc", "win")):
                attention(name, 8, lambda h: [both(TL[:, 18 + h // 2, :], h)],
                          lambda h: [both(KT2[:, 2 * a_ + h // 4, :], h)],
                          lambda h, j: R2[:, j, (640 if a_ == 0 else 896) + 64 * (h // 4):(640 if a_ == 0 else 896) + 64 * (h // 4) + 64],
                          64, lambda n: None, turn_o=False)
            for n in range(NT):
                turn(f"attn {n}", [(ATT[:, n, j * P:(j + 1) * P], P, j * P) for j in range(4)], (sum_done, at("win o 3")))

            pe.wait_ge(dve_step, at("ssm out"))
            pe.wait_ge(turn_done, at("attn T 3"))
            feature_tiles("wout2", range(8), lambda k: TL[:, 6 + k, :], to_turn=True)

        @block.scalar
        def _(act):
            def step(ins, name=None, sem_=act_step):
                n = up(sem_, name)
                ins.then_inc(sem_, 1)
                act.wait_ge(sem_, n)

            drained = [0]

            def drain(out, name=None, func=ACT.Identity, bias=0.0, scale=1.0, cols=T, rows_=P, src=None):
                n = drained[0]
                drained[0] += 1
                act.wait_ge(gemm_full, n + 1)
                b = G[n % 3][0:rows_, 0:cols] if src is None else src(G[n % 3])
                step(act.activation(out, b, func, bias=bias, scale=scale), name, gemm_done)

            def attention_exp(name, heads, logits=None):
                for i in range(NT * heads):
                    n, h = divmod(i, heads)
                    cols = (n + 1) * P
                    act.wait_ge(dve_step, at(f"{name} max {i}"))
                    if i >= 2:
                        act.wait_ge(turn_full, at(f"full {name} turn {i - 2}"))
                    if h == 0 and n >= 2:
                        act.wait_ge(sum_done, at(f"{name} o {n - 2}"))
                    src = S[(at(f"full {name} score {i}") - 1) % 2][:, 0:cols] if logits is None else logits(i, cols)
                    step(act.activation(probs[:, i % 2 * T:i % 2 * T + cols], src, ACT.Exp,
                                        bias=stat[:, 8 + i % 2:9 + i % 2], scale=1.0,
                                        accum_out=stat[:, 16 + (n % 2) * 8 + h:17 + (n % 2) * 8 + h]),
                         f"{name} probs {i}", score_done)


            def weights_head(name):
                i, n = chunk_at[name], SPLIT.index(name)
                act.wait_ge(slot_in[i % SLOTS], 16 * (i // SLOTS + 1))
                if n >= 2:
                    act.wait_ge(*used(SPLIT[n - 2]))
                for z, c, cols in parts_of(name):
                    step(act.activation(head_of(name, z * KD, cols // P), chunk(name)[:, c:c + cols], ACT.Identity),
                         f"head {name} {z}")

            def head(name, dst, src):
                step(act.activation(dst, src, ACT.Identity), f"head {name}")

            def sums_out(name):
                drain(work[:, 0:T], f"mean {name}", bias=con("misc")[:, 1:2], scale=1.0 / D)
                step(act.activation(work[:, T:2 * T], work[:, 0:T], ACT.Sqrt), f"root {name}")

            act.wait_ge(const_in, 16)
            act.wait_ge(small_in, 64)
            sums_out("attn")
            dest = {"iq": 0, "ik": 4, "bf": 5, "bq": 9, "aq": 13, "ak": 17, "bg": 18}
            scales = {"bq": P ** -0.5, "aq": P ** -0.5, "bg": 0.5}

            def project(tiles_):
                for n, i in tiles_:
                    drain(TL[:, dest[n] + i, :], f"tile {n} {i}", scale=scales.get(n, 1.0))

            project(PROJ1)
            for n in range(NT):
                drain(ROW[:, n, 0:200], "have ik" if n == NT - 1 else None, cols=200)
            for i in range(24):
                n = 1 + i // 8
                act.wait_ge(score_full, at(f"full index {i}"))
                if i >= 2:
                    act.wait_ge(dve_step, at(f"index added {i - 2}"))
                step(act.activation(probs[:, i % 2 * T:i % 2 * T + (n + 1) * P], S[i % 2][:, 0:(n + 1) * P], ACT.Relu),
                     f"index relu {i}", score_done)
            project(PROJ1B)
            for n in range(NT):
                drain(ROW[:, n, 200:584], cols=384)
            for n in range(NT):
                k = drained[0]
                drained[0] += 1
                act.wait_ge(gemm_full, k + 1)
                step(act.activation(ROW[:, n, 584:712], G[k % 3][:, 0:128], ACT.Identity))
                step(act.activation(CKV[:, n, :], G[k % 3][:, 128:384], ACT.Identity),
                     "have bg" if n == NT - 1 else None, gemm_done)

            def drains1():
                for one in PROJ1C:
                    project([one])
                    yield
                for n in range(NT):
                    drain(CQ[:, n, :], "have cq" if n == NT - 1 else None, cols=384)
                    yield

            beside = drains1()

            f4, k4, w0 = tiles[:, 5 * T:9 * T], tiles[:, 0:4 * T], work[:, 0:4 * T]
            act.wait_ge(dve_step, at("chosen"))
            step(act.activation(k4, f4, ACT.Abs))
            step(act.activation(w0, k4, ACT.Exp, scale=-1.0), "rec u")
            step(act.activation(k4, f4, ACT.Relu))
            step(act.activation(k4, k4, ACT.Exp, scale=-1.0), "rec num")
            next(beside)
            act.wait_ge(dve_step, at("rec one plus u"))
            step(act.activation(w0, w0, ACT.Ln, bias=1.0), "rec ln")
            next(beside)
            act.wait_ge(dve_step, at("rec log sigmoid"))
            step(act.activation(w0, f4, ACT.Abs, bias=con("misc")[:, 3:4], scale=1.0))
            step(act.activation(w0, w0, ACT.Exp, scale=-1.0))
            step(act.activation(w0, w0, ACT.Ln, bias=1.0), "rec floor")
            next(beside)
            act.wait_ge(dve_step, at("rec log f"))
            next(beside)
            next(beside)
            step(act.activation(SILU_C, sm("c2"), ACT.Tanh, scale=0.5), "tanh c")
            step(act.activation(w0, tiles[:, 18 * T:22 * T], ACT.Tanh), "rec gate")
            for h in range(4):
                bt = TL[:, 5 + h, :]
                act.wait_ge(dve_step, at(f"rec args {h}"))
                step(act.activation(REC_E[0], bt, ACT.Exp), f"rec eb {h}")
                step(act.activation(REC_E[1], REC_E[1], ACT.Exp), f"rec el {h}")
                for l in range(LEVELS):
                    act.wait_ge(dve_step, at(f"rec args {h} {l}"))
                    step(act.activation(REC_E[l % 2], REC_E[l % 2], ACT.Exp), f"rec e {h} {l}")
                    if l == 3:
                        next(beside)

            for j in range(4):
                drain(TL[:, 5 + j, :], scale=MLA_SCALE)
            for n in range(NT):
                drain(QPE[:, n, :], "have qpe" if n == NT - 1 else None, scale=MLA_SCALE, cols=256)
            for j in range(4):
                drain(TL[:, j, :])
            for n in range(NT):
                drain(VC[:, n, :], "have vc" if n == NT - 1 else None)
            act.wait_ge(dve_step, at("angles"))
            step(act.activation(trig[:, P:2 * P], trig[:, 0:P], ACT.Sin))
            step(act.activation(trig[:, 0:P], trig[:, 0:P], ACT.Abs))
            step(act.activation(trig[:, 0:P], trig[:, 0:P], ACT.Sin, bias=con("misc")[:, 2:3], scale=-1.0), "trig")
            attention_exp("mla", 4)
            for i in range(8):
                drain(MODROW[i], "have mod" if i == 7 else None, cols=384, rows_=1)
            attention_exp("dsa", 4, lambda i, cols: LOGITS[i % 2][:, 0:cols])

            act.wait_ge(dve_step, at("dsa done"))
            for k in range(KD):
                head(f"attn {k}", H_HEAD[:, k, :], H[:, k, :])
                if k == 1:
                    weights_head("gate_0")
            weights_head("gate_1")
            for j in range(8):
                for b_ in range(3):
                    if j >= 1:
                        act.wait_ge(dve_step, at(f"mixed {j - 1}"))
                    drain(GATE[b_], f"gate {j} {b_}", func=ACT.Tanh, scale=0.5)
                if j < 7:
                    weights_head(SPLIT[j + 2])
            for k in range(KD):
                act.wait_ge(dve_step, at(f"mixed {k}"))
                head(f"mixed {k}", H_HEAD[:, k, :], TL[:, MIX[k], :])
            for name in ("wout_1", "wout_2", "ff_0", "ff_1"):
                weights_head(name)

            sums_out("ffn")
            for k in range(KD):
                act.wait_ge(dve_step, at(f"normed ffn {k}"))
                head(f"ffn {k}", H_HEAD[:, k, :], H[:, k, :])
            for j in range(NFF):
                if j >= 2:
                    act.wait_ge(turn_done, at(f"ff {j - 2}"))
                k = drained[0]
                drained[0] += 1
                act.wait_ge(gemm_full, k + 1)
                step(act.activation(part(work, j % 2 * T, T), G[k % 3][:, :], ACT.Tanh, scale=0.5))
                step(act.activation(part(work, (2 + j % 2) * T, T), G[k % 3][:, :], ACT.Identity, scale=0.5),
                     f"ff gate {j}", gemm_done)
                if j + 1 < NFF:
                    weights_head(SPLIT[SPLIT.index(f"ff_{j}") + 2])
                if 2 <= j < 6:
                    head(f"hidden {j - 2}", HIDDEN_HEAD[j - 2], TL[:, j - 2, :])
            act.wait_ge(*used(f"ff_{NFF - 1}"))
            for k in range(4, NFF):
                act.wait_ge(turn_done, at(f"ff {k}"))
                head(f"hidden {k}", HIDDEN_HEAD[k], TL[:, k, :])
            for j in range(1, 8):
                weights_head(f"down_{j}")
            sums_out("final")
            for k in range(KD):
                act.wait_ge(dve_step, at(f"normed final {k}"))
                step(act.activation(H[:, k, :], X[:, k, :], ACT.Square), f"squares block2 {k}")
            sums_out("block2")
            for k in range(KD):
                act.wait_ge(dve_step, at(f"scaled block2 {k}"))
                step(act.activation(H[:, k, :], H[:, k, :], ACT.Identity, bias=MOD[:, k:k + 1]), f"normed block2 {k}")
            scale2 = {"za": 0.5, "zs": 0.25}
            dest2 = {"kcr": 0, "vcr": 1, "u": 2, "za": 6, "zs": 10}
            def drains2():
                for n, i in PROJ2:
                    drain(TL[:, dest2[n] + i, :], f"have {n}" if i == 3 else f"have {n} {i}", scale=scale2.get(n, 1.0))
                    yield
                for a_, c_ in ((0, 384), (384, 384), (768, 280)):
                    for n in range(NT):
                        drain(R2[:, n, a_:a_ + c_], "have rows2" if (a_, n) == (768, NT - 1) else None, cols=c_)
                        yield

            units = drains2()
            step(act.activation(SC["dt"], sm("log_dt"), ACT.Exp), "dt")
            act.wait_ge(dve_step, at("ssm turn"))
            step(act.activation(SC["rho"], SC["rho"], ACT.Exp), "rho")
            step(act.activation(SC["s"], SC["turn"], ACT.Sin, scale=TWO_PI_IN))
            step(act.activation(SC["h"], SC["turn"], ACT.Sin, scale=TWO_PI_IN / 2))
            step(act.activation(SC["c"], SC["turn"], ACT.Abs))
            step(act.activation(SC["c"], SC["c"], ACT.Sin, scale=-TWO_PI_IN, bias=con("misc")[:, 2:3]), "ssm trig")
            for _ in range(4):
                next(units)
            for j in range(16):
                act.wait_ge(dve_step, at(f"phases {j}"))
                if j >= 2:
                    act.wait_ge(dve_step, at(f"states {j - 2}"))
                step(act.activation(SSM("sin", j), SSM("turns"), ACT.Sin, scale=TWO_PI_IN))
                step(act.activation(SSM("turns"), SSM("turns"), ACT.Abs))
                step(act.activation(SSM("cos", j), SSM("turns"), ACT.Sin, scale=-TWO_PI_IN, bias=con("misc")[:, 2:3]), f"waves {j}")
                drain(SSM("br", j))
                drain(SSM("bi", j), f"bu {j}")
                for _ in range(SIDE[j]):
                    next(units)
            for _ in units:
                pass
            act.wait_ge(sum_done, at("y 3"))
            step(act.activation(tiles[:, 2 * T:6 * T], tiles[:, 2 * T:6 * T], ACT.Gelu_apprx_tanh), "y gelu")
            step(act.activation(part(work, 0, 4 * T), tiles[:, 10 * T:14 * T], ACT.Tanh, scale=2.0), "tanh zs")
            for j in range(4):
                drain(part(work, (4 + j) * T, T), f"glu {j}", func=ACT.Tanh, scale=0.5, bias=GLUB[:, j:j + 1])
            act.wait_ge(dve_step, at("ssm out"))
            for kv in "kv":
                drain(HROW(kv)[0:2 * NCMP, :], f"hidden {kv}", func=ACT.Gelu_apprx_tanh, cols=256, rows_=2 * NCMP)
            drain(KCRAW[0:NCMP, :], "have kc", cols=P, rows_=NCMP)
            drain(VCMP[0:NCMP, :], "have vcmp", cols=P, rows_=NCMP)
            act.wait_ge(dve_step, at("branch logits"))
            for z in range(3):
                step(act.activation(GB[z], GB[z], ACT.Tanh, scale=0.5), "branch gates" if z == 2 else None)
            for i in range(8):
                n, e = divmod(i, 2)
                act.wait_ge(score_full, at(f"full cmp {i}"))
                if i >= 1:
                    act.wait_ge(turn_done, at(f"cmp probsT {i - 1}"))
                step(act.activation(CMP_P, S[(at(f"full cmp {i}") - 1) % 2][:, 0:4 * NCMP], ACT.Identity),
                     f"cmp score {i}", score_done)
                act.wait_ge(dve_step, at(f"cmp less max {i}"))
                step(act.activation(CMP_P, CMP_P, ACT.Exp), f"cmp exp {i}")
            attention_exp("slc", 8)
            attention_exp("win", 8)
            act.wait_ge(dve_step, at("gates free"))
            w2t = part(wide, 6 * T, 4 * T)
            step(act.activation(w2t, tiles[:, 6 * T:10 * T], ACT.Tanh), "tanh za")

        @block.vector
        def _(dve):
            def step(ins, name=None, sem_=dve_step):
                n = up(sem_, name)
                ins.then_inc(sem_, 1)
                dve.wait_ge(sem_, n)

            turned = [0]

            def split(name, x, head, rest):
                dve.wait_ge(act_step, at(f"head {name}"))
                tt(rest, x, head.bitcast(F32), ALU.subtract, f"split {name}")

            def weights_split(name, only=(0, 1, 2)):
                for z, c, cols in parts_of(name):
                    if z in only:
                        split(f"{name} {z}", chunk(name)[:, c:c + cols], head_of(name, z * KD, cols // P),
                              chunk(name, ring_r)[:, c:c + cols])

            def rms_scale(name, gain, out, source=X, mark="normed", heads=None):
                a, y, z = work[:, 0:T], work[:, T:2 * T], work[:, 2 * T:3 * T]
                dve.wait_ge(gemm_done, at(f"mean {name}"))
                dve.wait_ge(act_step, at(f"root {name}"))
                step(dve.reciprocal(y, y))
                step(dve.tensor_tensor(z, y, y, ALU.mult))
                step(dve.tensor_tensor(z, z, a, ALU.mult))
                step(dve.tensor_scalar(z, z, -0.5, 1.5, ALU.mult, ALU.add))
                step(dve.tensor_tensor(y, y, z, ALU.mult), f"rstd {name}")
                for k in range(KD):
                    step(dve.scalar_tensor_tensor(out=out[:, k, :], in0=source[:, k, :], scalar=gain(k), in1=y,
                                                  op0=ALU.mult, op1=ALU.mult),
                         f"{mark} {name} {k}")
                    if heads is not None and k >= 2:
                        split(f"{name} {k - 2}", out[:, k - 2, :], heads[:, k - 2, :], H_REST[:, k - 2, :])
                if heads is not None:
                    for k in (KD - 2, KD - 1):
                        split(f"{name} {k}", out[:, k, :], heads[:, k, :], H_REST[:, k, :])
            def squares(name, k, out):
                step(dve.tensor_tensor(out, X[:, k, :], X[:, k, :], ALU.mult), f"squares {name} {k}")

            def take_turn(name, dst, scalar=None, cols=T, rows_=P, view=None, eng=None):
                n = turned[0]
                turned[0] += 1
                dve.wait_ge(turn_full, n + 1)
                src = U[n % 2][0:rows_, 0:cols]
                if view is not None:
                    src = view(src)
                if scalar is None:
                    ins = dve.tensor_copy(dst, src)
                else:
                    ins = dve.tensor_scalar(dst, src, scalar, None, ALU.mult)
                step(ins, name, turn_done)

            def attention_max(name, heads, finish, take_o=None, logits=None):
                items = [(n, h) for n in range(NT) for h in range(heads)]
                last = len(items)
                for i in range(last + 3):
                    if i < last:
                        n, h = items[i]
                        cols = (n + 1) * P
                        dve.wait_ge(score_full, at(f"full {name} score {i}"))
                        src = S[(at(f"full {name} score {i}") - 1) % 2][:, 0:cols]
                        if i >= 2:
                            dve.wait_ge(score_done, at(f"{name} probs {i - 2}"))
                        if logits is not None:
                            src = logits(i, n, h, src)
                        step(dve.tensor_reduce(stat[:, 8 + i % 2:9 + i % 2], src, AX.X, ALU.max, negate=True),
                             f"{name} max {i}")
                    if 1 <= i <= last:
                        n, h = items[i - 1]
                        if i - 1 >= 2:
                            dve.wait_ge(sum_full, at(f"{name} summed {i - 3}"))
                        take_turn(f"{name} probsT {i - 1}", probsT[:, (i - 1) % 2 * T:(i - 1) % 2 * T + (n + 1) * P],
                                  cols=(n + 1) * P)
                    if 2 <= i <= last + 1 and items[i - 2][1] == heads - 1:
                        finish(items[i - 2][0])
                    if take_o is not None and i >= 3 and items[i - 3][1] == heads - 1:
                        take_o(items[i - 3][0])


            def small_rstd(name, mean, n):
                step(dve.tensor_scalar(mean, mean, 1.0 / n, EPS, ALU.mult, ALU.add), f"mean {name}")
                dve.wait_ge(pool_step, at(f"rstd {name}"))

            def tt(out, a, b, op, name=None):
                step(dve.tensor_tensor(out, a, b, op), name)

            def ts(out, a, s1, s2, o1, o2=None, name=None):
                step(dve.tensor_scalar(out, a, s1, s2, o1, *([o2] if o2 is not None else [])), name)

            def stt(out, a, s_, b, o1, o2, name=None, sem_=dve_step):
                step(dve.scalar_tensor_tensor(out=out, in0=a, scalar=s_, in1=b, op0=o1, op1=o2), name, sem_)

            def sum_out(fill, write):
                dve.wait_ge(sum_full, at(fill))
                write(O[0])

            def probs_over_sums(name, dst, heads, gate=None):
                def finish(n):
                    last = (n + 1) * heads - 1
                    dve.wait_ge(score_done, at(f"{name} probs {last}"))
                    r = stat[:, 16 + (n % 2) * 8:16 + (n % 2) * 8 + heads]
                    step(dve.reciprocal(r, r))
                    if gate is not None:
                        tt(r, r, gate(n), ALU.mult)
                    dve.wait_ge(sum_full, at(f"{name} summed {last}"))
                    w = T // heads
                    o3 = O[0][:, :].rearrange("p (h d) -> p h d", h=heads)
                    rb = r.unsqueeze(2).broadcast_to([P, heads, w])
                    if gate is None:
                        if n:
                            dve.wait_ge(turn_full, at(f"full turn {name} o {n - 1}"))
                        step(dve.tensor_tensor(dst(n).rearrange("p (h d) -> p h d", h=heads), o3, rb, ALU.mult),
                             f"{name} o {n}", sum_done)
                    else:
                        t_ = part(wide, 4200, T)
                        step(dve.tensor_tensor(t_.rearrange("p (h d) -> p h d", h=heads), o3, rb, ALU.mult))
                        step(dve.tensor_tensor(dst(n), dst(n), t_, ALU.add), f"{name} o {n}", sum_done)
                return finish

            def o_to_tiles(name, first):
                def take(n):
                    take_turn(f"{name} oT {n}", TL[:, first:first + 4, n * P:(n + 1) * P],
                              view=lambda v: v.rearrange("p (j t) -> p j t", j=4))
                return take

            for k in range(KD):
                if k % 2 == 0:
                    dve.wait_ge(x_in[k // 2], 16)
                squares("attn", k, H[:, k, :])
            dve.wait_ge(small_in, 64)
            dve.wait_ge(const_in, 16)
            rms_scale("attn", lambda k: sm("g_attn")[:, k:k + 1], H)
            for i in range(24):
                n, h = 1 + i // 8, i % 8
                r, iw = probs[:, i % 2 * T:i % 2 * T + (n + 1) * P], ROW[:, n, 128 + h:129 + h]
                dve.wait_ge(score_done, at(f"index relu {i}"))
                if h == 0:
                    ts(INDEX[n], r, iw, None, ALU.mult, name=f"index added {i}")
                else:
                    stt(INDEX[n], r, iw, INDEX[n], ALU.mult, ALU.add, name=f"index added {i}")
            step(dve.tensor_copy(chosen[:, 0:P], causal))
            for n in range(1, NT):
                a = INDEX[n]
                ts(a, a, (64 ** -0.5) * (8 ** -0.5), None, ALU.mult)
                tt(a[:, n * P:(n + 1) * P], a[:, n * P:(n + 1) * P], causal, ALU.add)
                for _i in range(TOPK // 8):
                    step(dve.max(stat[:, 0:8], a))
                    step(dve.match_replace(out=a, in_to_replace=stat[:, 0:8], in_values=a, imm_value=TAKEN))
                ts(chosen[:, upto(n):upto(n + 1)], a, TAKEN, NEG, ALU.not_equal, ALU.mult, name="chosen" if n == 3 else None)

            f4, k4, w0, w1 = tiles[:, 5 * T:9 * T], tiles[:, 0:4 * T], work[:, 0:4 * T], work[:, 4 * T:8 * T]
            dve.wait_ge(gemm_done, at("have bg"))
            dve.wait_ge(act_step, at("rec u"))
            ts(w1, w0, 1.0, None, ALU.add, name="rec one plus u")
            step(dve.reciprocal(w1, w1))
            dve.wait_ge(act_step, at("rec num"))
            tt(k4, k4, w1, ALU.mult, "keys rec")
            dve.wait_ge(act_step, at("rec ln"))
            stt(f4, f4, 0.0, w0, ALU.min, ALU.subtract, name="rec log sigmoid")
            dve.wait_ge(act_step, at("rec floor"))
            stt(f4, f4, LOG_FLOOR, w0, ALU.max, ALU.add, name="rec log f")
            for h in range(4):
                bt = TL[:, 5 + h, :]
                step(dve.tensor_tensor_scan(bt, con("reset"), bt, 0.0, ALU.mult, ALU.add))
            dve.wait_ge(act_step, at("rec gate"))
            g4 = tiles[:, 18 * T:22 * T]
            stt(g4, w0, 1.0, g4, ALU.add, ALU.mult)
            for h in range(4):
                bt, q, k = TL[:, 5 + h, :], TL[:, 9 + h, :], TL[:, h, :]
                b4 = bt.rearrange("p (c t) -> p c t", c=4)
                e4 = REC_E[1].rearrange("p (c t) -> p c t", c=4)
                tt(e4, b4[:, :, P - 1:P].broadcast_to([P, 4, P]), b4, ALU.subtract, f"rec args {h}")
                dve.wait_ge(act_step, at(f"rec el {h}"))
                tt(REC_QX, q, REC_E[0], ALU.mult)
                tt(REC_KX, k, REC_E[1], ALU.mult)
                end = [REC_E[0][:, (c + 1) * P - 1:(c + 1) * P] for c in range(4)]
                ts(REC_QS[:, 0:P], REC_QX[:, 2 * P:3 * P], end[1], None, ALU.mult)
                ts(REC_QS[:, P:2 * P], REC_QX[:, 3 * P:4 * P], end[2], None, ALU.mult)
                ts(REC_QS[:, 2 * P:3 * P], REC_QS[:, P:2 * P], end[1], None, ALU.mult, name=f"rec cross {h}")
                step(dve.memset(REC_AT, 0.0))
                lev = con("level").rearrange("p (l t) -> p l t", l=LEVELS + 1)

                def take_level(l):
                    m = turned[0]
                    turned[0] += 1
                    dve.wait_ge(turn_full, m + 1)
                    mask = lev[:, l:l + 1, :].bitcast(I32).broadcast_to([P, 4, P])
                    step(dve.copy_predicated(REC_AT.rearrange("p (c t) -> p c t", c=4), mask,
                                             U[m % 2][:, :].rearrange("p (c t) -> p c t", c=4)),
                         f"rec weights {h}" if l == LEVELS else None, turn_done)

                def args(l):
                    m = 1 << l
                    bv = bt.rearrange("p (n t) -> p n t", t=2 * m)
                    ev = REC_E[l % 2].rearrange("p (n t) -> p n t", t=2 * m)
                    ref = bv[:, :, m - 1:m].broadcast_to([P, T // (2 * m), m])
                    tt(ev[:, :, 0:m], ref, bv[:, :, 0:m], ALU.subtract)
                    tt(ev[:, :, m:], bv[:, :, m:], ref, ALU.subtract, f"rec args {h} {l}")

                args(0)
                take_level(0)
                take_turn(None, REC_X[:, 0:4 * P])
                take_turn(None, REC_X[:, 4 * P:6 * P], cols=2 * P)
                for l in range(LEVELS):
                    m = 1 << l
                    if l + 1 < LEVELS:
                        args(l + 1)
                    dve.wait_ge(act_step, at(f"rec e {h} {l}"))
                    ev = REC_E[l % 2].rearrange("p (n t) -> p n t", t=2 * m)
                    ov = REC_QK[l % 2].rearrange("p (n t) -> p n t", t=2 * m)
                    kv_, qv = k.rearrange("p (n t) -> p n t", t=2 * m), q.rearrange("p (n t) -> p n t", t=2 * m)
                    tt(ov[:, :, 0:m], kv_[:, :, 0:m], ev[:, :, 0:m], ALU.mult)
                    tt(ov[:, :, m:], qv[:, :, m:], ev[:, :, m:], ALU.mult, f"rec scaled {h} {l}")
                    if l >= 1:
                        take_level(l)
                take_level(LEVELS)
                dve.wait_ge(sum_full, at(f"full rec o {h}"))
                step(dve.tensor_copy(REC_O[:, :, h * P:(h + 1) * P], O[0][:, :].rearrange("p (c t) -> p c t", c=4)),
                     None, sum_done)
            o16 = part(wide, 2560, 2048, k=16)
            tt(w0, part(wide, 2560, 2048), part(wide, 2560, 2048), ALU.mult)
            r16 = stat[:, 32:48]
            step(dve.tensor_reduce(r16, w0.rearrange("p (k t) -> p k t", k=16), AX.X, ALU.add))
            small_rstd("rec", r16, 128)
            tt(o16, o16, r16.unsqueeze(2).broadcast_to([P, 16, P]), ALU.mult, "rec normed")
            for n in range(NT):
                m = turned[0]
                turned[0] += 1
                dve.wait_ge(turn_full, m + 1)
                stt(TL[:, 9:13, n * P:(n + 1) * P], U[m % 2][:, :].rearrange("p (j t) -> p j t", j=4), sm("g_ob")[:, 0:1],
                    TL[:, 18:22, n * P:(n + 1) * P], ALU.mult, ALU.mult, f"rec oT {n}", turn_done)

            dve.wait_ge(gemm_done, at("have cq"))
            for name, v, wd, c0 in (("cq", CQ, 384, 48), ("ckv", CKV, 256, 52)):
                sq = part(work, 2560, 4 * wd, k=NT)
                tt(sq, v, v, ALU.mult)
                step(dve.tensor_reduce(stat[:, c0:c0 + 4], sq, AX.X, ALU.add))
                small_rstd(name, stat[:, c0:c0 + 4], wd)
                for n in range(NT):
                    ts(v[:, n, :], v[:, n, :], stat[:, c0 + n:c0 + n + 1], None, ALU.mult,
                       name="latents normed" if (name, n) == ("ckv", NT - 1) else None)
            for j in range(3):
                take_turn(None, CQT[:, j, :], scalar=sm("g_cq")[:, j:j + 1])
            for j in range(2):
                take_turn("ckvT" if j else None, CKVT[:, j, :], scalar=sm("g_ckv")[:, j:j + 1])
            pf, ang, kk = stat[:, 56:60], trig[:, 0:P], trig[:, P:2 * P]
            step(dve.tensor_copy(pf, pcol[:, :]))
            for n in range(NT):
                ts(ang[:, n * 32:(n + 1) * 32], con("invf"), pf[:, n:n + 1], None, ALU.mult)
            ts(kk, ang, 1.0 / TWO_PI, ROUND, ALU.mult, ALU.add)
            ts(kk, kk, ROUND, None, ALU.subtract)
            for c_ in PI_PARTS:
                stt(ang, kk, -c_, ang, ALU.mult, ALU.add)
            ts(ang, ang, PI_IN, -PI_IN, ALU.min, ALU.max, name="angles")
            dve.wait_ge(act_step, at("trig"))
            cos1, sin1 = part(trig, 0, P, k=NT), part(trig, P, P, k=NT)

            def rope(x1, x2, c_, s_, a, b, o1=None, o2=None, name=None):
                o1, o2 = x1 if o1 is None else o1, x2 if o2 is None else o2
                tt(a, x1, s_, ALU.mult)
                tt(b, x2, s_, ALU.mult)
                tt(o1, x1, c_, ALU.mult)
                tt(o1, o1, b, ALU.subtract)
                tt(o2, x2, c_, ALU.mult)
                tt(o2, o2, a, ALU.add, name)

            dve.wait_ge(gemm_done, at("have qpe"))
            ta, tb = part(wide, 512, 128), part(wide, 640, 128)
            a3, b3 = ta.rearrange("p (n t) -> p n t", n=4), tb.rearrange("p (n t) -> p n t", n=4)
            rope(ROW[:, :, 136:168], ROW[:, :, 168:200], cos1, sin1, a3, b3, KPE2[:, :, 0:32], KPE2[:, :, 32:64])
            step(dve.tensor_copy(KPE2[:, :, 64:128], KPE2[:, :, 0:64]))
            for n in range(NT):
                qv = QPE[:, n, :].rearrange("p (h t) -> p h t", h=4)
                cb, sb_ = [v[:, n:n + 1, :].broadcast_to([P, 4, 32]) for v in (cos1, sin1)]
                rope(qv[:, :, 0:32], qv[:, :, 32:64], cb, sb_, a3, b3, name="roped" if n == NT - 1 else None)
            take_turn(None, KPET)
            for j in range(2):
                take_turn("qpeT" if j else None, QPET[:, j, :])
            attention_max("mla", 4, probs_over_sums("mla", lambda n: work[:, 0:T], 4), o_to_tiles("mla", 5))

            dve.wait_ge(act_step, at("tanh c"))
            stt(SILU_C, SILU_C, 1.0, sm("c2"), ALU.add, ALU.mult)
            ts(SILU_C, SILU_C, 0.5, None, ALU.mult, name="silu c")
            inc, rest = stat[:, 64:80], stat[:, 80:96]
            tt(inc, sm("rel"), sm("rel_before"), ALU.subtract)
            for z in range(3):
                step(dve.tensor_copy(REL[z], inc), "increments" if z == 2 else None)
                step(dve.tensor_copy(rest, REL[z]))
                tt(inc, inc, rest, ALU.subtract)
            ts(KEYSTEP, pkey[:, :], con("least"), None, ALU.add)
            for c_, (key, queries) in enumerate(BIAS_PARTS):
                t0, t1 = queries[0] * P, (queries[-1] + 1) * P
                for g in range(32):
                    if g >= 8:
                        dve.wait_ge(steps_used, at(f"bias {c_} {g - 8}"))
                    ts(STEPS(g, t1 - t0), prow[:, t0:t1], KEYSTEP[:, 32 * key + g:32 * key + g + 1], None, ALU.is_ge,
                       name=f"steps {c_} {g}")
                for n in queries:
                    m = turned[0]
                    turned[0] += 1
                    dve.wait_ge(turn_full, m + 1)
                    lo = upto(n) + key * P
                    step(dve.tensor_tensor(BIAS[:, :, lo:lo + P], U[m % 2][:, :].rearrange("p (s h) -> p h s", h=4),
                                           chosen[:, lo:lo + P].unsqueeze(1).broadcast_to([P, 4, P]), ALU.add), None, turn_done)

            def biased(i, n, h, src):
                out = LOGITS[i % 2][:, 0:(n + 1) * P]
                tt(out, src, BIAS[:, h, upto(n):upto(n + 1)], ALU.add)
                return out

            attention_max("dsa", 4, probs_over_sums("dsa", lambda n: work[:, 0:T], 4), o_to_tiles("dsa", 13), biased)
            step(dve.memset(stat[:, 60:61], 0.0), "dsa done")
            m = turned[0]
            turned[0] += 1
            dve.wait_ge(turn_full, m + 1)
            step(dve.tensor_tensor(MOD, U[m % 2][:, 0:24], sm("b_ada"), ALU.add), None, turn_done)

            for k in range(KD):
                split(f"attn {k}", H[:, k, :], H_HEAD[:, k, :], H_REST[:, k, :])
                if k == 1:
                    weights_split("gate_0", (0,))
            weights_split("gate_0", (1, 2))
            weights_split("gate_1")

            for j in range(8):
                m0, m1 = part(work, 0, T), part(work, T, T)
                for b_ in range(3):
                    dve.wait_ge(gemm_done, at(f"gate {j} {b_}"))
                    m = turned[0]
                    turned[0] += 1
                    dve.wait_ge(turn_full, m + 1)
                    stt(m1 if b_ else m0, GATE[b_], 1.0, U[m % 2][:, :], ALU.add, ALU.mult, None, turn_done)
                    if b_ == 1:
                        tt(m0, m0, m1, ALU.add)
                    if b_ == 2:
                        tt(TL[:, MIX[j], :], m0, m1, ALU.add, f"mixed {j}")
                if j < 7:
                    weights_split(SPLIT[j + 2])
            for k in range(KD):
                split(f"mixed {k}", TL[:, MIX[k], :], H_HEAD[:, k, :], TL_REST[:, MIX[k], :])
            weights_split("wout_1")

            def add_to_x(scalar, after=None, squared=None):
                for j in range(8):
                    m = turned[0]
                    turned[0] += 1
                    dve.wait_ge(turn_full, m + 1)
                    stt(X[:, j, :], U[m % 2][:, :], scalar(j), X[:, j, :], ALU.mult, ALU.add, None, turn_done)
                    if squared:
                        squared(j)
                    if after and j in after:
                        weights_split(after[j])

            ts(GLUB, sm("glu_b"), 0.5, None, ALU.mult)
            add_to_x(lambda j: 0.5, {2: "wout_2", 5: "ff_0", 7: "ff_1"},
                     lambda j: squares("ffn", j, H[:, j, :]))
            rms_scale("ffn", lambda k: sm("g_ffn")[:, k:k + 1], H, heads=H_HEAD)
            for j in range(NFF):
                a, hb = part(work, j % 2 * T, T), part(work, (2 + j % 2) * T, T)
                dve.wait_ge(gemm_done, at(f"ff gate {j}"))
                stt(a, a, 1.0, hb, ALU.add, ALU.mult)
                m = turned[0]
                turned[0] += 1
                dve.wait_ge(turn_full, m + 1)
                step(dve.tensor_tensor(TL[:, j, :], a, U[m % 2][:, :], ALU.mult), f"ff {j}", turn_done)
                if j == NFF - 1:
                    tally.named["ff hidden"] = tally.named[f"ff {j}"]
                if j + 1 < NFF:
                    weights_split(SPLIT[SPLIT.index(f"ff_{j}") + 2])
                if 3 <= j < 7:
                    split(f"hidden {j - 3}", TL[:, j - 3, :], HIDDEN_HEAD[j - 3], TL_REST[:, j - 3, :])
            for k in range(4, NFF):
                split(f"hidden {k}", TL[:, k, :], HIDDEN_HEAD[k], TL_REST[:, k, :])
            weights_split("down_1")
            def squares_final(j):
                for k in {6: range(7), 7: (7,)}.get(j, ()):
                    if k == 6:
                        dve.wait_ge(turn_full, at("used down_7"))
                    squares("final", k, SQUARES[k])

            add_to_x(lambda j: 1.0, {j: f"down_{j + 2}" for j in range(6)}, squares_final)
            rms_scale("final", lambda k: sm("g_final")[:, k:k + 1], X)
            stt(GAIN2, MOD[:, 8:16], 1.0, sm("g_2"), ALU.add, ALU.mult)
            rms_scale("block2", lambda k: GAIN2[:, k:k + 1], H, mark="scaled")
            c = SC
            dve.wait_ge(act_step, at("dt"))
            tt(c["t"], sm("a_im"), c["dt"], ALU.mult)
            ts(c["t"], c["t"], 1.0 / TWO_PI, None, ALU.mult)
            ts(c["u"], c["t"], ROUND, None, ALU.add)
            ts(c["u"], c["u"], ROUND, None, ALU.subtract)
            tt(c["turn"], c["t"], c["u"], ALU.subtract)
            ts(c["u"], c["turn"], 384.0, None, ALU.add)
            ts(c["hi"], c["u"], 384.0, None, ALU.subtract)
            tt(c["lo"], c["turn"], c["hi"], ALU.subtract)
            tt(c["rho"], sm("a_re"), c["dt"], ALU.mult, "ssm turn")
            dve.wait_ge(act_step, at("ssm trig"))
            ts(c["t"], c["rho"], 1.0, None, ALU.subtract)
            tt(c["x"], c["t"], c["c"], ALU.mult)
            tt(c["u"], c["h"], c["h"], ALU.mult)
            stt(c["x"], c["u"], -2.0, c["x"], ALU.mult, ALU.add)
            tt(c["y"], c["rho"], c["s"], ALU.mult)
            tt(c["t"], sm("a_re"), sm("a_re"), ALU.mult)
            tt(c["u"], sm("a_im"), sm("a_im"), ALU.mult)
            tt(c["den"], c["t"], c["u"], ALU.add)
            step(dve.reciprocal(c["den"], c["den"]))
            tt(c["t"], c["x"], sm("a_re"), ALU.mult)
            tt(c["u"], c["y"], sm("a_im"), ALU.mult)
            tt(c["t"], c["t"], c["u"], ALU.add)
            tt(c["kr"], c["t"], c["den"], ALU.mult)
            tt(c["t"], c["y"], sm("a_re"), ALU.mult)
            tt(c["u"], c["x"], sm("a_im"), ALU.mult)
            tt(c["t"], c["t"], c["u"], ALU.subtract)
            tt(c["ki"], c["t"], c["den"], ALU.mult)
            dve.wait_ge(ssm_in, 16)
            kr_, ki_ = [c[n].unsqueeze(2).broadcast_to([P, 16, 32]) for n in ("kr", "ki")]
            t1, t2 = [SSM(n).rearrange("p (k t) -> p k t", k=16) for n in ("t1", "t2")]
            tt(t1, CC[1], ki_, ALU.mult)
            tt(t2, CC[0], ki_, ALU.mult)
            tt(CC[0], CC[0], kr_, ALU.mult)
            tt(CC[0], CC[0], t1, ALU.subtract)
            tt(CC[1], CC[1], kr_, ALU.mult)
            tt(CC[1], CC[1], t2, ALU.add)
            ts(CC[1], CC[1], -1.0, None, ALU.mult)

            def phases(j):
                hi, lo = c["hi"][:, j:j + 1], c["lo"][:, j:j + 1]
                r, t1, t2 = SSM("turns"), SSM("t1"), SSM("t2")
                ts(t1, con("time"), hi, None, ALU.mult)
                ts(t2, t1, ROUND, ROUND, ALU.add, ALU.subtract)
                tt(t1, t1, t2, ALU.subtract)
                stt(t1, con("time"), lo, t1, ALU.mult, ALU.add)
                ts(r, t1, 0.5, -0.5, ALU.min, ALU.max, name=f"phases {j}")

            def drain_y(ct):
                dve.wait_ge(sum_full, at(f"full y {4 * ct + 3}"))
                stt(TL[:, 2 + ct, :], TL[:, 2 + ct, :], sm("ssm_d")[:, ct:ct + 1], O[0][:, :], ALU.mult, ALU.add,
                    f"y {ct}", sum_done)

            phases(0)
            for j in range(16):
                s_, c_ = SSM("sin", j), SSM("cos", j)
                dve.wait_ge(act_step, at(f"waves {j}"))
                if j + 1 < 16:
                    phases(j + 1)
                dve.wait_ge(gemm_done, at(f"bu {j}"))
                t1, t2, wr, wi, br, bi_, sr, si = [SSM(n, j) for n in ("t1", "t2", "wr", "wi", "br", "bi", "sr", "si")]
                tt(wr, br, c_, ALU.mult)
                tt(t1, bi_, s_, ALU.mult)
                tt(wr, wr, t1, ALU.add)
                tt(t2, br, s_, ALU.mult)
                tt(wi, bi_, c_, ALU.mult)
                tt(wi, wi, t2, ALU.subtract)
                rho = c["rho"][:, j:j + 1].broadcast_to([P, T])
                step(dve.tensor_tensor_scan(br, rho, wr, 0.0, ALU.mult, ALU.add))
                step(dve.tensor_tensor_scan(bi_, rho, wi, 0.0, ALU.mult, ALU.add))
                if j >= 2:
                    dve.wait_ge(sum_full, at(f"full y {j - 2}"))
                tt(sr, br, c_, ALU.mult)
                tt(t1, bi_, s_, ALU.mult)
                tt(sr, sr, t1, ALU.subtract)
                tt(si, br, s_, ALU.mult)
                tt(t2, bi_, c_, ALU.mult)
                tt(si, si, t2, ALU.add, f"states {j}")
                if j % 4 == 0 and j:
                    drain_y(j // 4 - 1)
            drain_y(3)
            dve.wait_ge(act_step, at("tanh zs"))
            zs4 = tiles[:, 10 * T:14 * T]
            stt(zs4, part(work, 0, 4 * T), 1.0, zs4, ALU.add, ALU.mult)
            tt(zs4, zs4, tiles[:, 2 * T:6 * T], ALU.mult)
            for j in range(4):
                dve.wait_ge(gemm_done, at(f"glu {j}"))
                stt(TL[:, 10 + j, :], part(work, (4 + j) * T, T), 1.0, TL[:, 10 + j, :], ALU.add, ALU.mult,
                    "ssm out" if j == 3 else None)
            step(dve.memset(CB, 0.0))

            def blocks(kv, tile):
                pos = sm(f"pos_{kv}")
                for g in range(2):
                    r = slice(64 * g, 64 * g + 64)
                    src = TL[r, tile, :].rearrange("p (n l) -> p l n", l=16)
                    for hf in range(2):
                        tt(CB[r, 16 * hf:16 * hf + 16, g * NCMP:(g + 1) * NCMP], src[:, :, hf:hf + NCMP],
                           pos[r, 16 * hf:16 * hf + 16].unsqueeze(2).broadcast_to([64, 16, NCMP]), ALU.add,
                           f"blocks {kv}" if g and hf else None)

            blocks("k", 0)
            dve.wait_ge(gemm_done, at("have rows2"))
            ts(stat[:, 64:128], sm("g_q"), 0.125, None, ALU.mult)
            for name, c0, heads, gain, c1 in (("q", 0, 8, stat[:, 64:128], 128), ("ksl", 512, 2, sm("g_ks"), 160), ("kwn", 768, 2, sm("g_kw"), 168)):
                sq = part(work, 0, NT * heads * 64, k=NT)
                v = R2[:, :, c0:c0 + heads * 64]
                tt(sq, v, v, ALU.mult)
                r = stat[:, c1:c1 + NT * heads]
                step(dve.tensor_reduce(r, sq.rearrange("p n (h d) -> p n h d", h=heads), AX.X, ALU.add))
                small_rstd(name, r, 64)
                for n in range(NT):
                    vn = v[:, n, :].rearrange("p (h d) -> p h d", h=heads)
                    tt(vn, vn, r[:, n * heads:(n + 1) * heads].unsqueeze(2).broadcast_to([P, heads, 64]), ALU.mult)
                    tt(vn, vn, gain.unsqueeze(1).broadcast_to([P, heads, 64]), ALU.mult,
                       "q normed" if (name, n) == ("q", NT - 1) else None)
            dve.wait_ge(gemm_done, at("hidden k"))
            blocks("v", 1)
            for j in range(4):
                take_turn(None, TL[:, 14 + j, :])
            cos2, sin2 = con("cos2").rearrange("p (n t) -> p n t", n=NT), con("sin2").rearrange("p (n t) -> p n t", n=NT)
            ta, tb = [part(wide, 4200 + 256 * z, 256, k=8) for z in range(2)]
            for n in range(NT):
                qv = R2[:, n, 0:512].rearrange("p (h t) -> p h t", h=8)
                cb, sb_ = [v[:, n:n + 1, :].broadcast_to([P, 8, 32]) for v in (cos2, sin2)]
                rope(qv[:, :, 0:32], qv[:, :, 32:64], cb, sb_, ta, tb, name="q roped" if n == NT - 1 else None)
            for j in range(4):
                take_turn(None, TL[:, 18 + j, :])
            for kv in "kv":
                take_turn(f"hidden T {kv}", HID(kv)[:, :, 0:2 * NCMP], cols=P, view=lambda v: v.rearrange("p (k t) -> p k t", k=2)[:, :, 0:2 * NCMP])
            for a_, c0 in enumerate((512, 768)):
                for g in range(2):
                    x1, x2 = [R2[:, :, c0 + 64 * g + 32 * z:c0 + 64 * g + 32 * z + 32] for z in range(2)]
                    k2 = K2(2 * a_ + g)
                    aa, bb = [part(wide, 4200 + 256 * z, 128, k=4) for z in range(2)]
                    rope(x1, x2, cos2, sin2, aa, bb, k2[:, :, 0:32], k2[:, :, 32:64])
                    step(dve.tensor_copy(k2[:, :, 64:128], k2[:, :, 0:64]), "k roped" if (a_, g) == (1, 1) else None)
            for i in range(4):
                take_turn("kT 3" if i == 3 else None, KT2[:, i, :])
            dve.wait_ge(gemm_done, at("have vcmp"))
            kr = KCRAW[0:NCMP, :].rearrange("p (g t) -> p g t", g=2)
            kq = part(work, T, P)[0:NCMP].rearrange("p (g t) -> p g t", g=2)
            tt(kq, kr, kr, ALU.mult)
            step(dve.memset(stat[:, 32:34], 1.0))
            step(dve.tensor_reduce(stat[0:NCMP, 32:34], kq, AX.X, ALU.add))
            small_rstd("kc", stat[:, 32:34], 64)
            tt(kr, kr, stat[0:NCMP, 32:34].unsqueeze(2).broadcast_to([NCMP, 2, 64]), ALU.mult)
            for d in range(2):
                tt(KC2[0:NCMP, :, 64 * d:64 * d + 64], kr,
                   sm("g_kc")[0:NCMP, :].unsqueeze(1).broadcast_to([NCMP, 2, 64]), ALU.mult, "kc normed" if d else None)
            take_turn("kcT", KCT.rearrange("p (g t) -> p g t", g=2)[:, :, 0:NCMP], cols=64,
                      view=lambda v: v.rearrange("p (g t) -> p g t", g=2)[:, :, 0:NCMP])
            for z in range(3):
                step(dve.tensor_copy(GB[z], R2[:, :, 1024 + z:1048:3]), "branch logits" if z == 2 else None)
            dve.wait_ge(act_step, at("branch gates"))
            for z in range(3):
                ts(GB[z], GB[z], 0.5, 0.5, ALU.mult, ALU.add)
            cn = con("cmp_neg").rearrange("p (n t) -> p n t", n=NT)
            ck = con("cmp_ok").rearrange("p (n t) -> p n t", n=NT)
            for i in range(8):
                n, e = divmod(i, 2)
                s3 = CMP_P.rearrange("p (h t) -> p h t", h=4)
                m4 = stat[:, 8:12]
                dve.wait_ge(score_done, at(f"cmp score {i}"))
                tt(s3, s3, cn[:, n:n + 1, :].broadcast_to([P, 4, NCMP]), ALU.add)
                step(dve.tensor_reduce(m4, s3, AX.X, ALU.max))
                tt(s3, s3, m4.unsqueeze(2).broadcast_to([P, 4, NCMP]), ALU.subtract, f"cmp less max {i}")
                dve.wait_ge(act_step, at(f"cmp exp {i}"))
                tt(s3, s3, ck[:, n:n + 1, :].broadcast_to([P, 4, NCMP]), ALU.mult, f"cmp probs {i}")
                rs = stat[:, 16:24].rearrange("p (q e) -> p q e", e=2)[:, :, e:e + 1]
                step(dve.tensor_reduce(rs, s3, AX.X, ALU.add))
                if i:
                    dve.wait_ge(sum_full, at(f"cmp summed {i - 1}"))
                take_turn(f"cmp probsT {i}", probsT[0:NCMP, 0:T], rows_=NCMP)
                if e == 1:
                    r8 = stat[:, 16:24]
                    ts(r8, r8, 1e-30, None, ALU.max)
                    step(dve.reciprocal(r8, r8))
                    tt(r8, r8, GB[0][:, n, :], ALU.mult)
                    dve.wait_ge(sum_full, at(f"cmp summed {i}"))
                    step(dve.tensor_tensor(ATT[:, n, :].rearrange("p (h d) -> p h d", h=8),
                                           O[0][:, :].rearrange("p (h d) -> p h d", h=8),
                                           r8.unsqueeze(2).broadcast_to([P, 8, 64]), ALU.mult), None, sum_done)
            for z, name in ((1, "slc"), (2, "win")):
                attention_max(name, 8, probs_over_sums(name, lambda n: ATT[:, n, :], 8, gate=lambda n: GB[z][:, n, :]))
            step(dve.memset(stat[:, 60:61], 0.0), "gates free")
            dve.wait_ge(act_step, at("tanh za"))
            za4 = tiles[:, 6 * T:10 * T]
            stt(za4, part(wide, 6 * T, 4 * T), 1.0, za4, ALU.add, ALU.mult)
            for n in range(NT):
                m = turned[0]
                turned[0] += 1
                dve.wait_ge(turn_full, m + 1)
                v = TL[:, 6:10, n * P:(n + 1) * P]
                step(dve.tensor_tensor(v, U[m % 2][:, :].rearrange("p (j t) -> p j t", j=4), v, ALU.mult),
                     f"attn T {n}", turn_done)

            add_to_x(lambda j: MOD[:, 16 + j:17 + j])
            step(dve.memset(stat[:, 60:61], 0.0), "out ready")

        @block.gpsimd
        def _(pool):

            def step(ins, name=None):
                n = up(pool_step, name)
                ins.then_inc(pool_step, 1)
                pool.wait_ge(pool_step, n)

            pool.wait_ge(const_in, 16)
            half = con("misc")[:, 0:1]
            for name, c0, n in (("rec", 32, 16), ("cq", 48, 4), ("ckv", 52, 4), ("q", 128, 32), ("ksl", 160, 8),
                                ("kwn", 168, 8), ("kc", 32, 2)):
                v = stat[:, c0:c0 + n]
                pool.wait_ge(dve_step, at(f"mean {name}"))
                step(pool.tensor_tensor(v, v, half.broadcast_to([P, n]), ALU.pow), f"rstd {name}")
    return tally.named


def declare(nc):
    def din(name, shape, dt=F32):
        return nc.dram_tensor(name, shape, dt, kind="ExternalInput").ap()

    return [din("wstream", (len(plan()), P, CHUNK)), din("ssm", (P, 4 * T)), din("xT", (P, KD * T)), din("consts", (P, sum(CONST.values()))),
            din("small", (P, sum(SMALL.values()))), din("pos_row", (P, T), I32), din("pos_col", (P, NT), I32),
            din("pos_key", (P, P), I32),
            nc.dram_tensor("outT", (P, KD * T), F32, kind="ExternalOutput").ap()]


def kernel(**inputs):
    import concourse.bacc as _bacc
    from concourse.bass_utils import run_bass_kernel_spmd as _run

    a = {n: np.asarray(v) for n, v in inputs.items()}
    xT = a["x"][0].T.reshape(KD, P, T).transpose(1, 0, 2).reshape(P, -1)
    pos = a["positions"][0].astype(np.int32)
    c, s = constants(), small_inputs(a)
    arrays = {
        "wstream": weight_stream(a), "ssm": state_space_matrices(a), "xT": np.ascontiguousarray(xT),
        "consts": np.ascontiguousarray(np.concatenate([c[n] for n in CONST], 1)),
        "small": np.ascontiguousarray(np.concatenate([s[n] for n in SMALL], 1)),
        "pos_row": np.ascontiguousarray(np.broadcast_to(pos, (P, T))),
        "pos_col": np.ascontiguousarray(pos.reshape(NT, P).T),
        "pos_key": np.ascontiguousarray(np.repeat(pos.reshape(P, 4).T, 32, axis=0)),
    }
    trial = _bacc.Bacc("TRN2", target_bir_lowering=False, num_devices=1)
    known = two_blocks_kernel(trial, *declare(trial), None)
    nc = _bacc.Bacc("TRN2", target_bir_lowering=False, num_devices=1)
    two_blocks_kernel(nc, *declare(nc), known)
    r = _run(nc, [arrays], core_ids=[0])
    out = r.results[0]["outT"]
    return np.ascontiguousarray(out.reshape(P, KD, T).transpose(2, 1, 0).reshape(1, T, D))
```
